# Optimizing a Trainium2 kernel written in Bass

```python
import jax
import jax.numpy as jnp
from jax import lax
import numpy as np
import jax, jax.numpy as jnp

D_MODEL = 1024
BATCH = 1
SEQ = 256
DEPTH = 1

GDN_HEADS = 8
GDN_DK = 128
GDN_DV = 128
GDN_CONV = 4
CHUNK = 64
SC_WIDTH = D_MODEL
SC_CONV = 3
D_FF_RAW = (8 * D_MODEL + 2) // 3
D_FF = (D_FF_RAW + 255) // 256 * 256
EPS = 1e-6
N_MOD = 6

QK_W = GDN_HEADS * GDN_DK
V_W = GDN_HEADS * GDN_DV
QKV_W = 2 * QK_W + V_W
Q_OFF = 0
K_OFF = Q_OFF + QK_W
V_OFF = K_OFF + QK_W
Z_OFF = V_OFF + V_W
A_OFF = Z_OFF + V_W
BETA_OFF = A_OFF + GDN_HEADS
SCB_OFF = BETA_OFF + GDN_HEADS
SCC_OFF = SCB_OFF + SC_WIDTH
SCX_OFF = SCC_OFF + SC_WIDTH
GA_OFF = SCX_OFF + SC_WIDTH
GB_OFF = GA_OFF + D_MODEL
IN_COLS = GB_OFF + D_MODEL


def rms_norm(x, w):
    xf = x.astype(jnp.float32)
    y = xf * lax.rsqrt(jnp.mean(xf * xf, axis=-1, keepdims=True) + EPS)
    return (y * w.astype(jnp.float32)).astype(x.dtype)

def l2_normalize(x):
    xf = x.astype(jnp.float32)
    return (xf * lax.rsqrt(jnp.sum(xf * xf, axis=-1, keepdims=True) + EPS)).astype(x.dtype)

def modulate(h, shift, scale):
    return h * (1.0 + scale[:, None, :]) + shift[:, None, :]

def causal_depthwise_conv(x, w):
    width, ch = w.shape
    return lax.conv_general_dilated(
        x, w[:, None, :].astype(x.dtype), window_strides=(1,), padding=[(width - 1, 0)],
        dimension_numbers=("NWC", "WIO", "NWC"), feature_group_count=ch)

def gated_delta_rule_chunked(q, k, v, g, beta):
    f32 = jnp.float32
    out_dtype = v.dtype
    b, s, h, dk = q.shape
    dv = v.shape[-1]
    n = s // CHUNK

    def to_chunks(t):
        t = t.astype(f32).reshape((b, n, CHUNK, h) + t.shape[3:])
        return jnp.moveaxis(t, 3, 1)

    q, k, v, g, beta = map(to_chunks, (q, k, v, g, beta))
    q = q * (dk ** -0.5)
    g = jnp.cumsum(g, axis=-1)
    idx = jnp.arange(CHUNK)
    causal = idx[:, None] >= idx[None, :]
    strict = idx[:, None] > idx[None, :]
    decay = jnp.exp(jnp.where(causal, g[..., :, None] - g[..., None, :], -jnp.inf))

    k_beta = k * beta[..., None]
    v_beta = v * beta[..., None]
    lower = jnp.where(strict, jnp.einsum("bhncd,bhnsd->bhncs", k_beta, k) * decay, 0.0)
    eye = jnp.eye(CHUNK, dtype=f32)
    t_inv = lax.linalg.triangular_solve(eye + lower, jnp.broadcast_to(eye, lower.shape),
                                        left_side=True, lower=True, unit_diagonal=True)
    eg = jnp.exp(g)
    u = jnp.einsum("bhncs,bhnse->bhnce", t_inv, v_beta)
    w = jnp.einsum("bhncs,bhnsd->bhncd", t_inv, k_beta * eg[..., None])
    qk = jnp.where(causal, jnp.einsum("bhncd,bhnsd->bhncs", q, k) * decay, 0.0)
    q_g = q * eg[..., None]
    g_last = g[..., -1]
    k_dec = k * jnp.exp(g_last[..., None] - g)[..., None]

    def step(state, xs):
        q_c, qk_c, u_c, w_c, k_c, gl = xs
        v_new = u_c - jnp.einsum("bhcd,bhde->bhce", w_c, state)
        o = jnp.einsum("bhcd,bhde->bhce", q_c, state) + jnp.einsum("bhcs,bhse->bhce", qk_c, v_new)
        state = state * jnp.exp(gl)[..., None, None] + jnp.einsum("bhcd,bhce->bhde", k_c, v_new)
        return state, o

    xs = tuple(jnp.moveaxis(t, 2, 0) for t in (q_g, qk, u, w, k_dec, g_last))
    state0 = jnp.zeros((b, h, dk, dv), f32)
    _, o = lax.scan(step, state0, xs)
    o = jnp.transpose(o, (1, 0, 3, 2, 4)).reshape(b, s, h, dv)
    return o.astype(out_dtype)

def hybrid_mixer(h, w_in, gdn_conv_w, a_log, dt_bias, gdn_norm_w, w_gdn_proj, sc_conv_w, w_sc_out, w_o):
    b, s, _ = h.shape
    p = h @ w_in
    qkv = jax.nn.silu(causal_depthwise_conv(p[..., Q_OFF:Z_OFF], gdn_conv_w))
    q = l2_normalize(qkv[..., Q_OFF:K_OFF].reshape(b, s, GDN_HEADS, GDN_DK))
    k = l2_normalize(qkv[..., K_OFF:V_OFF].reshape(b, s, GDN_HEADS, GDN_DK))
    v = qkv[..., V_OFF:Z_OFF].reshape(b, s, GDN_HEADS, GDN_DV)
    z = p[..., Z_OFF:A_OFF].reshape(b, s, GDN_HEADS, GDN_DV)
    g = -jnp.exp(a_log) * jax.nn.softplus(p[..., A_OFF:BETA_OFF] + dt_bias)
    beta = jax.nn.sigmoid(p[..., BETA_OFF:SCB_OFF])
    o = gated_delta_rule_chunked(q, k, v, g, beta)
    o = rms_norm(o, gdn_norm_w) * jax.nn.silu(z)
    y_a = o.reshape(b, s, V_W) @ w_gdn_proj
    gb = p[..., SCB_OFF:SCC_OFF]
    gc = p[..., SCC_OFF:SCX_OFF]
    xin = p[..., SCX_OFF:GA_OFF]
    y_b = (gb * causal_depthwise_conv(gc * xin, sc_conv_w)) @ w_sc_out
    gate_a = jax.nn.sigmoid(p[..., GA_OFF:GB_OFF])
    gate_b = jax.nn.sigmoid(p[..., GB_OFF:IN_COLS])
    return (gate_a * y_a + gate_b * y_b) @ w_o

def swiglu(h, w_ffn_in, w_ffn_out):
    gu = h @ w_ffn_in
    return (jax.nn.silu(gu[..., :D_FF]) * gu[..., D_FF:]) @ w_ffn_out

def first_inputs(seed: int = 0) -> dict:
    key = jax.random.key(seed)
    ks = jax.random.split(key, 22)
    nrm = jax.random.normal
    D = D_MODEL
    x = nrm(ks[0], (BATCH, SEQ, D), jnp.float32)
    c = nrm(ks[1], (BATCH, D), jnp.float32)
    w_ada = nrm(ks[2], (DEPTH, D, N_MOD * D), jnp.float32) * (0.5 * D ** -0.5)
    b_ada = 0.02 * nrm(ks[3], (DEPTH, N_MOD * D), jnp.float32)
    norm1_w = 1.0 + 0.02 * nrm(ks[4], (DEPTH, D), jnp.float32)
    w_in = nrm(ks[5], (DEPTH, D, IN_COLS), jnp.float32) * D ** -0.5
    gdn_conv_w = nrm(ks[6], (DEPTH, GDN_CONV, QKV_W), jnp.float32) * GDN_CONV ** -0.5
    gdn_a_log = jnp.log(jax.random.uniform(ks[7], (DEPTH, GDN_HEADS), jnp.float32, 1.0, 16.0))
    dt = jnp.exp(jax.random.uniform(ks[8], (DEPTH, GDN_HEADS), jnp.float32,
                                    float(np.log(1e-3)), float(np.log(1e-1))))
    gdn_dt_bias = jnp.log(jnp.expm1(dt))
    gdn_norm_w = 1.0 + 0.02 * nrm(ks[9], (DEPTH, GDN_DV), jnp.float32)
    w_gdn_proj = nrm(ks[10], (DEPTH, V_W, D), jnp.float32) * V_W ** -0.5
    sc_conv_w = nrm(ks[11], (DEPTH, SC_CONV, SC_WIDTH), jnp.float32) * SC_CONV ** -0.5
    w_sc_out = nrm(ks[12], (DEPTH, SC_WIDTH, D), jnp.float32) * SC_WIDTH ** -0.5
    w_o = nrm(ks[13], (DEPTH, D, D), jnp.float32) * D ** -0.5
    norm2_w = 1.0 + 0.02 * nrm(ks[14], (DEPTH, D), jnp.float32)
    w_ffn_in = nrm(ks[15], (DEPTH, D, 2 * D_FF), jnp.float32) * D ** -0.5
    w_ffn_out = nrm(ks[16], (DEPTH, D_FF, D), jnp.float32) * D_FF ** -0.5
    w_ada_f = nrm(ks[17], (D, 2 * D), jnp.float32) * (0.5 * D ** -0.5)
    b_ada_f = 0.02 * nrm(ks[18], (2 * D,), jnp.float32)
    normf_w = 1.0 + 0.02 * nrm(ks[19], (D,), jnp.float32)
    return {"x": x, "c": c, "w_ada": w_ada, "b_ada": b_ada, "norm1_w": norm1_w, "w_in": w_in,
            "gdn_conv_w": gdn_conv_w, "gdn_a_log": gdn_a_log, "gdn_dt_bias": gdn_dt_bias,
            "gdn_norm_w": gdn_norm_w, "w_gdn_proj": w_gdn_proj, "sc_conv_w": sc_conv_w,
            "w_sc_out": w_sc_out, "w_o": w_o, "norm2_w": norm2_w, "w_ffn_in": w_ffn_in,
            "w_ffn_out": w_ffn_out, "w_ada_f": w_ada_f, "b_ada_f": b_ada_f, "normf_w": normf_w}

def first_block(x, c, w_ada, b_ada, norm1_w, w_in, gdn_conv_w, gdn_a_log, gdn_dt_bias, gdn_norm_w,
              w_gdn_proj, sc_conv_w, w_sc_out, w_o, norm2_w, w_ffn_in, w_ffn_out, w_ada_f, b_ada_f,
              normf_w):
    c_act = jax.nn.silu(c)
    for l in range(DEPTH):
        mod = c_act @ w_ada[l] + b_ada[l]
        sh1, sc1, g1, sh2, sc2, g2 = jnp.split(mod, N_MOD, axis=-1)
        h = modulate(rms_norm(x, norm1_w[l]), sh1, sc1)
        mix = hybrid_mixer(h, w_in[l], gdn_conv_w[l], gdn_a_log[l], gdn_dt_bias[l], gdn_norm_w[l],
                           w_gdn_proj[l], sc_conv_w[l], w_sc_out[l], w_o[l])
        x = x + g1[:, None, :] * mix
        h = modulate(rms_norm(x, norm2_w[l]), sh2, sc2)
        x = x + g2[:, None, :] * swiglu(h, w_ffn_in[l], w_ffn_out[l])
    shf, scf = jnp.split(c_act @ w_ada_f + b_ada_f, 2, axis=-1)
    return modulate(rms_norm(x, normf_w), shf, scf)


DEPTH_2 = 2

N_MIXERS = 2
N_GLA = (DEPTH_2 + 1) // 2
N_MLA = DEPTH_2 // 2

GLA_HEADS = 4
GLA_DK = D_MODEL // 2 // GLA_HEADS
GLA_DV = D_MODEL // GLA_HEADS
GLA_GATE_RANK = 16
GLA_TAU = 16.0
GLA_CHUNK = 64

MLA_HEADS = 8
MLA_NOPE = 128
MLA_ROPE = 64
MLA_VDIM = 128
MLA_Q_RANK = 384
MLA_KV_RANK = 256
ROPE_THETA = 10000.0
Q_BLOCK = 128

D_FF_2 = -(-8 * D_MODEL // (3 * 256)) * 256


def rmsnorm(t, g):
    tf = t.astype(jnp.float32)
    y = tf * lax.rsqrt(jnp.mean(tf * tf, axis=-1, keepdims=True) + EPS)
    return (y * g.astype(jnp.float32)).astype(t.dtype)

def modulate_2(t, g, shift, scale):
    return rmsnorm(t, g) * (1.0 + scale[:, None, :]) + shift[:, None, :]

def gla_chunked(q, k, v, log_a):
    B, S, H, DK = q.shape
    DV = v.shape[-1]
    C = GLA_CHUNK
    n = S // C

    def to_chunks(t):
        return t.astype(jnp.float32).reshape(B, n, C, H, t.shape[-1]).transpose(1, 0, 3, 2, 4)

    qc, kc, vc, gc = to_chunks(q), to_chunks(k), to_chunks(v), to_chunks(log_a)
    causal = jnp.tril(jnp.ones((C, C), dtype=bool))[:, :, None]

    def step(state, inp):
        qi, ki, vi, gi = inp
        b = jnp.cumsum(gi, axis=-2)
        o_inter = jnp.einsum('bhck,bhkv->bhcv', qi * jnp.exp(b), state)
        diff = b[:, :, :, None, :] - b[:, :, None, :, :]
        decay = jnp.exp(jnp.where(causal, diff, -jnp.inf))
        attn = jnp.einsum('bhik,bhjk,bhijk->bhij', qi, ki, decay)
        o_intra = jnp.einsum('bhij,bhjv->bhiv', attn, vi)
        b_last = b[:, :, -1:, :]
        new_state = state * jnp.exp(b_last[:, :, 0, :])[..., None] + jnp.einsum(
            'bhck,bhcv->bhkv', ki * jnp.exp(b_last - b), vi)
        return new_state, o_inter + o_intra

    state0 = jnp.zeros((B, H, DK, DV), jnp.float32)
    _, o = lax.scan(step, state0, (qc, kc, vc, gc))
    return o.transpose(1, 0, 3, 2, 4).reshape(B, S, H, DV)

def gla_mixer(h, w_in, w_gate, b_gate, g_out, w_out):
    B, S, _ = h.shape
    H, DK, DV = GLA_HEADS, GLA_DK, GLA_DV
    proj = h @ w_in
    q, k, v, r, glr = jnp.split(proj, [H * DK, 2 * H * DK, 2 * H * DK + H * DV,
                                       2 * H * DK + 2 * H * DV], axis=-1)
    q = q.reshape(B, S, H, DK) * (DK ** -0.5)
    k = k.reshape(B, S, H, DK)
    v = v.reshape(B, S, H, DV)
    r = r.reshape(B, S, H, DV)
    log_a = jax.nn.log_sigmoid((glr @ w_gate + b_gate).astype(jnp.float32)) / GLA_TAU
    o = gla_chunked(q, k, v, log_a.reshape(B, S, H, DK)).astype(h.dtype)
    o = rmsnorm(o, g_out) * jax.nn.silu(r)
    return o.reshape(B, S, H * DV) @ w_out

def apply_rope(t, cos, sin):
    tf = t.astype(jnp.float32).reshape(*t.shape[:-1], -1, 2)
    t1, t2 = tf[..., 0], tf[..., 1]
    out = jnp.stack([t1 * cos - t2 * sin, t1 * sin + t2 * cos], axis=-1).reshape(t.shape)
    return out.astype(t.dtype)

def mla_mixer(h, cos, sin, w_in, g_q, w_q_up, g_kv, w_kv_up, w_out):
    B, S, _ = h.shape
    H = MLA_HEADS
    proj = h @ w_in
    cq, ckv, k_rope = jnp.split(proj, [MLA_Q_RANK, MLA_Q_RANK + MLA_KV_RANK], axis=-1)
    q = (rmsnorm(cq, g_q) @ w_q_up).reshape(B, S, H, MLA_NOPE + MLA_ROPE)
    q_nope, q_rope = jnp.split(q, [MLA_NOPE], axis=-1)
    kv = (rmsnorm(ckv, g_kv) @ w_kv_up).reshape(B, S, H, MLA_NOPE + MLA_VDIM)
    k_nope, v = jnp.split(kv, [MLA_NOPE], axis=-1)
    q_rope = apply_rope(q_rope, cos, sin)
    k_rope = apply_rope(k_rope[:, :, None, :], cos, sin)[:, :, 0, :]

    scale = (MLA_NOPE + MLA_ROPE) ** -0.5
    nb = S // Q_BLOCK
    qn = q_nope.reshape(B, nb, Q_BLOCK, H, MLA_NOPE).transpose(1, 0, 2, 3, 4)
    qr = q_rope.reshape(B, nb, Q_BLOCK, H, MLA_ROPE).transpose(1, 0, 2, 3, 4)
    kpos = jnp.arange(S)

    def block(args):
        qn_b, qr_b, idx = args
        s = (jnp.einsum('bqhd,bkhd->bhqk', qn_b, k_nope)
             + jnp.einsum('bqhd,bkd->bhqk', qr_b, k_rope)).astype(jnp.float32) * scale
        qpos = idx * Q_BLOCK + jnp.arange(Q_BLOCK)
        mask = kpos[None, :] <= qpos[:, None]
        p = jax.nn.softmax(jnp.where(mask, s, -jnp.inf), axis=-1)
        return jnp.einsum('bhqk,bkhd->bqhd', p.astype(v.dtype), v)

    o = lax.map(block, (qn, qr, jnp.arange(nb)))
    o = o.transpose(1, 0, 2, 3, 4).reshape(B, S, H * MLA_VDIM)
    return o @ w_out

def swiglu_2(h, w_in, w_out):
    gate, up = jnp.split(h @ w_in, 2, axis=-1)
    return (jax.nn.silu(gate) * up) @ w_out

def second_inputs(seed: int = 0) -> dict:
    key = jax.random.key(seed)
    ks = jax.random.split(key, 24)
    D = D_MODEL
    f32 = jnp.float32

    def w(k, shape, fan_in):
        return jax.random.normal(k, shape, f32) * (fan_in ** -0.5)

    def gain(k, shape):
        return 1.0 + 0.02 * jax.random.normal(k, shape, f32)

    x = jax.random.normal(ks[0], (BATCH, SEQ, D), f32)
    c = jax.random.normal(ks[1], (BATCH, D), f32)
    offsets = jax.random.randint(ks[2], (BATCH, 1), 0, 4096, dtype=jnp.int32)
    positions = offsets + jnp.arange(SEQ, dtype=jnp.int32)[None, :]

    gla_in = 2 * GLA_HEADS * GLA_DK + 2 * GLA_HEADS * GLA_DV + GLA_GATE_RANK
    mla_in = MLA_Q_RANK + MLA_KV_RANK + MLA_ROPE
    return {
        "x": x,
        "c": c,
        "positions": positions,
        "ada_w": w(ks[3], (DEPTH_2, D, 6 * D), D),
        "ada_b": 0.02 * jax.random.normal(ks[4], (DEPTH_2, 6 * D), f32),
        "norm_mix": gain(ks[5], (DEPTH_2, D)),
        "norm_ffn": gain(ks[6], (DEPTH_2, D)),
        "gla_w_in": w(ks[7], (N_GLA, D, gla_in), D),
        "gla_w_gate": w(ks[8], (N_GLA, GLA_GATE_RANK, GLA_HEADS * GLA_DK), GLA_GATE_RANK),
        "gla_b_gate": 0.1 * jax.random.normal(ks[9], (N_GLA, GLA_HEADS * GLA_DK), f32),
        "gla_g_out": gain(ks[10], (N_GLA, GLA_DV)),
        "gla_w_out": w(ks[11], (N_GLA, GLA_HEADS * GLA_DV, D), GLA_HEADS * GLA_DV),
        "mla_w_in": w(ks[12], (N_MLA, D, mla_in), D),
        "mla_g_q": gain(ks[13], (N_MLA, MLA_Q_RANK)),
        "mla_w_q_up": w(ks[14], (N_MLA, MLA_Q_RANK, MLA_HEADS * (MLA_NOPE + MLA_ROPE)), MLA_Q_RANK),
        "mla_g_kv": gain(ks[15], (N_MLA, MLA_KV_RANK)),
        "mla_w_kv_up": w(ks[16], (N_MLA, MLA_KV_RANK, MLA_HEADS * (MLA_NOPE + MLA_VDIM)), MLA_KV_RANK),
        "mla_w_out": w(ks[17], (N_MLA, MLA_HEADS * MLA_VDIM, D), MLA_HEADS * MLA_VDIM),
        "ffn_w_in": w(ks[18], (DEPTH_2, D, 2 * D_FF_2), D),
        "ffn_w_out": w(ks[19], (DEPTH_2, D_FF_2, D), D_FF_2),
        "final_norm": gain(ks[20], (D,)),
    }

def second_block(x, c, positions, ada_w, ada_b, norm_mix, norm_ffn,
              gla_w_in, gla_w_gate, gla_b_gate, gla_g_out, gla_w_out,
              mla_w_in, mla_g_q, mla_w_q_up, mla_g_kv, mla_w_kv_up, mla_w_out,
              ffn_w_in, ffn_w_out, final_norm):
    inv_freq = ROPE_THETA ** (-jnp.arange(0, MLA_ROPE, 2, dtype=jnp.float32) / MLA_ROPE)
    ang = positions.astype(jnp.float32)[..., None] * inv_freq
    cos = jnp.cos(ang)[:, :, None, :]
    sin = jnp.sin(ang)[:, :, None, :]
    c_act = jax.nn.silu(c)

    for i in range(DEPTH_2):
        mod = c_act @ ada_w[i] + ada_b[i]
        sh1, sc1, g1, sh2, sc2, g2 = jnp.split(mod, 6, axis=-1)
        h = modulate_2(x, norm_mix[i], sh1, sc1)
        j = i // N_MIXERS
        if i % N_MIXERS == 0:
            y = gla_mixer(h, gla_w_in[j], gla_w_gate[j], gla_b_gate[j], gla_g_out[j], gla_w_out[j])
        else:
            y = mla_mixer(h, cos, sin, mla_w_in[j], mla_g_q[j], mla_w_q_up[j],
                          mla_g_kv[j], mla_w_kv_up[j], mla_w_out[j])
        x = x + g1[:, None, :] * y
        h = modulate_2(x, norm_ffn[i], sh2, sc2)
        x = x + g2[:, None, :] * swiglu_2(h, ffn_w_in[i], ffn_w_out[i])

    return rmsnorm(x, final_norm)


def setup_inputs(seed=0):
    out = dict(first_inputs(seed))
    for name, value in second_inputs(seed + 1).items():
        if name != "x":
            out[name + "_2"] = value
    return out


def reference(
    x, c, w_ada, b_ada, norm1_w, w_in, gdn_conv_w, gdn_a_log, gdn_dt_bias, gdn_norm_w,
    w_gdn_proj, sc_conv_w, w_sc_out, w_o, norm2_w, w_ffn_in, w_ffn_out, w_ada_f, b_ada_f,
    normf_w, c_2, positions_2, ada_w_2, ada_b_2, norm_mix_2, norm_ffn_2, gla_w_in_2,
    gla_w_gate_2, gla_b_gate_2, gla_g_out_2, gla_w_out_2, mla_w_in_2, mla_g_q_2, mla_w_q_up_2,
    mla_g_kv_2, mla_w_kv_up_2, mla_w_out_2, ffn_w_in_2, ffn_w_out_2, final_norm_2,
):
    x = first_block(
        x, c, w_ada, b_ada, norm1_w, w_in, gdn_conv_w, gdn_a_log, gdn_dt_bias, gdn_norm_w,
        w_gdn_proj, sc_conv_w, w_sc_out, w_o, norm2_w, w_ffn_in, w_ffn_out, w_ada_f, b_ada_f,
        normf_w,
    )
    return second_block(
        x, c_2, positions_2, ada_w_2, ada_b_2, norm_mix_2, norm_ffn_2, gla_w_in_2, gla_w_gate_2,
        gla_b_gate_2, gla_g_out_2, gla_w_out_2, mla_w_in_2, mla_g_q_2, mla_w_q_up_2, mla_g_kv_2,
        mla_w_kv_up_2, mla_w_out_2, ffn_w_in_2, ffn_w_out_2, final_norm_2,
    )


_drawn_inputs = setup_inputs


def setup_inputs(seed=0):
    import zlib

    import numpy as np

    out = dict(_drawn_inputs(seed))
    spreads = {}
    factors = {'norm1_w': 5.473,
     'gdn_norm_w': 8.0,
     'norm2_w': 8.0,
     'norm_mix_2': 2.739,
     'norm_ffn_2': 3.241,
     'gla_g_out_2': 5.718,
     'mla_g_q_2': 8.0,
     'mla_g_kv_2': 8.0,
     'final_norm_2': 2.864}
    for name, (base, spread) in spreads.items():
        noise = np.random.default_rng([zlib.crc32(name.encode()), seed]).standard_normal(out[name].shape)
        drawn = base * np.exp(spread * noise) if base else spread * noise
        out[name] = jnp.asarray(drawn.astype(out[name].dtype))
    for name, factor in factors.items():
        out[name] = (out[name] * factor).astype(out[name].dtype)
    return out
```

```python
from contextlib import ExitStack

import numpy as np

import concourse.bass as bass
from concourse import mybir

F32 = mybir.dt.float32
I32 = mybir.dt.int32
ALU = mybir.AluOpType
ACT = mybir.ActivationFunctionType
AX_X = mybir.AxisListType.X

P = 128
EPS = 1e-6
CHUNK = 64
LEVELS = 6


class Signals:

    def __init__(self, ctx, nc):
        self.ctx, self.nc, self.made = ctx, nc, {}

    def __call__(self, name):
        if name not in self.made:
            self.made[name] = self.ctx.enter_context(self.nc.semaphore(name))
        return self.made[name]


class Stream:

    slots_filled = {}
    slot_user = {}
    blocks = 0

    def __init__(self, n, per, first, wide=1):
        cls = Stream
        self.n, self.per, self.wide = n, per, wide
        self.slots = [first + j * wide for j in range(per)]
        self.block0 = cls.blocks
        self.fill0, self.free = [], []
        for j, s in enumerate(self.slots):
            spans = range(s, s + wide)
            self.free.append(max(cls.slot_user.get(x, 0) for x in spans))
            self.fill0.append(cls.slots_filled.get(s, 0))
            cls.slots_filled[s] = self.fill0[-1] + n
            for x in spans:
                cls.slot_user[x] = self.block0 + (n - 1) * per + j + 1
        cls.blocks += n * per
        self.end = cls.blocks

    def landed(self, i, j):
        return 16 * self.fill0[j] + 16 * i + 16

    def done(self, i, j):
        return self.block0 + i * self.per + j + 1


def program(nc, a, out):
    x, c1, c2, pos = a["x"], a["c"], a["c_2"], a["positions_2"]
    SEQ, D = x.shape[1:]
    KB = D // P
    NT = SEQ // P
    NCH = SEQ // CHUNK
    H1 = a["gdn_a_log"].shape[1]
    W_QKV = a["gdn_conv_w"].shape[2]
    TAPS1, TAPS2 = a["gdn_conv_w"].shape[1], a["sc_conv_w"].shape[1]
    DFF = a["w_ffn_out"].shape[1]
    FB = DFF // P
    Q_OFF, K_OFF, V_OFF, Z_OFF = 0, D, 2 * D, 3 * D
    AB_OFF = 4 * D
    SCB_OFF = AB_OFF + 2 * H1
    SCC_OFF, SCX_OFF, GA_OFF, GB_OFF = (SCB_OFF + n * D for n in (1, 2, 3, 4))
    H2 = 4
    DK2 = a["gla_w_gate_2"].shape[2] // H2
    RANK = a["gla_w_gate_2"].shape[1]
    TAU = 16.0
    R_OFF2 = 2 * H2 * DK2 + D
    H3 = 8
    NOPE, ROPE = 128, 64
    QR, KVR = a["mla_w_q_up_2"].shape[1], a["mla_w_kv_up_2"].shape[1]
    QB, KVB = QR // P, KVR // P
    MLA_COLS = QR + KVR + ROPE
    ADA = 512
    T = SEQ

    ctx = ExitStack()
    with ctx:
        S = Signals(ctx, nc)

        def sb(name, shape, dt=F32):
            return ctx.enter_context(nc.sbuf_tensor(name, shape, dt))

        bank = [ctx.enter_context(nc.psum_tensor(f"bank{n}", [P, 512], F32)) for n in range(8)]
        ADA_BANK = bank[7]

        HALF = 9
        SLOT = KB * P
        ring = sb("ring", [P, 2 * HALF * SLOT])
        ada_w = sb("ada_w", [P, 2, KB // 2, ADA])
        ada_acc = sb("ada_acc", [P, ADA])
        xT = sb("xT", [P, KB, T])
        hT = sb("hT", [P, KB, T])
        big = sb("big", [P, 4 * KB, T])
        rstd = sb("rstd", [P, T])
        lnb = sb("lnb", [P, 2 * T])
        ident = sb("ident", [P, P])
        ones = sb("ones", [P, P])
        halves = sb("halves", [P, LEVELS, P])
        causal = sb("causal", [P, P])
        strict = sb("strict", [P, P])
        chunk_ones = sb("chunk_ones", [P, P])
        chunk_rows = sb("chunk_rows", [P, 2, P])
        vrows = sb("vrows", [P, 4, P])
        bias_cols = sb("bias_cols", [P, 160])
        vec_cols = sb("vec_cols", [P, 120])
        conv_cols = sb("conv_cols", [P, TAPS1 * W_QKV // P])
        mod = sb("mod", [P, 160])
        nscale = sb("nscale", [P, KB])
        cact = sb("cact", [P, 2 * KB])
        evac = sb("evac", [P, 4, T])
        wab = sb("wab", [P, KB, 2 * H1])
        head_rows = sb("head_rows", [P, 2, H1])

        xtok = big[:, 0:KB, :].rearrange("p b t -> p (b t)").rearrange("p (n d) -> p n d", n=NT)
        sq = big[:, 3 * KB:4 * KB, :]

        def rows(ap, n):
            return ap.rearrange("(r p) -> r p", p=P) if len(ap.shape) == 1 else ap.rearrange("a (r p) -> (a r) p", p=P)

        V_N1, V_N2, V_NF, V_MIX, V_FFN2, V_FIN = 0, 8, 16, 24, 40, 56
        V_C, V_C2, V_SC, V_GN, V_GG, V_GQ, V_GKV, V_BG, V_END = 64, 72, 80, 104, 105, 107, 110, 112, 116
        tables = [
            [(0, rows(a["b_ada"], 48)), (48, rows(a["b_ada_f"], 16)), (64, rows(a["ada_b_2"][0:1], 48)),
             (112, rows(a["ada_b_2"][1:2, 0:16 * P], 16))],
            [(0, rows(a["ada_b_2"][1:2, 16 * P:6 * D], 32))],
            [(V_N1, rows(a["norm1_w"], 8)), (V_N2, rows(a["norm2_w"], 8)), (V_NF, rows(a["normf_w"], 8)),
             (V_MIX, rows(a["norm_mix_2"], 16)), (V_FFN2, rows(a["norm_ffn_2"], 16)), (V_FIN, rows(a["final_norm_2"], 8)),
             (V_C, rows(c1, 8)), (V_C2, rows(c2, 8)), (V_SC, a["sc_conv_w"][0].rearrange("k (r p) -> (k r) p", p=P)),
             (V_GN, a["gdn_norm_w"]), (V_GG, rows(a["gla_g_out_2"], 2)), (V_GQ, rows(a["mla_g_q_2"], 3)),
             (V_GKV, rows(a["mla_g_kv_2"], 2)), (V_BG, rows(a["gla_b_gate_2"], 4))],
            [(0, a["gdn_conv_w"][0].rearrange("k (r p) -> (k r) p", p=P))],
        ]
        table_rows = [128, 32, V_END, TAPS1 * W_QKV // P]
        n_table_dmas = sum(len(t) for t in tables) + 4

        SCRATCH = 12034
        scratch = sb("scratch", [P, SCRATCH])
        taken = [0]

        def piece(shape):
            n = int(np.prod(shape))
            ap = scratch[:, taken[0]:taken[0] + n]
            taken[0] += n
            assert taken[0] <= SCRATCH, taken[0]
            if len(shape) == 2:
                ap = ap.rearrange("p (a b) -> p a b", a=shape[0])
            elif len(shape) == 3:
                ap = ap.rearrange("p (a b c) -> p a b c", a=shape[0], b=shape[1])
            elif len(shape) == 4:
                ap = ap.rearrange("p (a b c d) -> p a b c d", a=shape[0], b=shape[1], c=shape[2])
            return ap

        PAD = TAPS1 - 1
        NHV = 16
        qkv_pad = piece((3, T + PAD))
        conv = piece((3, T))
        act3 = piece((3, T))
        sq2 = piece((2, T))
        rn2 = conv[:, 0:2, :]
        kq = piece((2, T))
        gmat = piece((4, P))
        dec = piece((NT, P))
        egb = piece((NT * P,))
        bstrict = piece((NT, P))
        qkdec = piece((NT, P))
        ldec = piece((NT, P))
        LT = piece((NT, P))
        QKT = piece((NT, P))
        LTm = piece((LEVELS, NT, P))
        kdec = piece((NT, P))
        kbeg = piece((NT, P))
        vb = piece((NT, P))
        inv = piece((2, NT, P))
        xs = piece((NT, P))
        wz = piece((NCH, P))
        vnew = piece((NT, P))
        state = piece((P,))
        qg = piece((NT * P,))
        onrm = piece((NT * P,))
        scb = piece((T,))
        scc = piece((T,))
        scx_pad = piece((T + TAPS2 - 1,))
        scv = piece((T,))
        hv = piece((H1, NHV))
        hcur = piece((NHV,))
        ab_in = piece((NT, 2, H1))
        ab_t = piece((5, NT, H1))

        taken[0] = 0
        DV2 = 2
        gb = piece((H2, T))
        expo = piece((8 * T,))
        gl_a, gl_m = (expo[:, n * H2 * T:(n + 1) * H2 * T].rearrange("p (h t) -> p h t", h=H2) for n in range(2))
        qkv2 = piece((4, T))
        kt = piece((LEVELS, T))
        qt = piece((LEVELS, NT, CHUNK))
        halves_c = piece((LEVELS, CHUNK))
        qe = piece((T,))
        kd = piece((T,))
        qk2 = piece((T,))
        kd_tok = piece((NT, P))
        v_tok = piece((NT, DV2 * P))
        qk_col = piece((NT,))
        segment = piece((H2 * T,))
        taken[0] -= H2 * T
        att_l = piece((NT, LEVELS, CHUNK))
        att = piece((NT, P))
        states = piece((NCH - 1, DV2 * P))
        sq_o = piece((DV2, T))
        on2 = piece((DV2, T))
        wglr = piece((KB, RANK))
        glr = piece((T,))
        wgate = piece((H2 * DK2,))

        taken[0] = 0
        lat = piece((NT, QR + KVR + ROPE))
        lat_sq = piece((QR,))
        lat_ss = piece((NT, 2))
        lat_ln = piece((NT, 2))
        lat_rn = piece((NT, 2))
        cqT = piece((QB, T))
        ckvT = piece((KVB, T))
        krT = piece((T,))
        k_rot = piece((NT, 2, ROPE))
        qkT = piece((2, 2, T))
        vr = piece((2, NT * (NOPE + ROPE)))
        q_rot = piece((NT, 2, ROPE))
        rot_u = piece((2, 4, NT, ROPE // 2))
        qrT = piece((T,))
        neg3 = piece((3, P))
        sc3 = piece((2, 3 * P))
        p3 = piece((2, 3 * P))
        mx3 = piece((2, NT))
        nm3 = piece((2, NT))
        sum3 = piece((2, NT))
        inv3 = piece((2, NT))
        pT3 = piece((2, 3 * P))

        pos_i = sb("pos_i", [NT, P], I32)
        pos_f = sb("pos_f", [NT, P])
        pos_c = sb("pos_c", [P, NT])
        inv_freq = sb("inv_freq", [P, ROPE // 2])
        angle = sb("angle", [P, NT, ROPE // 2])
        turns = sb("turns", [P, NT, ROPE // 2])
        sin_t = sb("sin_t", [P, NT, ROPE // 2])
        cos_t = sb("cos_t", [P, NT, ROPE // 2])

        oall, ybin = big[:, 0:KB, :], big[:, KB:2 * KB, :]
        gates = big[:, 2 * KB:4 * KB, :]

        Stream.slots_filled, Stream.slot_user, Stream.blocks = {}, {}, 0
        st_h1 = Stream(H1, 9, 0)
        st_p1 = Stream(KB // 2, 4, HALF)
        st_o1 = Stream(KB // 4, 4, 0)
        st_f1 = Stream(FB // 2, 4, HALF)
        st_d1 = Stream(KB // 2, 2, 0, wide=3)

        st_h2 = Stream(H2, 6, HALF)
        st_o2 = Stream(KB // 4, 4, 0)
        st_f2 = Stream(FB // 2, 4, HALF)
        st_d2 = Stream(KB // 2, 2, 0, wide=3)
        st_lat = Stream(1, 1, HALF, wide=6)
        st_h3 = Stream(H3 // 2, 4, 0)
        st_o3 = Stream(KB // 4, 4, HALF)
        st_f3 = Stream(FB // 2, 4, 0)
        st_d3 = Stream(KB // 2, 2, HALF, wide=3)

        def slot(s, kb=KB, n=P):
            return ring[:, s * SLOT:s * SLOT + kb * n].rearrange("p (k n) -> p k n", k=kb)

        STEPS1 = 24
        G1 = 3
        ready_step = [-(-KB * (j + 1) // G1) for j in range(9)]
        w_in = a["w_in"][0]
        head_cols = [Q_OFF, K_OFF, V_OFF, SCB_OFF, SCC_OFF, SCX_OFF, GA_OFF, GB_OFF, Z_OFF]

        G2 = 8
        STEPS2 = 6
        ready_step2 = [-(-KB * (j + 1) // G2) for j in range(6)]
        head_cols2 = [(R_OFF2, 2), (R_OFF2 + P, 2), (2 * H2 * DK2, 2), (2 * H2 * DK2 + P, 2), (0, 1), (H2 * DK2, 1)]
        NORMS = [(V_N1, KB), (V_N2, 4 * KB), (V_NF, 7 * KB), (V_MIX, 9 * KB), (V_FFN2, 12 * KB), (V_MIX + KB, 15 * KB),
                 (V_FFN2 + KB, 18 * KB)]

        def kview(w):
            return w.rearrange("(k p) n -> p k n", p=P)

        ADA_PRE = 5
        N_LOOP1 = H1 - 1

        eps_col = sb("eps_col", [P, 1])
        causal_q = sb("causal_q", [P, P])
        block = ctx.enter_context(nc.Block())

        @block.sync
        def _(sp):
            def load_ada(m, w, col):
                for h in range(2):
                    sp.wait_ge(S("ada_used"), 2 * m + h + 1)
                    rows = w[:, h * D // 2:(h + 1) * D // 2, bass.ds(col, ADA)].rearrange("l (k p) n -> p (l k) n", p=P)
                    sp.dma_start(ada_w[:, h], rows).then_inc(S(f"ada_landed{h}"), 16)

            def load_block(st, i, j, src):
                sp.dma_start(src[0], src[1]).then_inc(S(f"landed{st.slots[j]}"), 16)

            def stream(st, src, extra=None, used=lambda j: j):
                for j in range(st.per):
                    if st.free[j]:
                        sp.wait_ge(S("gemm_done"), st.free[j])
                    load_block(st, 0, j, src(0, j))
                if extra:
                    extra(0)
                with sp.Fori(1, st.n) as i:
                    for j in range(st.per):
                        sp.wait_ge(S("gemm_done"), st.done(i - 1, used(j)))
                        load_block(st, i, j, src(i, j))
                    if extra:
                        extra(i)

            sp.dma_start(xtok, x[0].rearrange("(n p) d -> p n d", p=P)).then_inc(S("x_landed"), 16)
            for n, table in enumerate(tables):
                for r, src in table:
                    sp.dma_start(vrows[r:r + src.shape[0], n, :], src).then_inc(S("rows_landed"), 16)
            sp.dma_start(wab[:, :, :], kview(w_in)[:, :, AB_OFF:AB_OFF + 2 * H1]).then_inc(S("rows_landed"), 16)
            sp.dma_start(head_rows[:, 0, :], a["gdn_dt_bias"].broadcast_to([P, H1])).then_inc(S("rows_landed"), 16)
            sp.dma_start(head_rows[:, 1, :], a["gdn_a_log"].broadcast_to([P, H1])).then_inc(S("rows_landed"), 16)
            sp.dma_start(pos_i[:, :], pos.rearrange("a (n p) -> (a n) p", p=P)).then_inc(S("rows_landed"), 16)
            for m in range(ADA_PRE):
                load_ada(m, a["w_ada"], m * ADA)
            wv = kview(w_in)

            def ada1(i):
                if isinstance(i, int):
                    return
                load_ada(ADA_PRE + 2 * (i - 1), a["w_ada"], (ADA_PRE - 1) * ADA + i * ADA)
                load_ada(ADA_PRE + 2 * (i - 1) + 1, a["ada_w_2"][0:1], i * ADA - ADA)

            stream(st_h1, lambda i, j: (slot(st_h1.slots[j]), wv[:, :, bass.ds(i * P + head_cols[j], P)]), extra=ada1)
            m0 = ADA_PRE + 2 * N_LOOP1
            wa, wb = kview(a["w_gdn_proj"][0]), kview(a["w_sc_out"][0])

            def ada2(i):
                load_ada(m0 + i, a["w_ada_f"].rearrange("(l k) n -> l k n", l=1), i * ADA)

            stream(st_p1, lambda i, j: (slot(st_p1.slots[j]), (wa, wb)[j % 2][:, :, bass.ds(i * 2 * P + (j // 2) * P, P)]), extra=ada2)
            m1 = m0 + st_p1.n
            wo = kview(a["w_o"][0])

            def ada3(i):
                load_ada(m1 + i, a["ada_w_2"][bass.ds(i, 1)], 11 * ADA)

            stream(st_o1, lambda i, j: (slot(st_o1.slots[j]), wo[:, :, bass.ds(i * 4 * P + j * P, P)]), extra=ada3)
            m2 = m1 + st_o1.n
            wf = kview(a["w_ffn_in"][0])

            def ada4(i):
                load_ada(m2 + i, a["ada_w_2"][1:2], i * ADA)

            stream(st_f1, lambda i, j: (slot(st_f1.slots[j]), wf[:, :, bass.ds(i * 2 * P + (j // 2) * P + (j % 2) * DFF, P)]), extra=ada4)
            m3 = m2 + st_f1.n
            wd = kview(a["w_ffn_out"][0])

            def ada5(i):
                load_ada(m3 + i, a["ada_w_2"][0:1], i * ADA + N_LOOP1 * ADA)

            stream(st_d1, lambda i, j: (slot(st_d1.slots[j], FB), wd[:, :, bass.ds(i * 2 * P + j * P, P)]), extra=ada5)

            wg = kview(a["gla_w_in_2"][0])
            sp.wait_ge(S("head_out"), H1)
            sp.dma_start(wglr, wg[:, :, R_OFF2 + D:R_OFF2 + D + RANK]).then_inc(S("glr_landed"), 16)
            sp.dma_start(wgate[0:RANK, :], a["gla_w_gate_2"][0]).then_inc(S("glr_landed"), 16)
            stream(st_h2, lambda i, j: (slot(st_h2.slots[j]), wg[:, :, bass.ds(i * (P * head_cols2[j][1]) + head_cols2[j][0], P)]))
            wo2 = kview(a["gla_w_out_2"][0])
            stream(st_o2, lambda i, j: (slot(st_o2.slots[j]), wo2[:, :, bass.ds(i * 4 * P + j * P, P)]))

            def ffn_stream(st_f, st_d, layer):
                wf, wd = kview(a["ffn_w_in_2"][layer]), kview(a["ffn_w_out_2"][layer])
                stream(st_f, lambda i, j: (slot(st_f.slots[j]), wf[:, :, bass.ds(i * 2 * P + (j // 2) * P + (j % 2) * DFF, P)]))
                stream(st_d, lambda i, j: (slot(st_d.slots[j], FB), wd[:, :, bass.ds(i * 2 * P + j * P, P)]))

            ffn_stream(st_f2, st_d2, 0)
            sp.wait_ge(S("gemm_done"), st_lat.free[0])
            sp.dma_start(slot(HALF, KB, MLA_COLS), kview(a["mla_w_in_2"][0])).then_inc(S(f"landed{HALF}"), 16)
            wq, wkv = kview(a["mla_w_q_up_2"][0]), kview(a["mla_w_kv_up_2"][0])

            def head3_src(i, j):
                if j % 2 == 0:
                    n = NOPE + ROPE
                    return slot(st_h3.slots[j], QB, n), wq[:, :, bass.ds(i * 2 * n + j // 2 * n, n)]
                n = 2 * NOPE
                return slot(st_h3.slots[j], KVB, n), wkv[:, :, bass.ds(i * 2 * n + j // 2 * n, n)]

            stream(st_h3, head3_src, used=lambda j: j | 1)
            wo3 = kview(a["mla_w_out_2"][0])
            stream(st_o3, lambda i, j: (slot(st_o3.slots[j]), wo3[:, :, bass.ds(i * 4 * P + j * P, P)]))
            ffn_stream(st_f3, st_d3, 1)
            for n in range(NT):
                sp.wait_ge(S("y_copied"), (n + 1) * KB // 4)
                sp.dma_start(out[0, n * P:(n + 1) * P, :], xtok[:, n, :]).then_inc(S("stored"), 16)
            sp.wait_ge(S("stored"), 16 * NT)

        @block.gpsimd
        def _(pool):
            pool.memset(ident[:, :], 1.0).then_inc(S("const"), 1)
            pool.memset(ones[:, :], 1.0).then_inc(S("ones"), 1)
            pool.memset(halves[:, :, :], 0.0).then_inc(S("const"), 1)
            pool.memset(causal_q[:, :], 1.0).then_inc(S("causal_q"), 1)
            pool.wait_ge(S("causal_q"), 1)
            pool.affine_select(out=causal_q[:, :], in_=causal_q[:, :], compare_op=ALU.is_ge, fill=0.0, base=0,
                               pattern=[[-1, P]], channel_multiplier=1).then_inc(S("masks"), 1)
            pool.memset(chunk_ones[:, :], 1.0).then_inc(S("const"), 1)
            pool.memset(chunk_rows[:, :, :], 1.0).then_inc(S("const"), 1)
            pool.memset(qkv_pad[:, :, 0:PAD], 0.0).then_inc(S("padded"), 1)
            pool.memset(scx_pad[:, 0:TAPS2 - 1], 0.0).then_inc(S("padded"), 1)
            pool.memset(wz, 0.0).then_inc(S("padded"), 1)
            for f in range(ROPE // 2):
                pool.memset(inv_freq[:, f:f + 1], float(np.float32(10000.0 ** (-2.0 * f / ROPE)))).then_inc(S("masks"), 1)
            pool.wait_ge(S("const"), 4)
            n = 4
            pool.affine_select(out=ident[:, :], in_=ident[:, :], compare_op=ALU.is_equal, fill=0.0, base=0,
                               pattern=[[-1, P]], channel_multiplier=1).then_inc(S("ident"), 1)
            for l in range(LEVELS):
                b = 1 << l
                v = halves[:, l, :].rearrange("p (n h b) -> p n h b", h=2, b=b)[:, :, 1, :]
                pool.memset(v, 1.0).then_inc(S("const"), 1)
                n += 1
                pool.wait_ge(S("const"), n)
                pool.affine_select(out=v, in_=v, compare_op=ALU.is_ge, fill=0.0, base=0,
                                   pattern=[[-2 * b, P // (2 * b)], [0, b]], channel_multiplier=1).then_inc(S("const"), 1)
                n += 1
                pool.wait_ge(S("const"), n)
                pool.affine_select(out=v, in_=v, compare_op=ALU.is_ge, fill=0.0, base=b - 1,
                                   pattern=[[2 * b, P // (2 * b)], [0, b]], channel_multiplier=-1).then_inc(S("const"), 1)
                n += 1
            v = chunk_ones[:, :].rearrange("p (n b) -> p n b", b=CHUNK)
            for v, pat in ((v, CHUNK), (chunk_rows[:, :, :], P)):
                pool.affine_select(out=v, in_=v, compare_op=ALU.is_ge, fill=0.0, base=0,
                                   pattern=[[-CHUNK, 2], [0, pat]], channel_multiplier=1).then_inc(S("const"), 1)
                n += 1
                pool.wait_ge(S("const"), n)
                pool.affine_select(out=v, in_=v, compare_op=ALU.is_ge, fill=0.0, base=CHUNK - 1,
                                   pattern=[[CHUNK, 2], [0, pat]], channel_multiplier=-1).then_inc(S("const"), 1)
                n += 1
            pool.wait_ge(S("const"), n)
            pool.wait_ge(S("ident"), 1)
            pool.tensor_tensor(strict[:, :], halves[:, 0, :], halves[:, 1, :], ALU.add).then_inc(S("const"), 1)
            for l in range(2, LEVELS):
                n += 1
                pool.wait_ge(S("const"), n)
                pool.tensor_tensor(strict[:, :], strict[:, :], halves[:, l, :], ALU.add).then_inc(S("const"), 1)
            n += 1
            pool.wait_ge(S("const"), n)
            pool.tensor_tensor(causal[:, :], strict[:, :], ident[:, :], ALU.add).then_inc(S("masks"), 1)

        @block.tensor
        def _(pe):
            def ada_sum(m):
                pe.wait_ge(S("ada_mac"), 8 * m + 8)
                if isinstance(m, int) and m == 0:
                    pe.wait_ge(S("pos"), 2)
                pe.wait_ge(S("mod_ready"), m + 1)
                for b in range(ADA // P):
                    mm = pe.matmul(ADA_BANK[:, b:b + 1], ada_acc[:, b * P:(b + 1) * P], ones[:, 0:1], start=True, stop=True)
                mm.then_inc(S("ada_sum"), 1)

            def norm_sum(n):
                pe.wait_ge(S("norm_sq"), n + 1)
                pe.wait_ge(S("norm_free"), n + 1)
                for f in range(KB):
                    mm = pe.matmul(bank[6][:, 0:T], ones[:, :], sq[:, f, :], start=f == 0, stop=f == KB - 1)
                mm.then_inc(S("norm_sum"), 1)

            def block_product(st, i, j, acc, rhs, nacc, kb=KB, part=None):
                w = slot(st.slots[j], kb)
                for k in part if part is not None else range(kb):
                    if k == 0:
                        pe.wait_ge(S(f"landed{st.slots[j]}"), st.landed(i, j))
                        pe.wait_ge(S("evacuated"), st.done(i, j) + 3 - nacc)
                    mm = pe.matmul(acc[:, 0:T], w[:, k, :], rhs[:, k, :], start=k == 0, stop=k == kb - 1)
                    if k == kb - 1:
                        mm.then_inc(S("gemm_done"), 1)

            def stream(st, rhs, kb=KB, extra=None):
                pe.wait_ge(S("evacuated"), st.block0 + 3)
                with pe.Fori(0, st.n) as i:
                    for j in range(st.per):
                        block_product(st, i, j, bank[j % 2], rhs(j), 2, kb)
                    if extra:
                        extra(i)

            pe.wait_ge(S("rows_landed"), 16 * n_table_dmas)
            pe.wait_ge(S("ident"), 1)
            for n, r in enumerate(table_rows):
                mm = pe.matmul(bank[3 + n][:, 0:r], vrows[0:r, n, :], ident[0:r, 0:r], start=True, stop=True, is_transpose=True)
            mm.then_inc(S("turned"), 1)
            pe.wait_ge(S("pos"), 1)
            pe.matmul(ADA_BANK[:, 0:NT], pos_f[:, :], ident[0:NT, 0:NT], start=True, stop=True, is_transpose=True).then_inc(S("turned"), 1)
            pe.wait_ge(S("x_landed"), 16)
            for g in range(KB // 2):
                if g >= 2:
                    pe.wait_ge(S("x_copied"), g - 1)
                for q in range(4):
                    f, n = 2 * g + q // 2, q % 2
                    mm = pe.matmul(bank[g % 2][:, q * P:(q + 1) * P], xtok[:, n, f * P:(f + 1) * P], ident[:, :],
                                   start=True, stop=True, is_transpose=True)
                mm.then_inc(S("turned"), 1)
            pe.wait_ge(S("ones"), 1)
            norm_sum(0)
            for m in range(ADA_PRE):
                ada_sum(m)

            pe.wait_ge(S("rows_landed"), 16 * n_table_dmas)
            pe.wait_ge(S("h_ready"), KB)
            for n in range(NT):
                for k in range(KB):
                    mm = pe.matmul(bank[3][:, n * 2 * H1:(n + 1) * 2 * H1], hT[:, k, n * P:(n + 1) * P], wab[:, k, :],
                                   start=k == 0, stop=k == KB - 1)
            mm.then_inc(S("gates_done"), 1)

            def head_sums():
                pe.wait_ge(S("g_ready"), 1)
                pe.wait_ge(S("masks"), ROPE // 2 + 2)
                g = ab_t[:, 4]
                for n in range(NT):
                    pe.matmul(bank[4][:, n * H1:(n + 1) * H1], causal[:, :], g[:, n, :], start=True, stop=True)
                    pe.matmul(bank[4][:, (NT + n) * H1:(NT + n + 1) * H1], chunk_ones[:, :], g[:, n, :], start=True, stop=True)
                    for c in range(2):
                        k = 2 * NT + 2 * n + c
                        mm = pe.matmul(bank[4][:, k * H1:(k + 1) * H1], chunk_rows[:, c, :], g[:, n, :], start=True, stop=True)
                mm.then_inc(S("gates_done"), 1)

            def head1(i, gemm, chain):
                at = [0]

                def products(n):
                    for _ in range(n if gemm else 0):
                        j, k = divmod(at[0], KB)
                        block_product(st_h1, i, j, bank[j % 3], hT, 3, part=[k])
                        at[0] += 1

                if not chain:
                    products(9 * KB)
                    return
                n = i
                kT, qT = kq[:, 0, :], kq[:, 1, :]
                tok = [slice(t * P, (t + 1) * P) for t in range(NT)]

                products(G1)
                pe.wait_ge(S("gmat"), 4 * n)
                pe.matmul(bank[4][:, :], ones[:, :], gmat.rearrange("p a b -> p (a b)"), start=True, stop=True).then_inc(S("gb_done"), 1)
                products(G1)
                pe.wait_ge(S("qk_sq"), n)
                pe.matmul(bank[3][:, :], ones[:, :], sq2.rearrange("p a b -> p (a b)"), start=True, stop=True).then_inc(S("qk_sum"), 1)
                products(G1)
                pe.wait_ge(S("kq_ready"), 2 * n)
                for t in range(NT):
                    mm = pe.matmul(bank[5][:, t * 2 * P:(t + 1) * 2 * P], kT[:, tok[t]], kq[:, :, tok[t]], start=True, stop=True)
                mm.then_inc(S("kk_done"), 1)
                products(G1)
                for q in range(4):
                    src = (kT, act3[:, 2, :])[q // 2]
                    mm = pe.matmul(bank[6][:, q * P:(q + 1) * P], src[:, tok[q % 2]], ident[:, :], start=True, stop=True, is_transpose=True)
                mm.then_inc(S("kv_turned"), 1)
                products(G1)
                pe.wait_ge(S("levels"), 2 * n)
                for t in range(NT):
                    mm = pe.matmul(bank[3][:, tok[t]], LTm[:, 0, t, :], ident[:, :], start=True, stop=True)
                mm.then_inc(S("x_done"), 1)
                for l in range(1, LEVELS):
                    products(G1)
                    pe.wait_ge(S("inv"), 7 * (n - 1) + l + 1)
                    for t in range(NT):
                        mm = pe.matmul(bank[3][:, tok[t]], LTm[:, l, t, :], inv[:, 0, t, :], start=True, stop=True)
                    mm.then_inc(S("x_done"), 1)
                    products(G1)
                    pe.wait_ge(S("xs"), 5 * (n - 1) + l)
                    for t in range(NT):
                        pe.matmul(bank[4][:, t * P:(t + 1) * P], inv[:, 1, t, :], xs[:, t, :], start=True, stop=True)
                        mm = pe.matmul(bank[4][:, (NT + t) * P:(NT + t + 1) * P], xs[:, t, :], inv[:, 1, t, :], start=True, stop=True)
                    mm.then_inc(S("y_done"), 1)
                products(G1)
                pe.wait_ge(S("inv"), 7 * n)
                pe.wait_ge(S("tok_copied"), 6 * n)
                for t in range(NT):
                    mm = pe.matmul(bank[5][:, tok[t]], kbeg[:, t, :], inv[:, 1, t, :], start=True, stop=True)
                mm.then_inc(S("w_done"), 1)
                for t in range(NT):
                    mm = pe.matmul(bank[3][:, tok[t]], inv[:, 1, t, :], vb[:, t, :], start=t == 0, stop=True, skip_group_check=True)
                mm.then_inc(S("v_done"), 1)
                for c in range(NCH):
                    t, r = c // 2, slice(c % 2 * CHUNK, c % 2 * CHUNK + CHUNK)
                    cols = slice(c * CHUNK, (c + 1) * CHUNK)
                    if c:
                        products(G1)
                        if c == 1:
                            pe.wait_ge(S("wz"), 2 * n)
                        pe.wait_ge(S("state"), 3 * (n - 1) + c)
                        pe.matmul(bank[3][:, tok[t]], wz[:, c, :], state, start=False, stop=True, skip_group_check=True).then_inc(S("v_done"), 1)
                        if c == 1:
                            pe.wait_ge(S("qg"), n)
                        pe.matmul(bank[6][:, cols], state, qg[:, cols], start=c == 1, stop=False, skip_group_check=True)
                    if c < NCH - 1:
                        products(G1)
                        pe.wait_ge(S("vnew"), 4 * (n - 1) + c + 1)
                        pe.matmul(bank[4][:, 0:P], kdec[r, t, :], vnew[r, t, :], start=True, stop=True).then_inc(S("s_done"), 1)
                    if c % 2:
                        pe.wait_ge(S("vnew"), 4 * (n - 1) + c + 1)
                        mm = pe.matmul(bank[6][:, tok[t]], vnew[:, t, :], QKT[:, t, :], start=False, stop=c == NCH - 1, skip_group_check=True)
                mm.then_inc(S("o_done"), 1)
                products(9 * KB - at[0])
                pe.wait_ge(S("o_sq"), n)
                pe.matmul(bank[5][:, 0:T], ones[:, :], onrm, start=True, stop=True).then_inc(S("o_sum"), 1)

            pe.wait_ge(S("evacuated"), 3)
            head_sums()
            head1(0, True, False)
            with pe.Fori(1, H1) as i:
                head1(i, True, True)
                ada_sum(ADA_PRE + 2 * (i - 1))
                ada_sum(ADA_PRE + 2 * (i - 1) + 1)
            head1(H1, False, True)
            m = ADA_PRE + 2 * N_LOOP1
            pe.wait_ge(S("head_out"), H1)
            stream(st_p1, lambda j: (oall, ybin)[j % 2], extra=lambda i: ada_sum(m + i))
            m1 = m + st_p1.n
            pe.wait_ge(S("mix_ready"), KB)
            stream(st_o1, lambda j: hT, extra=lambda i: ada_sum(m1 + i))
            m2 = m1 + st_o1.n
            norm_sum(1)
            pe.wait_ge(S("h_ready"), 2 * KB)
            stream(st_f1, lambda j: hT, extra=lambda i: ada_sum(m2 + i))
            m3 = m2 + st_f1.n
            pe.wait_ge(S("ffn_act"), FB)
            stream(st_d1, lambda j: big, FB, extra=lambda i: ada_sum(m3 + i))
            norm_sum(2)
            norm_sum(3)
            pe.wait_ge(S("h_ready"), 4 * KB)
            pe.wait_ge(S("glr_landed"), 32)
            for k in range(KB):
                mm = pe.matmul(bank[3][0:RANK, 0:T], wglr[:, k, :], hT[:, k, :], start=k == 0, stop=k == KB - 1)
            mm.then_inc(S("gates_done"), 1)
            pe.wait_ge(S("gate_act"), 1)
            for h in range(H2):
                mm = pe.matmul(bank[4 + h // 2][:, h % 2 * T:(h % 2 + 1) * T], wgate[0:RANK, h * DK2:(h + 1) * DK2], glr[0:RANK, :],
                               start=True, stop=True)
            mm.then_inc(S("gates_done"), 1)

            def head2(i, gemm, chain):
                at = [0]

                def products(n):
                    for _ in range(n if gemm else 0):
                        j, k = divmod(at[0], KB)
                        block_product(st_h2, i, j, bank[j % 3], hT, 3, part=[k])
                        at[0] += 1

                if not chain:
                    products(6 * KB)
                    return
                n = i
                tok = [slice(t * P, (t + 1) * P) for t in range(NT)]
                products(G2)
                pe.wait_ge(S("evacuated"), st_h2.done(i - 1, 3) + 3)
                for q in range(4):
                    mm = pe.matmul(bank[3][:, (q % 2 * 2 + q // 2) * P:(q % 2 * 2 + q // 2 + 1) * P], qkv2[:, 2 + q // 2, tok[q % 2]], ident[:, :],
                                   start=True, stop=True, is_transpose=True)
                mm.then_inc(S("v2_turned"), 1)
                products(G2)
                pe.wait_ge(S("scaled2"), 15 * (n - 1) + 2)
                for t in range(NT):
                    mm = pe.matmul(bank[4][:, tok[t]], kd[:, tok[t]], ident[:, :], start=True, stop=True, is_transpose=True)
                mm.then_inc(S("kd_turned"), 1)
                products(G2)
                pe.wait_ge(S("scaled2"), 15 * n)
                pe.wait_ge(S("tok2"), 2 * n)
                for t in range(NT):
                    for l in range(LEVELS):
                        pe.matmul(bank[3 + t][:, l * CHUNK:(l + 1) * CHUNK], kt[:, l, tok[t]], qt[:, l, t, :], start=True, stop=True)
                    mm = pe.matmul(bank[3 + t][:, 2 * T - 1:2 * T], qk2[:, tok[t]], ones[:, 0:1], start=True, stop=True)
                mm.then_inc(S("att_done"), 1)
                for c in range(2):
                    r = slice(c * CHUNK, (c + 1) * CHUNK)
                    if c == 1:
                        pe.wait_ge(S("kv_done"), 3 * (n - 1) + 1)
                    pe.matmul(bank[6][:, c * T:(c + 1) * T], kd_tok[r, 0, :], v_tok[r, 0, :], start=True, stop=True).then_inc(S("kv_done"), 1)
                products(G2)
                pe.wait_ge(S("state2"), 3 * (n - 1) + 2)
                mm = pe.matmul(bank[6][:, 0:T], kd_tok[0:CHUNK, 1, :], v_tok[0:CHUNK, 1, :], start=True, stop=True)
                mm.then_inc(S("kv_done"), 1)
                products(G2)
                pe.wait_ge(S("att"), 8 * n)
                pe.wait_ge(S("state2"), 3 * n)
                for d in range(DV2):
                    for t in range(NT):
                        pe.matmul(bank[5][:, d * T + t * P:d * T + (t + 1) * P], v_tok[:, t, d * P:(d + 1) * P], att[:, t, :],
                                  start=d == 0 and t == 0, stop=False, skip_group_check=True)
                    for c in range(1, NCH):
                        mm = pe.matmul(bank[5][:, d * T + c * CHUNK:d * T + (c + 1) * CHUNK], states[:, c - 1, d * P:(d + 1) * P],
                                       qe[:, c * CHUNK:(c + 1) * CHUNK], start=False, stop=True, skip_group_check=True)
                mm.then_inc(S("o2_done"), 1)
                products(6 * KB - at[0])
                pe.wait_ge(S("o2_sq"), n)
                for d in range(DV2):
                    mm = pe.matmul(bank[4][:, 0:T], ones[:, :], sq_o[:, d, :], start=d == 0, stop=d == DV2 - 1)
                mm.then_inc(S("o2_sum"), 1)

            pe.wait_ge(S("evacuated"), st_h2.block0 + 3)
            head2(0, True, False)
            with pe.Fori(1, H2) as i:
                head2(i, True, True)
            head2(H2, False, True)
            pe.wait_ge(S("head2_out"), H2)
            stream(st_o2, lambda j: big)

            def ffn(n, st_f, st_d):
                norm_sum(n)
                pe.wait_ge(S("h_ready"), (n + 1) * KB)
                stream(st_f, lambda j: hT)
                pe.wait_ge(S("ffn_act"), (n // 2) * FB)
                stream(st_d, lambda j: big, FB)

            ffn(4, st_f2, st_d2)
            norm_sum(5)
            pe.wait_ge(S("h_ready"), 6 * KB)
            pe.wait_ge(S(f"landed{HALF}"), st_lat.landed(0, 0))
            pe.wait_ge(S("evacuated"), st_lat.block0 + 3)
            wl = slot(HALF, KB, MLA_COLS)
            for t in range(NT):
                for c0, c1_, b in ((0, QR, 2 * t), (QR, MLA_COLS, 2 * t + 1)):
                    for k in range(KB):
                        mm = pe.matmul(bank[b][:, 0:c1_ - c0], hT[:, k, t * P:(t + 1) * P], wl[:, k, c0:c1_], start=k == 0, stop=k == KB - 1)
            mm.then_inc(S("gemm_done"), 1)
            pe.wait_ge(S("lat_scaled"), 2 * NT)
            for t in range(NT):
                for k in range(QB):
                    pe.matmul(bank[4 + t][:, k * P:(k + 1) * P], lat[:, t, k * P:(k + 1) * P], ident[:, :], start=True, stop=True, is_transpose=True)
            for t in range(NT):
                for k in range(KVB):
                    mm = pe.matmul(bank[6][:, (2 * t + k) * P:(2 * t + k + 1) * P], lat[:, t, QR + k * P:QR + (k + 1) * P], ident[:, :],
                                   start=True, stop=True, is_transpose=True)
            mm.then_inc(S("lat_turned"), 1)
            pe.wait_ge(S("k_rot"), 4)
            for t in range(NT):
                mm = pe.matmul(ADA_BANK[:, t * P:(t + 1) * P], k_rot[:, t].rearrange("p e f -> p (e f)"), ident[:, :],
                               start=True, stop=True, is_transpose=True)
            mm.then_inc(S("lat_turned"), 1)
            pe.wait_ge(S("latT"), 2 * QB + 2 * KVB + 1)
            with pe.Fori(0, st_h3.n) as i:
                tok = [slice(t * P, (t + 1) * P) for t in range(NT)]
                wq = [slot(st_h3.slots[2 * e], QB, NOPE + ROPE) for e in range(2)]
                wkv = [slot(st_h3.slots[2 * e + 1], KVB, 2 * NOPE) for e in range(2)]
                for e in range(2):
                    pe.wait_ge(S(f"landed{st_h3.slots[2 * e]}"), st_h3.landed(i, 2 * e))
                    pe.wait_ge(S(f"landed{st_h3.slots[2 * e + 1]}"), st_h3.landed(i, 2 * e + 1))
                    if e == 0:
                        pe.wait_ge(S("free3"), i + 1)
                    for k in range(QB):
                        pe.matmul(bank[e][:, 0:T], wq[e][:, k, 0:NOPE], cqT[:, k, :], start=k == 0, stop=k == QB - 1)
                    for k in range(KVB):
                        mm = pe.matmul(bank[e][:, T:2 * T], wkv[e][:, k, 0:NOPE], ckvT[:, k, :], start=k == 0, stop=k == KVB - 1)
                    mm.then_inc(S("gemm_done"), 1)
                    for t in range(NT):
                        for k in range(KVB):
                            pe.matmul(bank[2 + e][:, tok[t]], ckvT[:, k, tok[t]], wkv[e][:, k, NOPE:2 * NOPE], start=k == 0, stop=k == KVB - 1)
                        for k in range(QB):
                            mm = pe.matmul(bank[2 + e][:, T + t * ROPE:T + (t + 1) * ROPE], cqT[:, k, tok[t]], wq[e][:, k, NOPE:NOPE + ROPE],
                                           start=k == 0, stop=k == QB - 1)
                    mm.then_inc(S("gemm_done"), 1)
                pe.wait_ge(S("q_rot"), 4 * i + 4)
                for t in range(NT):
                    mm = pe.matmul(bank[4][:, tok[t]], q_rot[:, t].rearrange("p e f -> p (e f)"), ident[:, :],
                                   start=True, stop=True, is_transpose=True)
                mm.then_inc(S("qr_turned"), 1)
                for e in range(2):
                    half = slice(e * ROPE, (e + 1) * ROPE)
                    if e == 0:
                        pe.wait_ge(S("qrT"), i + 1)
                    for t in range(NT):
                        cols = slice(t * P, 3 * P if t else P)
                        keys = slice(0, (t + 1) * P)
                        pe.matmul(bank[5 + e][:, cols], qkT[:, e, 0, tok[t]], qkT[:, e, 1, keys], start=True, stop=False)
                        mm = pe.matmul(bank[5 + e][:, cols], qrT[half, tok[t]], krT[half, keys], start=False, stop=True)
                    mm.then_inc(S("score3"), 1)
                for e in range(2):
                    pe.wait_ge(S("p3"), 4 * i + 2 * e + 2)
                    for q in range(3):
                        mm = pe.matmul(bank[e][:, q * P:(q + 1) * P], p3[:, e, q * P:(q + 1) * P], ident[:, :], start=True, stop=True, is_transpose=True)
                    mm.then_inc(S("p3_turned"), 1)
                for e in range(2):
                    pe.wait_ge(S("pT3"), 2 * i + e + 1)
                    pe.matmul(bank[2 + e][:, 0:T], vr[:, e, 0:P], pT3[:, e, 0:T], start=True, stop=False, skip_group_check=True)
                    pe.matmul(bank[2 + e][:, P:T], vr[:, e, P:2 * P], pT3[:, e, T:T + P], start=False, stop=True, skip_group_check=True)\
                      .then_inc(S("o3_done"), 1)
            pe.wait_ge(S("o3"), H3)
            stream(st_o3, lambda j: big)
            ffn(6, st_f3, st_d3)
            norm_sum(7)
            pe.wait_ge(S("h_scaled"), 8 * KB + 1)
            for n in range(NT):
                for g in range(KB // 4):
                    m = n * (KB // 4) + g
                    if m >= 2:
                        pe.wait_ge(S("y_copied"), m - 1)
                    for q in range(4):
                        f = 4 * g + q
                        mm = pe.matmul(bank[m % 2][:, q * P:(q + 1) * P], hT[:, f, n * P:(n + 1) * P], ident[:, :], start=True, stop=True, is_transpose=True)
                    mm.then_inc(S("turned"), 1)

        @block.scalar
        def _(act):
            def norm(n, ready, count):
                act.wait_ge(S(ready), count)
                act.activation(sq[:, :, :], xT[:, :, :], ACT.Square).then_inc(S("norm_sq"), 1)
                act.wait_ge(S("norm_sum"), n + 1)
                act.wait_ge(S("h_scaled"), KB * n + 1)
                act.activation(lnb[:, 0:T], bank[6][:, 0:T], ACT.Ln, bias=eps_col[:, 0:1], scale=1.0 / D).then_inc(S("norm_free"), 1)
                act.wait_ge(S("norm_free"), n + 2)
                act.activation(rstd[:, :], lnb[:, 0:T], ACT.Exp, scale=-0.5).then_inc(S("rstd"), 1)

            def shift(n, dst, col):
                for f in range(KB):
                    act.wait_ge(S("h_scaled"), KB * n + f + 2)
                    act.activation(dst[:, f, :], dst[:, f, :], ACT.Identity, bias=mod[:, col + f:col + f + 1])\
                       .then_inc(S("h_ready"), 1)

            def copy_out(st, i, j, dst, nacc, func=ACT.Copy, scale=1.0, bank_of=None):
                act.wait_ge(S("gemm_done"), st.done(i, j))
                return act.activation(dst, bank[(j % nacc)][:, 0:T], func, scale=scale).then_inc(S("evacuated"), 1)

            act.sem_inc(S("free3"), 1)
            act.sem_inc(S("lat_sq"), 1)
            act.sem_inc(S("evacuated"), 3)
            act.sem_inc(S("norm_free"), 1)
            for n, dst in enumerate((bias_cols[:, 0:P], bias_cols[:, P:160], vec_cols[:, 0:V_END], conv_cols[:, :])):
                act.wait_ge(S("turned"), 1)
                act.activation(dst, bank[3 + n][:, 0:table_rows[n]], ACT.Copy).then_inc(S("cols_ready"), 1)
            act.wait_ge(S("cols_ready"), 4)
            act.activation(cact[:, :], vec_cols[:, V_C:V_C + 2 * KB], ACT.Silu).then_inc(S("c_ready"), 1)
            for g in range(KB // 2):
                act.wait_ge(S("turned"), 2 + g + 1)
                act.activation(xT[:, 2 * g:2 * g + 2, :].rearrange("p a b -> p (a b)"), bank[g % 2][:, :], ACT.Copy).then_inc(S("x_copied"), 1)
            act.wait_ge(S("angles"), 1)
            act.activation(sin_t[:, :, :], sin_t[:, :, :], ACT.Sin).then_inc(S("rotary"), 1)
            act.activation(cos_t[:, :, :], cos_t[:, :, :], ACT.Sin).then_inc(S("rotary"), 1)
            norm(0, "x_copied", KB // 2)
            act.wait_ge(S("mod_ready"), 5)
            shift(0, hT, 0)
            act.wait_ge(S("rows_landed"), 16 * n_table_dmas)
            act.activation(head_rows[:, 1, :], head_rows[:, 1, :], ACT.Exp).then_inc(S("ab_act"), 1)
            act.wait_ge(S("ab_copied"), 1)
            act.activation(ab_t[:, 0], ab_in[:, :, 0, :], ACT.Abs).then_inc(S("ab_act"), 1)
            act.wait_ge(S("ab_act"), 2)
            act.activation(ab_t[:, 1], ab_t[:, 0], ACT.Exp, scale=-1.0).then_inc(S("ab_act"), 1)
            act.wait_ge(S("ab_act"), 3)
            act.activation(ab_t[:, 2], ab_t[:, 1], ACT.Ln, bias=1.0).then_inc(S("ab_act"), 1)
            act.wait_ge(S("ab_copied"), 2)
            act.activation(ab_t[:, 3], ab_in[:, :, 1, :], ACT.Exp, scale=-1.0).then_inc(S("ab_act"), 1)
            act.wait_ge(S("hv"), 4)
            hvt = hv.rearrange("p h v -> p v h")
            act.activation(hvt[:, 6:6 + NT, :], hvt[:, 4:4 + NT, :], ACT.Exp).then_inc(S("hv_act"), 1)
            act.activation(hvt[:, 8:8 + NT, :], hvt[:, 8:8 + NT, :], ACT.Exp).then_inc(S("hv_act"), 1)
            act.activation(hvt[:, 10:10 + NCH, :], hvt[:, 10:10 + NCH, :], ACT.Exp).then_inc(S("hv_act"), 1)

            dests = ([qkv_pad[:, b, PAD:PAD + T] for b in range(3)] + [scb, scc, scx_pad[:, TAPS2 - 1:TAPS2 - 1 + T]])

            def copy_out1(i, j):
                if j < 3:
                    if not (isinstance(i, int) and i == 0):
                        act.wait_ge(S("conv"), 12 * i)
                    dst = dests[j]
                elif j < 6:
                    if not (isinstance(i, int) and i == 0):
                        act.wait_ge(S("short"), 5 * i)
                    dst = dests[j]
                elif j < 8:
                    dst = gates[:, bass.ds(i + (j - 6) * KB, 1), :] if not isinstance(i, int) else gates[:, i + (j - 6) * KB, :]
                else:
                    dst = oall[:, bass.ds(i, 1), :] if not isinstance(i, int) else oall[:, i, :]
                copy_out(st_h1, i, j, dst, 3)

            def head1(i, gemm, chain):
                at = [0]

                def copies(step):
                    while gemm and at[0] < 9 and ready_step[at[0]] <= step:
                        copy_out1(i, at[0])
                        at[0] += 1

                if not chain:
                    copies(99)
                    return
                n = i
                z = oall[:, bass.ds(i - 1, 1), :] if not isinstance(i, int) else oall[:, i - 1, :]
                act.wait_ge(S("conv"), 12 * n)
                act.activation(act3, conv, ACT.Silu).then_inc(S("silu"), 1)
                act.wait_ge(S("evacuated"), st_h1.done(i - 1, 8) + 3)
                act.activation(z, z, ACT.Silu).then_inc(S("silu"), 1)
                act.wait_ge(S("silu"), 2 * n - 1)
                act.activation(sq2, act3[:, 0:2, :], ACT.Square).then_inc(S("qk_sq"), 1)
                copies(2)
                act.wait_ge(S("dec_in"), 4 * n)
                act.activation(dec, dec, ACT.Exp).then_inc(S("dec"), 1)
                act.activation(egb, bank[4][:, 0:NT * P], ACT.Exp).then_inc(S("dec"), 1)
                act.wait_ge(S("qk_sum"), n)
                act.activation(lnb[:, :], bank[3][:, :], ACT.Ln, bias=eps_col[:, 0:1]).then_inc(S("qk_rn"), 1)
                act.wait_ge(S("qk_rn"), 2 * n - 1)
                act.activation(rn2.rearrange("p a b -> p (a b)"), lnb[:, :], ACT.Exp, scale=-0.5).then_inc(S("qk_rn"), 1)
                copies(3)
                act.wait_ge(S("kv_turned"), n)
                for q, (dst, src, v) in enumerate(((kdec, 0, 8), (kbeg, 0, 6), (vb, 2, 2))):
                    for t in range(NT):
                        if dst is kbeg:
                            act.activation(dst[:, t, :], bank[6][:, (src + t) * P:(src + t + 1) * P], ACT.Copy, scale=hcur[:, 14 + t:15 + t])\
                               .then_inc(S("tok_copied"), 1)
                        else:
                            act.activation(dst[:, t, :], bank[6][:, (src + t) * P:(src + t + 1) * P], ACT.Copy, scale=hcur[:, v + t:v + t + 1])\
                               .then_inc(S("tok_copied"), 1)
                copies(5)
                for l in range(1, LEVELS):
                    copies(4 + 2 * l)
                    act.wait_ge(S("x_done"), 6 * (n - 1) + l + 1)
                    act.activation(xs.rearrange("p a b -> p (a b)"), bank[3][:, 0:NT * P], ACT.Copy).then_inc(S("xs"), 1)
                    copies(5 + 2 * l)
                copies(16)
                act.wait_ge(S("w_done"), n)
                wzv = wz.rearrange("p (t c) k -> p t c k", t=NT)
                for c in range(2):
                    act.activation(wzv[:, :, c, c * CHUNK:(c + 1) * CHUNK],
                                   bank[5][:, 0:NT * P].rearrange("p (t c k) -> p t c k", t=NT, c=2)[:, :, c, :], ACT.Copy, scale=-1.0)\
                       .then_inc(S("wz"), 1)
                copies(23)
                act.wait_ge(S("o_done"), n)
                act.activation(onrm, bank[6][:, 0:T], ACT.Square).then_inc(S("o_sq"), 1)
                copies(24)
                act.wait_ge(S("o_sum"), n)
                act.activation(lnb[:, 0:T], bank[5][:, 0:T], ACT.Ln, bias=eps_col[:, 0:1], scale=1.0 / P).then_inc(S("o_rn"), 1)
                act.wait_ge(S("o_rn"), 2 * n - 1)
                act.activation(lnb[:, T:2 * T], lnb[:, 0:T], ACT.Exp, scale=-0.5).then_inc(S("o_rn"), 1)

            act.wait_ge(S("padded"), 3)
            head1(0, True, False)
            with act.Fori(1, H1) as i:
                head1(i, True, True)
            head1(H1, False, True)
            for b in range(2):
                act.activation(gates[:, b * KB:(b + 1) * KB, :], gates[:, b * KB:(b + 1) * KB, :], ACT.Sigmoid).then_inc(S("gates"), 1)
            with act.Fori(0, st_p1.n) as i:
                for j in range(4):
                    act.wait_ge(S("mixed"), 2 * i + j // 2 + 1)
                    copy_out(st_p1, i, j, evac[:, j, :], 2)
            with act.Fori(0, st_o1.n) as i:
                for j in range(4):
                    act.wait_ge(S("o_added"), 4 * i + j + 1)
                    copy_out(st_o1, i, j, evac[:, j, :], 2, scale=mod[:, bass.ds(4 * i + 2 * KB + j, 1)])
            norm(1, "x_ready", KB)
            shift(1, hT, 3 * KB)
            with act.Fori(0, st_f1.n) as i:
                for j in range(4):
                    act.wait_ge(S("ffn_free"), 2 * i + j // 2 + 1)
                    copy_out(st_f1, i, j, evac[:, j, :], 2, func=ACT.Silu if j % 2 == 0 else ACT.Copy)
            with act.Fori(0, st_d1.n) as i:
                for j in range(2):
                    act.wait_ge(S("d_added"), 2 * i + j + 1)
                    copy_out(st_d1, i, j, evac[:, j, :], 2, scale=mod[:, bass.ds(2 * i + 5 * KB + j, 1)])
            norm(2, "x_ready", 2 * KB)
            shift(2, xT, 6 * KB)
            norm(3, "h_ready", 3 * KB)
            shift(3, hT, 8 * KB)
            act.wait_ge(S("gates_done"), 3)
            act.activation(glr[0:RANK, :], bank[3][0:RANK, 0:T], ACT.Copy).then_inc(S("gate_act"), 1)
            act.wait_ge(S("gates_done"), 4)
            for h in range(H2):
                act.activation(gb[:, h, :], bank[4 + h // 2][:, h % 2 * T:(h % 2 + 1) * T], ACT.Identity, bias=vec_cols[:, V_BG + h:V_BG + h + 1])\
                   .then_inc(S("gate_act"), 1)
            act.wait_ge(S("gate_act"), 1 + H2)
            act.activation(gl_a, gb, ACT.Abs).then_inc(S("gate_act"), 1)
            act.wait_ge(S("gate_act"), H2 + 2)
            act.activation(gl_a, gl_a, ACT.Exp, scale=-1.0).then_inc(S("gate_act"), 1)
            act.wait_ge(S("gate_act"), H2 + 3)
            act.activation(gl_a, gl_a, ACT.Ln, bias=1.0).then_inc(S("gate_act"), 1)

            def copy_out2(i, j):
                first = isinstance(i, int) and i == 0
                if j < 2:
                    dst = big[:, 2 * i + j, :] if isinstance(i, int) else big[:, bass.ds(2 * i + j, 1), :]
                else:
                    if not first:
                        if j < 4:
                            act.wait_ge(S("v2_turned"), i)
                        else:
                            act.wait_ge(S("scaled2"), 15 * i)
                    dst = qkv2[:, {2: 2, 3: 3, 4: 0, 5: 1}[j], :]
                copy_out(st_h2, i, j, dst, 3, scale=float(DK2) ** -0.5 if j == 4 else 1.0)

            def head2(i, gemm, chain):
                at = [0]

                def copies(step):
                    while gemm and at[0] < 6 and ready_step2[at[0]] <= step:
                        copy_out2(i, at[0])
                        at[0] += 1

                if not chain:
                    copies(99)
                    return
                n = i
                r = big[:, bass.ds(2 * i - 2, 2), :] if not isinstance(i, int) else big[:, 2 * i - 2:2 * i, :]
                act.wait_ge(S("evacuated"), st_h2.done(i - 1, 1) + 3)
                act.activation(r, r, ACT.Silu).then_inc(S("expo_done"), 1)
                act.wait_ge(S("expo"), 14 * n)
                act.activation(expo, expo, ACT.Exp, scale=1.0 / TAU).then_inc(S("expo_done"), 1)
                copies(1)
                act.wait_ge(S("v2_turned"), n)
                act.activation(v_tok.rearrange("p t d -> p (t d)"), bank[3][:, :], ACT.Copy).then_inc(S("tok2"), 1)
                act.wait_ge(S("kd_turned"), n)
                act.activation(kd_tok.rearrange("p t d -> p (t d)"), bank[4][:, 0:NT * P], ACT.Copy).then_inc(S("tok2"), 1)
                copies(5)
                act.wait_ge(S("o2_done"), n)
                act.activation(sq_o.rearrange("p d t -> p (d t)"), bank[5][:, :], ACT.Square).then_inc(S("o2_sq"), 1)
                copies(6)
                act.wait_ge(S("o2_sum"), n)
                act.activation(lnb[:, 0:T], bank[4][:, 0:T], ACT.Ln, bias=eps_col[:, 0:1], scale=1.0 / (DV2 * P)).then_inc(S("o2_rn"), 1)
                act.wait_ge(S("o2_rn"), 2 * n - 1)
                act.activation(lnb[:, T:2 * T], lnb[:, 0:T], ACT.Exp, scale=-0.5).then_inc(S("o2_rn"), 1)

            head2(0, True, False)
            with act.Fori(1, H2) as i:
                head2(i, True, True)
            head2(H2, False, True)

            def out_blocks(st, sem, base, per, gate):
                with act.Fori(0, st.n) as i:
                    for j in range(per):
                        act.wait_ge(S(sem), base + per * i + j + 1)
                        copy_out(st, i, j, evac[:, j, :], 2, scale=mod[:, bass.ds(per * i + gate * KB + j, 1)])

            def ffn(n, st_f, st_d, shift_sec, ready):
                norm(n, "x_ready", ready * KB)
                shift(n, hT, shift_sec * KB)
                base = (n // 2 - 1) * FB
                with act.Fori(0, st_f.n) as i:
                    for j in range(4):
                        act.wait_ge(S("ffn_free"), base + 2 * i + j // 2 + 1)
                        copy_out(st_f, i, j, evac[:, j, :], 2, func=ACT.Silu if j % 2 == 0 else ACT.Copy)
                out_blocks(st_d, "d_added", (n // 2 - 1) * KB, 2, shift_sec + 2)

            out_blocks(st_o2, "o_added", KB, 4, 10)
            ffn(4, st_f2, st_d2, 11, 3)
            norm(5, "x_ready", 4 * KB)
            shift(5, hT, 14 * KB)
            act.wait_ge(S("gemm_done"), st_lat.end)
            for t in range(NT):
                for q, (b, n) in enumerate(((2 * t, QR), (2 * t + 1, KVR))):
                    act.wait_ge(S("lat_sq"), 2 * t + q + 1)
                    act.activation(lat_sq[:, 0:n], bank[b][:, 0:n], ACT.Square, accum_out=lat_ss[:, t, q:q + 1]).then_inc(S("lat_sq"), 1)
            act.wait_ge(S("lat_sq"), 2 * NT + 1)
            for q, n in enumerate((QR, KVR)):
                act.activation(lat_ln[:, :, q], lat_ss[:, :, q], ACT.Ln, bias=eps_col[:, 0:1], scale=1.0 / n).then_inc(S("lat_rn"), 1)
            act.wait_ge(S("lat_rn"), 2)
            act.activation(lat_rn, lat_ln, ACT.Exp, scale=-0.5).then_inc(S("lat_rn"), 1)
            act.wait_ge(S("lat_rn"), 3)
            for t in range(NT):
                act.activation(lat[:, t, 0:QR], bank[2 * t][:, 0:QR], ACT.Copy, scale=lat_rn[:, t, 0:1]).then_inc(S("lat_scaled"), 1)
                act.activation(lat[:, t, QR:QR + KVR], bank[2 * t + 1][:, 0:KVR], ACT.Copy, scale=lat_rn[:, t, 1:2]).then_inc(S("lat_scaled"), 1)
            for t in range(NT):
                act.activation(lat[:, t, QR + KVR:MLA_COLS], bank[2 * t + 1][:, KVR:KVR + ROPE], ACT.Copy).then_inc(S("k_raw"), 1)
            act.wait_ge(S("lat_turned"), 1)
            for t in range(NT):
                for k in range(QB):
                    act.activation(cqT[:, k, t * P:(t + 1) * P], bank[4 + t][:, k * P:(k + 1) * P], ACT.Copy, scale=vec_cols[:, V_GQ + k:V_GQ + k + 1])\
                       .then_inc(S("latT"), 1)
                for k in range(KVB):
                    act.activation(ckvT[:, k, t * P:(t + 1) * P], bank[6][:, (2 * t + k) * P:(2 * t + k + 1) * P], ACT.Copy,
                                   scale=vec_cols[:, V_GKV + k:V_GKV + k + 1]).then_inc(S("latT"), 1)
            act.wait_ge(S("lat_turned"), 2)
            act.activation(krT, ADA_BANK[:, 0:T], ACT.Copy).then_inc(S("latT"), 1)
            act.wait_ge(S("k_raw"), NT)
            act.wait_ge(S("lat_scaled"), 2 * NT)
            act.sem_inc(S("evacuated"), 1)
            SCALE3 = float(NOPE + ROPE) ** -0.5
            with act.Fori(0, st_h3.n) as i:
                for e in range(2):
                    act.wait_ge(S("gemm_done"), st_h3.done(i, 2 * e))
                    act.activation(qkT[:, e].rearrange("p a t -> p (a t)"), bank[e][:, :], ACT.Copy).then_inc(S("evacuated"), 1)
                    act.wait_ge(S("gemm_done"), st_h3.done(i, 2 * e + 1))
                    act.activation(vr[:, e, :], bank[2 + e][:, 0:NT * (NOPE + ROPE)], ACT.Copy).then_inc(S("evacuated"), 1)
                act.wait_ge(S("qr_turned"), i + 1)
                act.activation(qrT, bank[4][:, 0:T], ACT.Copy).then_inc(S("qrT"), 1)
                for e in range(2):
                    for t in range(NT):
                        act.wait_ge(S("nm3"), 2 * i + e + 1)
                        cols = slice(t * P, 3 * P if t else P)
                        act.activation(p3[:, e, cols], sc3[:, e, cols], ACT.Exp, bias=nm3[:, e, t:t + 1], scale=SCALE3,
                                       accum_out=sum3[:, e, t:t + 1]).then_inc(S("exp3"), 1)
                for e in range(2):
                    act.wait_ge(S("p3_turned"), 2 * i + e + 1)
                    act.activation(pT3[:, e, :], bank[e][:, 0:3 * P], ACT.Copy).then_inc(S("pT3"), 1)
                for e in range(2):
                    act.wait_ge(S("o3_done"), 2 * i + e + 1)
                    act.activation(big[:, bass.ds(2 * i + e, 1), :], bank[2 + e][:, 0:T], ACT.Copy).then_inc(S("o3"), 1)
                act.wait_ge(S("o3"), 2 * i + 2)
                act.sem_inc(S("free3"), 1)
            out_blocks(st_o3, "o_added", 2 * KB, 4, 16)
            ffn(6, st_f3, st_d3, 17, 5)
            norm(7, "x_ready", 6 * KB)
            for m in range(NT * KB // 4):
                act.wait_ge(S("turned"), 2 + KB // 2 + m + 1)
                n, g = divmod(m, KB // 4)
                act.activation(xtok[:, n, g * 512:(g + 1) * 512], bank[m % 2][:, :], ACT.Copy).then_inc(S("y_copied"), 1)

        @block.vector
        def _(dve):
            def ada_mac(m, c0, col):
                for k in range(KB):
                    if k % 4 == 0:
                        dve.wait_ge(S(f"ada_landed{k // 4}"), 16 * m + 16)
                    w = ada_w[:, k // 4, k % 4, :]
                    if k == 0:
                        if not (isinstance(m, int) and m == 0):
                            dve.wait_ge(S("ada_sum"), m)
                        dve.tensor_scalar(ada_acc[:, :], w, cact[:, c0:c0 + 1], None, ALU.mult).then_inc(S("ada_mac"), 1)
                    else:
                        dve.wait_ge(S("ada_mac"), 8 * m + k)
                        dve.scalar_tensor_tensor(ada_acc[:, :], w, cact[:, c0 + k:c0 + k + 1], ada_acc[:, :], ALU.mult, ALU.add)\
                           .then_inc(S("ada_mac"), 1)
                    if k % 4 == 3:
                        dve.wait_ge(S("ada_mac"), 8 * m + k + 1)
                        dve.sem_inc(S("ada_used"), 1)

            def ada_bias(m, col):
                dve.wait_ge(S("ada_sum"), m + 1)
                dve.tensor_tensor(mod[:, bass.ds(col, 4)], ADA_BANK[:, 0:4], bias_cols[:, bass.ds(col, 4)], ALU.add).then_inc(S("mod_ready"), 1)

            def norm_scale(n, w_col, sc_col):
                dve.wait_ge(S("nscale"), n + 1)
                dve.wait_ge(S("h_scaled"), KB * n + 1)
                dve.scalar_tensor_tensor(nscale[:, :], mod[:, sc_col:sc_col + KB], 1.0, vec_cols[:, w_col:w_col + KB], ALU.add, ALU.mult)\
                   .then_inc(S("nscale"), 1)
                dve.wait_ge(S("nscale"), n + 2)
                dve.wait_ge(S("rstd"), n + 1)

            def norm_apply(n, dst):
                for f in range(KB):
                    dve.scalar_tensor_tensor(dst[:, f, :], xT[:, f, :], nscale[:, f:f + 1], rstd[:, :], ALU.mult, ALU.mult)\
                       .then_inc(S("h_scaled"), 1)

            dve.memset(eps_col[:, :], EPS).then_inc(S("angle"), 1)
            dve.sem_inc(S("ada_used"), 2)
            dve.sem_inc(S("mod_ready"), 1)
            dve.sem_inc(S("h_scaled"), 1)
            dve.sem_inc(S("nscale"), 1)
            dve.sem_inc(S("mixed"), 2)
            dve.sem_inc(S("o_added"), 4)
            dve.sem_inc(S("d_added"), 2)
            dve.sem_inc(S("ffn_free"), 2)
            dve.wait_ge(S("rows_landed"), 16 * n_table_dmas)
            dve.tensor_copy(pos_f[:, :], pos_i[:, :]).then_inc(S("pos"), 1)
            dve.wait_ge(S("turned"), 2)
            dve.tensor_copy(pos_c[:, :], ADA_BANK[:, 0:NT]).then_inc(S("pos"), 1)
            dve.wait_ge(S("pos"), 2)
            dve.wait_ge(S("masks"), ROPE // 2 + 2)
            for t in range(NT):
                dve.tensor_scalar(angle[:, t, :], inv_freq[:, :], pos_c[:, t:t + 1], None, ALU.mult).then_inc(S("angle"), 1)
            dve.wait_ge(S("angle"), 1 + NT)
            TWO_PI, ROUND = 2 * np.pi, 1.5 * 2.0 ** 23
            n = 1 + NT
            for dst, src, scalar, op0, in1, op1 in (
                    (turns, angle, 1 / TWO_PI, ALU.mult, ROUND, ALU.add), (turns, turns, ROUND, ALU.subtract, None, None),
                    (sin_t, turns, -6.25, ALU.mult, angle, ALU.add), (sin_t, turns, -17 / 512, ALU.mult, sin_t, ALU.add),
                    (sin_t, turns, -(TWO_PI - 6.25 - 17 / 512), ALU.mult, sin_t, ALU.add),
                    (sin_t, sin_t, float(np.float32(3.1415925)), ALU.min, -float(np.float32(3.1415925)), ALU.max),
                    (cos_t, sin_t, TWO_PI / 4, ALU.add, None, None), (turns, cos_t, np.pi, ALU.is_gt, -TWO_PI, ALU.mult),
                    (cos_t, turns, 0.0, ALU.add, cos_t, ALU.add),
                    (cos_t, cos_t, float(np.float32(3.1415925)), ALU.min, -float(np.float32(3.1415925)), ALU.max)):
                if in1 is None:
                    ins = dve.tensor_scalar(dst[:, :, :], src[:, :, :], scalar, None, op0)
                elif isinstance(in1, float):
                    ins = dve.tensor_scalar(dst[:, :, :], src[:, :, :], scalar, in1, op0, op1)
                else:
                    ins = dve.scalar_tensor_tensor(dst[:, :, :], src[:, :, :], scalar, in1[:, :, :], op0, op1)
                ins.then_inc(S("angle"), 1)
                n += 1
                dve.wait_ge(S("angle"), n)
            dve.sem_inc(S("angles"), 1)
            dve.wait_ge(S("c_ready"), 1)
            for m in range(ADA_PRE):
                ada_mac(m, 0, 4 * m)
                ada_bias(m, 4 * m)
            dve.wait_ge(S("mod_ready"), 1 + ADA_PRE)
            norm_scale(0, V_N1, KB)
            norm_apply(0, hT)
            dve.wait_ge(S("gates_done"), 1)
            ps = bank[3][:, 0:NT * 2 * H1].rearrange("p (n k h) -> p n k h", n=NT, k=2)
            for n in range(NT):
                dve.tensor_tensor(ab_in[:, n, 0, :], ps[:, n, 0, :], head_rows[:, 0, :], ALU.add).then_inc(S("ab_part"), 1)
            dve.wait_ge(S("ab_part"), NT)
            dve.sem_inc(S("ab_copied"), 1)
            dve.tensor_copy(ab_in[:, :, 1, :], ps[:, :, 1, :]).then_inc(S("ab_copied"), 1)
            dve.wait_ge(S("ab_act"), 4)
            dve.scalar_tensor_tensor(ab_t[:, 0], ab_in[:, :, 0, :], 0.0, ab_t[:, 2], ALU.max, ALU.add).then_inc(S("ab_part"), 1)
            dve.wait_ge(S("ab_part"), NT + 1)
            for n in range(NT):
                dve.scalar_tensor_tensor(ab_t[:, 4, n], ab_t[:, 0, n], -1.0, head_rows[:, 1, :], ALU.mult, ALU.mult).then_inc(S("ab_part"), 1)
            dve.wait_ge(S("ab_part"), 2 * NT + 1)
            dve.sem_inc(S("g_ready"), 1)
            hvt = hv.rearrange("p h v -> p v h")
            dve.tensor_copy(hvt[:, 0:NT, :], ab_t[:, 4]).then_inc(S("hv"), 1)
            dve.wait_ge(S("ab_act"), 5)
            dve.tensor_scalar(ab_t[:, 1], ab_t[:, 3], 1.0, None, ALU.add).then_inc(S("ab_part"), 1)
            dve.wait_ge(S("ab_part"), 2 * NT + 2)
            dve.reciprocal(hvt[:, 2:2 + NT, :], ab_t[:, 1]).then_inc(S("hv"), 1)
            dve.wait_ge(S("gates_done"), 2)
            sums = bank[4][:, 0:8 * H1].rearrange("p (k h) -> p k h", h=H1)
            dve.tensor_copy(hvt[:, 4:4 + NT, :], sums[:, 0:NT, :]).then_inc(S("hv"), 1)
            dve.wait_ge(S("hv"), 3)
            dve.tensor_copy(hvt[:, 10:10 + NCH, :], sums[:, 2 * NT:2 * NT + NCH, :]).then_inc(S("ab_part"), 1)
            dve.wait_ge(S("ab_part"), 2 * NT + 3)
            dve.tensor_tensor(hvt[:, 8:8 + NT, :], sums[:, NT:2 * NT, :], hvt[:, 4:4 + NT, :], ALU.subtract).then_inc(S("hv"), 1)
            dve.wait_ge(S("hv_act"), 3)
            dve.tensor_tensor(hvt[:, 14:14 + NT, :], hvt[:, 6:6 + NT, :], hvt[:, 2:2 + NT, :], ALU.mult).then_inc(S("hv"), 1)
            dve.wait_ge(S("hv"), 5)

            def col(tile, first, i):
                return tile[:, first + i:first + i + 1] if isinstance(i, int) else tile[:, bass.ds(i + first, 1)]

            def part(tile, i):
                return tile[:, i, :] if isinstance(i, int) else tile[:, bass.ds(i, 1), :]

            def short_conv(i):
                n = i
                dve.wait_ge(S("evacuated"), st_h1.done(i, 5) + 3)
                x_in = scx_pad[:, TAPS2 - 1:TAPS2 - 1 + T]
                dve.tensor_tensor(x_in, x_in, scc, ALU.mult).then_inc(S("short"), 1)
                for k in range(TAPS2):
                    dve.wait_ge(S("short"), 5 * n + k + 1)
                    w = col(vec_cols, V_SC + k * KB, i)
                    if k == 0:
                        dve.tensor_scalar(scv, scx_pad[:, 0:T], w, None, ALU.mult).then_inc(S("short"), 1)
                    else:
                        dve.scalar_tensor_tensor(scv, scx_pad[:, k:k + T], w, scv, ALU.mult, ALU.add).then_inc(S("short"), 1)
                dve.wait_ge(S("short"), 5 * n + TAPS2 + 1)
                dve.tensor_tensor(part(ybin, i), scv, scb, ALU.mult).then_inc(S("short"), 1)

            def head1(i, gemm, chain):
                if not chain:
                    short_conv(i)
                    return
                n = i
                c = i - 1
                dve.tensor_copy(hcur, part(hv, c)).then_inc(S("hcur"), 1)
                dve.wait_ge(S("hcur"), n)
                for t in range(NT):
                    dve.tensor_scalar(gmat[:, t, :], causal[:, :], hcur[:, t:t + 1], None, ALU.mult).then_inc(S("gmat"), 1)
                    dve.tensor_scalar(gmat[:, NT + t, :], ident[:, :], hcur[:, 2 + t:3 + t], None, ALU.mult).then_inc(S("gmat"), 1)
                dve.wait_ge(S("evacuated"), st_h1.done(c, 2) + 3)
                for k in range(TAPS1):
                    for b in range(3):
                        w = col(conv_cols, k * 3 * KB + b * KB, c)
                        if k == 0:
                            dve.tensor_scalar(conv[:, b, :], qkv_pad[:, b, 0:T], w, None, ALU.mult).then_inc(S("conv"), 1)
                        else:
                            dve.wait_ge(S("conv"), 12 * c + 3 * k + b - 3 + 1)
                            dve.scalar_tensor_tensor(conv[:, b, :], qkv_pad[:, b, k:k + T], w, conv[:, b, :], ALU.mult, ALU.add)\
                               .then_inc(S("conv"), 1)
                dve.wait_ge(S("gb_done"), n)
                for t in range(NT):
                    dve.tensor_scalar(dec[:, t, :], bank[4][:, t * P:(t + 1) * P], hcur[:, 4 + t:5 + t], 0.0, ALU.subtract, ALU.min)\
                       .then_inc(S("dec_in"), 1)
                for t in range(NT):
                    dve.tensor_tensor(bstrict[:, t, :], bank[4][:, (NT + t) * P:(NT + t + 1) * P], strict[:, :], ALU.mult)\
                       .then_inc(S("dec_in"), 1)
                dve.wait_ge(S("qk_rn"), 2 * n)
                dve.scalar_tensor_tensor(kq[:, 1, :], act3[:, 0, :], float(P) ** -0.5, rn2[:, 0, :], ALU.mult, ALU.mult).then_inc(S("kq_ready"), 1)
                dve.tensor_tensor(kq[:, 0, :], act3[:, 1, :], rn2[:, 1, :], ALU.mult).then_inc(S("kq_ready"), 1)
                dve.wait_ge(S("dec"), 2 * n - 1)
                for t in range(NT):
                    dve.tensor_tensor(qkdec[:, t, :], dec[:, t, :], causal[:, :], ALU.mult).then_inc(S("masked"), 1)
                dve.wait_ge(S("dec_in"), 4 * n)
                dve.tensor_tensor(ldec, dec, bstrict, ALU.mult).then_inc(S("masked"), 1)
                dve.wait_ge(S("masked"), 3 * n)
                dve.wait_ge(S("kk_done"), n)
                kk = bank[5][:, :].rearrange("p (t w c) -> p t w c", t=NT, w=2)
                dve.tensor_tensor(LT, kk[:, :, 0, :], ldec, ALU.mult).then_inc(S("kk_used"), 1)
                dve.tensor_tensor(QKT, kk[:, :, 1, :], qkdec, ALU.mult).then_inc(S("kk_used"), 1)
                dve.wait_ge(S("kk_used"), 2 * n)
                for t in range(NT):
                    dve.tensor_tensor(LTm[:, :, t, :], LT[:, t:t + 1, :].broadcast_to([P, LEVELS, P]), halves[:, :, :], ALU.mult)\
                       .then_inc(S("levels"), 1)
                dve.wait_ge(S("levels"), 2 * n)
                idb = ident[:, :].rearrange("p (a b) -> p a b", a=1).broadcast_to([P, NT, P])
                dve.tensor_tensor(inv[:, 1], idb, LTm[:, 0], ALU.subtract).then_inc(S("inv"), 1)
                dve.wait_ge(S("x_done"), 6 * c + 1)
                dve.scalar_tensor_tensor(inv[:, 0], bank[3][:, 0:NT * P].rearrange("p (t c) -> p t c", t=NT), -1.0, idb, ALU.mult, ALU.add)\
                   .then_inc(S("inv"), 1)
                dve.wait_ge(S("dec"), 2 * n)
                dve.wait_ge(S("kq_ready"), 2 * n)
                dve.tensor_tensor(qg, kq[:, 1, :], egb, ALU.mult).then_inc(S("qg"), 1)
                for l in range(1, LEVELS):
                    dve.wait_ge(S("y_done"), 5 * c + l)
                    dve.wait_ge(S("inv"), 7 * c + l + 1)
                    flat = inv.rearrange("p a t c -> p (a t c)")
                    dve.tensor_tensor(flat, flat, bank[4][:, :], ALU.subtract).then_inc(S("inv"), 1)
                for ch in range(NCH):
                    t, r = ch // 2, slice(ch % 2 * CHUNK, ch % 2 * CHUNK + CHUNK)
                    dve.wait_ge(S("v_done"), 4 * c + ch + 1)
                    dve.tensor_copy(vnew[r, t, :], bank[3][r, t * P:(t + 1) * P]).then_inc(S("vnew"), 1)
                    if ch < NCH - 1:
                        dve.wait_ge(S("s_done"), 3 * c + ch + 1)
                        if ch == 0:
                            dve.tensor_copy(state, bank[4][:, 0:P]).then_inc(S("state"), 1)
                        else:
                            dve.wait_ge(S("state"), 3 * c + ch)
                            dve.scalar_tensor_tensor(state, state, hcur[:, 10 + ch:11 + ch], bank[4][:, 0:P], ALU.mult, ALU.add).then_inc(S("state"), 1)
                if gemm:
                    short_conv(i)
                dve.wait_ge(S("o_rn"), 2 * n)
                dve.scalar_tensor_tensor(onrm, bank[6][:, 0:T], vec_cols[:, V_GN:V_GN + 1], lnb[:, T:2 * T], ALU.mult, ALU.mult).then_inc(S("o_norm"), 1)
                dve.wait_ge(S("o_norm"), n)
                dve.wait_ge(S("silu"), 2 * n)
                dve.tensor_tensor(part(oall, c), part(oall, c), onrm, ALU.mult).then_inc(S("head_out"), 1)

            head1(0, True, False)
            with dve.Fori(1, H1) as i:
                head1(i, True, True)
                for q in range(2):
                    m = ADA_PRE + 2 * (i - 1) + q
                    mcol = (4 * ADA_PRE - 4 + 4 * i) if q == 0 else (8 * KB - 4 + 4 * i)
                    ada_mac(m, q * KB, mcol)
                    ada_bias(m, mcol)
            head1(H1, False, True)
            m = ADA_PRE + 2 * N_LOOP1
            dve.wait_ge(S("gates"), 2)
            with dve.Fori(0, st_p1.n) as i:
                for q in range(2):
                    dve.wait_ge(S("evacuated"), st_p1.done(i, 2 * q + 1) + 3)
                    for b in range(2):
                        dve.tensor_tensor(evac[:, 2 * q + b, :], evac[:, 2 * q + b, :], gates[:, bass.ds(2 * i + q + b * KB, 1), :], ALU.mult)\
                           .then_inc(S("gated"), 1)
                    dve.wait_ge(S("gated"), 4 * i + 2 * q + 2)
                    dve.tensor_tensor(hT[:, bass.ds(2 * i + q, 1), :], evac[:, 2 * q, :], evac[:, 2 * q + 1, :], ALU.add).then_inc(S("mix_ready"), 1)
                    dve.wait_ge(S("mix_ready"), 2 * i + q + 1)
                    dve.sem_inc(S("mixed"), 1)
                ada_mac(m + i, 0, 0)
                ada_bias(m + i, 4 * i + 6 * KB)
            m1 = m + st_p1.n

            with dve.Fori(0, st_o1.n) as i:
                for j in range(4):
                    dve.wait_ge(S("evacuated"), st_o1.done(i, j) + 3)
                    xf = xT[:, bass.ds(4 * i + j, 1), :]
                    dve.tensor_tensor(xf, xf, evac[:, j, :], ALU.add).then_inc(S("o_added"), 1)
                ada_mac(m1 + i, KB, 0)
                ada_bias(m1 + i, 48 * i + 64 + 44)
            dve.wait_ge(S("o_added"), 4 + KB)
            dve.sem_inc(S("x_ready"), KB)
            m2 = m1 + st_o1.n
            norm_scale(1, V_N2, 4 * KB)
            norm_apply(1, hT)
            with dve.Fori(0, st_f1.n) as i:
                for q in range(2):
                    dve.wait_ge(S("evacuated"), st_f1.done(i, 2 * q + 1) + 3)
                    dve.tensor_tensor(big[:, bass.ds(2 * i + q, 1), :], evac[:, 2 * q, :], evac[:, 2 * q + 1, :], ALU.mult).then_inc(S("ffn_act"), 1)
                    dve.wait_ge(S("ffn_act"), 2 * i + q + 1)
                    dve.sem_inc(S("ffn_free"), 1)
                ada_mac(m2 + i, KB, 0)
                ada_bias(m2 + i, 4 * i + 64 + 48)
            m3 = m2 + st_f1.n
            with dve.Fori(0, st_d1.n) as i:
                for j in range(2):
                    dve.wait_ge(S("evacuated"), st_d1.done(i, j) + 3)
                    xf = xT[:, bass.ds(2 * i + j, 1), :]
                    dve.tensor_tensor(xf, xf, evac[:, j, :], ALU.add).then_inc(S("d_added"), 1)
                ada_mac(m3 + i, KB, 0)
                ada_bias(m3 + i, 4 * i + 64 + 4 * N_LOOP1)
            dve.wait_ge(S("d_added"), 2 + KB)
            dve.sem_inc(S("x_ready"), KB)
            norm_scale(2, V_NF, 7 * KB)
            norm_apply(2, xT)
            norm_scale(3, *NORMS[3])
            norm_apply(3, hT)
            dve.memset(segment, 1.0).then_inc(S("segment"), 1)
            dve.wait_ge(S("segment"), 1)
            dve.memset(segment.rearrange("p (c k) -> p c k", k=CHUNK)[:, :, 0:1], 0.0).then_inc(S("segment"), 1)
            dve.memset(kt, 0.0).then_inc(S("segment"), 1)
            for l in range(LEVELS):
                b = 1 << l
                dve.tensor_copy(halves_c[:, l, :].rearrange("p (n b) -> p n b", b=b), halves[:, l, :].rearrange("p (n h b) -> p n h b", h=2, b=b)[:, :, 1, :])\
                   .then_inc(S("segment"), 1)
            dve.wait_ge(S("gate_act"), H2 + 4)
            dve.scalar_tensor_tensor(gl_m, gb, 0.0, gl_a, ALU.min, ALU.subtract).then_inc(S("gate_log"), 1)
            dve.wait_ge(S("gate_log"), 1)
            dve.wait_ge(S("segment"), 3 + LEVELS)
            dve.tensor_tensor_scan(gb.rearrange("p h t -> p (h t)"), segment, gl_m.rearrange("p h t -> p (h t)"), 0.0, ALU.mult, ALU.add)\
               .then_inc(S("gate_log"), 1)
            dve.wait_ge(S("gate_log"), 2)

            def head2(i):
                n, c = i, i - 1
                cum = expo[:, 7 * T:8 * T]
                dve.tensor_copy(cum, part(gb, c)).then_inc(S("expo"), 1)
                dve.wait_ge(S("expo"), 14 * c + 1)
                for l in range(LEVELS):
                    b = 1 << l
                    v = cum.rearrange("p (n h b) -> p n h b", h=2, b=b)
                    ref = v[:, :, 0, b - 1:b].broadcast_to([P, T // (2 * b), b])
                    e = expo[:, l * T:(l + 1) * T].rearrange("p (h n b) -> p h n b", h=2, b=b)
                    dve.tensor_tensor(e[:, 0], ref, v[:, :, 0, :], ALU.subtract).then_inc(S("expo"), 1)
                    dve.tensor_tensor(e[:, 1], v[:, :, 1, :], ref, ALU.subtract).then_inc(S("expo"), 1)
                v = cum.rearrange("p (n k) -> p n k", k=CHUNK)
                dve.tensor_tensor(expo[:, 6 * T:7 * T].rearrange("p (n k) -> p n k", k=CHUNK), v[:, :, CHUNK - 1:CHUNK].broadcast_to([P, NCH, CHUNK]), v,
                                  ALU.subtract).then_inc(S("expo"), 1)
                dve.wait_ge(S("evacuated"), st_h2.done(c, 5) + 3)
                q, k = qkv2[:, 0, :], qkv2[:, 1, :]
                dve.tensor_tensor(qk2, q, k, ALU.mult).then_inc(S("scaled2"), 1)
                dve.wait_ge(S("expo_done"), 2 * n)
                dve.tensor_tensor(kd, k, expo[:, 6 * T:7 * T], ALU.mult).then_inc(S("scaled2"), 1)
                for l in range(LEVELS):
                    b = 1 << l
                    e = expo[:, l * T:(l + 1) * T].rearrange("p (h n b) -> p h n b", h=2, b=b)
                    kv, qv = (w.rearrange("p (n h b) -> p n h b", h=2, b=b) for w in (k, q))
                    dve.tensor_tensor(kt[:, l, :].rearrange("p (n h b) -> p n h b", h=2, b=b)[:, :, 0, :], kv[:, :, 0, :], e[:, 0], ALU.mult)\
                       .then_inc(S("scaled2"), 1)
                    dve.tensor_tensor(qt[:, l].rearrange("p t k -> p (t k)").rearrange("p (n b) -> p n b", b=b), qv[:, :, 1, :], e[:, 1], ALU.mult)\
                       .then_inc(S("scaled2"), 1)
                dve.tensor_tensor(qe, q, cum, ALU.mult).then_inc(S("scaled2"), 1)
                dve.wait_ge(S("att_done"), n)
                for t in range(NT):
                    dve.tensor_copy(qk_col[:, t:t + 1], bank[3 + t][:, 2 * T - 1:2 * T]).then_inc(S("att_l"), 1)
                    dve.tensor_tensor(att_l[:, t], bank[3 + t][:, 0:LEVELS * CHUNK].rearrange("p (l k) -> p l k", l=LEVELS), halves_c, ALU.mult)\
                       .then_inc(S("att_l"), 1)
                dve.wait_ge(S("att_l"), 4 * n)
                for t in range(NT):
                    dve.tensor_scalar(att[:, t, :], ident[:, :], qk_col[:, t:t + 1], None, ALU.mult).then_inc(S("att"), 1)
                for l in range(LEVELS):
                    b = 1 << l
                    dve.wait_ge(S("att"), 8 * c + l + 2)
                    v = att.rearrange("p t (n h b) -> p t n h b", h=2, b=b)[:, :, :, 1, :]
                    dve.tensor_tensor(v, v, att_l[:, :, l, :].rearrange("p t (n b) -> p t n b", b=b), ALU.add).then_inc(S("att"), 1)
                dve.wait_ge(S("kv_done"), 3 * c + 2)
                dve.tensor_copy(states[:, 0, :], bank[6][:, 0:T]).then_inc(S("state2"), 1)
                for ch in range(1, NCH - 1):
                    dve.wait_ge(S("state2"), 3 * c + ch)
                    if ch == 2:
                        dve.wait_ge(S("kv_done"), 3 * c + 3)
                    last = cum[:, (ch + 1) * CHUNK - 1:(ch + 1) * CHUNK]
                    dve.scalar_tensor_tensor(states[:, ch, :], states[:, ch - 1, :], last, bank[6][:, (ch % 2) * T:(ch % 2 + 1) * T], ALU.mult, ALU.add)\
                       .then_inc(S("state2"), 1)
                dve.wait_ge(S("o2_rn"), 2 * n)
                for d in range(DV2):
                    dve.scalar_tensor_tensor(on2[:, d, :], bank[5][:, d * T:(d + 1) * T], vec_cols[:, V_GG + d:V_GG + d + 1], lnb[:, T:2 * T],
                                             ALU.mult, ALU.mult).then_inc(S("o2_norm"), 1)
                dve.wait_ge(S("o2_norm"), 2 * n)
                dve.wait_ge(S("expo_done"), 2 * n)
                r = big[:, bass.ds(2 * i - 2, 2), :] if not isinstance(i, int) else big[:, 2 * i - 2:2 * i, :]
                dve.tensor_tensor(r, r, on2, ALU.mult).then_inc(S("head2_out"), 1)

            with dve.Fori(1, H2) as i:
                head2(i)
            head2(H2)

            def add_blocks(st, per, sem, base):
                with dve.Fori(0, st.n) as i:
                    for j in range(per):
                        dve.wait_ge(S("evacuated"), st.done(i, j) + 3)
                        xf = xT[:, bass.ds(per * i + j, 1), :]
                        dve.tensor_tensor(xf, xf, evac[:, j, :], ALU.add).then_inc(S(sem), 1)
                dve.wait_ge(S(sem), base)
                dve.sem_inc(S("x_ready"), KB)

            def ffn(n, st_f, st_d):
                norm_scale(n, *NORMS[n])
                norm_apply(n, hT)
                base = (n // 2 - 1) * FB
                with dve.Fori(0, st_f.n) as i:
                    for q in range(2):
                        dve.wait_ge(S("evacuated"), st_f.done(i, 2 * q + 1) + 3)
                        dve.tensor_tensor(big[:, bass.ds(2 * i + q, 1), :], evac[:, 2 * q, :], evac[:, 2 * q + 1, :], ALU.mult).then_inc(S("ffn_act"), 1)
                        dve.wait_ge(S("ffn_act"), base + 2 * i + q + 1)
                        dve.sem_inc(S("ffn_free"), 1)
                add_blocks(st_d, 2, "d_added", 2 + (n // 2) * KB)

            add_blocks(st_o2, 4, "o_added", 4 + 2 * KB)
            ffn(4, st_f2, st_d2)
            norm_scale(5, *NORMS[5])
            norm_apply(5, hT)
            for q in (0, 2):
                dve.tensor_scalar(neg3[:, q, :], causal_q[:, :], 1.0, 1e30, ALU.subtract, ALU.mult).then_inc(S("neg3"), 1)
            dve.memset(neg3[:, 1, :], 0.0).then_inc(S("neg3"), 1)

            def rotate(dst, src, tmp, sem, base, name):
                v = src.rearrange("p t (f two) -> p t f two", two=2)
                for q, (part_, table) in enumerate(((0, cos_t), (1, sin_t), (0, sin_t), (1, cos_t))):
                    dve.tensor_tensor(tmp[:, q], v[:, :, :, part_], table[:, :, :], ALU.mult).then_inc(S(name), 1)
                dve.wait_ge(S(name), base + 4)
                dve.tensor_tensor(dst[:, :, 0:ROPE // 2], tmp[:, 0], tmp[:, 1], ALU.subtract).then_inc(S(sem), 1)
                dve.tensor_tensor(dst[:, :, ROPE // 2:ROPE], tmp[:, 2], tmp[:, 3], ALU.add).then_inc(S(sem), 1)

            dve.wait_ge(S("k_raw"), NT)
            dve.wait_ge(S("rotary"), 2)
            for e in range(2):
                rotate(k_rot[:, :, e], lat[:, :, QR + KVR:MLA_COLS], rot_u[:, e], "k_rot", 4 * e, "k_rot_t")
            dve.wait_ge(S("neg3"), 3)
            SCALE3 = float(NOPE + ROPE) ** -0.5
            with dve.Fori(0, st_h3.n) as i:
                for e in range(2):
                    dve.wait_ge(S("evacuated"), st_h3.done(i, 2 * e + 1) + 3)
                    rotate(q_rot[:, :, e], vr[:, e, NT * NOPE:].rearrange("p (t f) -> p t f", t=NT), rot_u[:, e], "q_rot", 8 * i + 4 * e, "q_rot_t")
                for e in range(2):
                    dve.wait_ge(S("score3"), 2 * i + e + 1)
                    dve.tensor_tensor(sc3[:, e, :], bank[5 + e][:, 0:3 * P], neg3.rearrange("p a b -> p (a b)"), ALU.add).then_inc(S("sc3"), 1)
                for e in range(2):
                    dve.wait_ge(S("sc3"), 2 * i + e + 1)
                    for t in range(NT):
                        dve.tensor_reduce(mx3[:, e, t:t + 1], sc3[:, e, (t * P):(3 * P if t else P)], AX_X, ALU.max).then_inc(S("mx3"), 1)
                    dve.wait_ge(S("mx3"), 4 * i + 2 * e + 2)
                    dve.tensor_scalar(nm3[:, e, :], mx3[:, e, :], -SCALE3, None, ALU.mult).then_inc(S("nm3"), 1)
                for e in range(2):
                    dve.wait_ge(S("exp3"), 4 * i + 2 * e + 2)
                    dve.reciprocal(inv3[:, e, :], sum3[:, e, :]).then_inc(S("inv3"), 1)
                    dve.wait_ge(S("inv3"), 2 * i + e + 1)
                    for t in range(NT):
                        cols = slice(t * P, 3 * P if t else P)
                        dve.tensor_scalar(p3[:, e, cols], p3[:, e, cols], inv3[:, e, t:t + 1], None, ALU.mult).then_inc(S("p3"), 1)
            add_blocks(st_o3, 4, "o_added", 4 + 3 * KB)
            ffn(6, st_f3, st_d3)
            dve.wait_ge(S("rstd"), 8)
            for f in range(KB):
                dve.scalar_tensor_tensor(hT[:, f, :], xT[:, f, :], vec_cols[:, V_FIN + f:V_FIN + f + 1], rstd[:, :], ALU.mult, ALU.mult)\
                   .then_inc(S("h_scaled"), 1)


def kernel(**inputs):
    from concourse import bacc
    from concourse.bass_utils import run_bass_kernel_spmd

    nc = bacc.Bacc("TRN2", target_bir_lowering=False, num_devices=1)
    arrays, views = {}, {}
    for name, value in inputs.items():
        value = np.ascontiguousarray(value)
        arrays[f"in_{name}"] = value
        views[name] = nc.dram_tensor(f"in_{name}", value.shape, mybir.dt.from_np(value.dtype), kind="ExternalInput").ap()
    shape = arrays["in_x"].shape
    out = nc.dram_tensor("out", shape, F32, kind="ExternalOutput").ap()
    program(nc, views, out)
    result = run_bass_kernel_spmd(nc, [arrays], core_ids=[0])
    return result.results[0]["out"]
```

```python
from contextlib import ExitStack

import numpy as np

import concourse.bass as bass
from concourse import mybir

F32 = mybir.dt.float32
I32 = mybir.dt.int32
ALU = mybir.AluOpType
ACT = mybir.ActivationFunctionType
AX_X = mybir.AxisListType.X

P = 128
EPS = 1e-6
CHUNK = 64
LEVELS = 6


class Signals:

    def __init__(self, ctx, nc):
        self.ctx, self.nc, self.made = ctx, nc, {}

    def __call__(self, name):
        if name not in self.made:
            self.made[name] = self.ctx.enter_context(self.nc.semaphore(name))
        return self.made[name]


class Stream:

    slots_filled = {}
    slot_user = {}
    blocks = 0

    def __init__(self, n, per, first, wide=1):
        cls = Stream
        self.n, self.per, self.wide = n, per, wide
        self.slots = [first + j * wide for j in range(per)]
        self.block0 = cls.blocks
        self.fill0, self.free = [], []
        for j, s in enumerate(self.slots):
            spans = range(s, s + wide)
            self.free.append(max(cls.slot_user.get(x, 0) for x in spans))
            self.fill0.append(cls.slots_filled.get(s, 0))
            cls.slots_filled[s] = self.fill0[-1] + n
            for x in spans:
                cls.slot_user[x] = self.block0 + (n - 1) * per + j + 1
        cls.blocks += n * per
        self.end = cls.blocks

    def landed(self, i, j):
        return 16 * self.fill0[j] + 16 * i + 16

    def done(self, i, j):
        return self.block0 + i * self.per + j + 1


def program(nc, a, out):
    x, c1, c2, pos = a["x"], a["c"], a["c_2"], a["positions_2"]
    SEQ, D = x.shape[1:]
    KB = D // P
    NT = SEQ // P
    NCH = SEQ // CHUNK
    H1 = a["gdn_a_log"].shape[1]
    W_QKV = a["gdn_conv_w"].shape[2]
    TAPS1, TAPS2 = a["gdn_conv_w"].shape[1], a["sc_conv_w"].shape[1]
    DFF = a["w_ffn_out"].shape[1]
    FB = DFF // P
    Q_OFF, K_OFF, V_OFF, Z_OFF = 0, D, 2 * D, 3 * D
    AB_OFF = 4 * D
    SCB_OFF = AB_OFF + 2 * H1
    SCC_OFF, SCX_OFF, GA_OFF, GB_OFF = (SCB_OFF + n * D for n in (1, 2, 3, 4))
    H2 = 4
    DK2 = a["gla_w_gate_2"].shape[2] // H2
    RANK = a["gla_w_gate_2"].shape[1]
    TAU = 16.0
    R_OFF2 = 2 * H2 * DK2 + D
    H3 = 8
    NOPE, ROPE = 128, 64
    QR, KVR = a["mla_w_q_up_2"].shape[1], a["mla_w_kv_up_2"].shape[1]
    QB, KVB = QR // P, KVR // P
    MLA_COLS = QR + KVR + ROPE
    ADA = 512
    T = SEQ

    ctx = ExitStack()
    with ctx:
        S = Signals(ctx, nc)

        def sb(name, shape, dt=F32):
            return ctx.enter_context(nc.sbuf_tensor(name, shape, dt))

        bank = [ctx.enter_context(nc.psum_tensor(f"bank{n}", [P, 512], F32)) for n in range(8)]
        ADA_BANK = bank[7]

        HALF = 9
        SLOT = KB * P
        ring = sb("ring", [P, 2 * HALF * SLOT])
        ada_w = sb("ada_w", [P, 2, KB // 2, ADA])
        ada_acc = sb("ada_acc", [P, ADA])
        xT = sb("xT", [P, KB, T])
        hT = sb("hT", [P, KB, T])
        big = sb("big", [P, 4 * KB, T])
        rstd = sb("rstd", [P, T])
        lnb = sb("lnb", [P, 2 * T])
        ident = sb("ident", [P, P])
        ones = sb("ones", [P, P])
        halves = sb("halves", [P, LEVELS, P])
        causal = sb("causal", [P, P])
        strict = sb("strict", [P, P])
        chunk_ones = sb("chunk_ones", [P, P])
        chunk_rows = sb("chunk_rows", [P, 2, P])
        vrows = sb("vrows", [P, 3, P])
        bias_cols = sb("bias_cols", [P, 160])
        vec_cols = sb("vec_cols", [P, 92])
        n1_cols = sb("n1_cols", [P, KB])
        conv_cols = sb("conv_cols", [P, TAPS1 * W_QKV // P])
        mod = sb("mod", [P, 160])
        nscale = sb("nscale", [P, KB])
        cact = sb("cact", [P, 2 * KB])
        evac = sb("evac", [P, 4, T])
        wab = sb("wab", [P, KB, 2 * H1])
        head_rows = sb("head_rows", [P, 2, H1])

        xtok = big[:, 0:KB, :].rearrange("p b t -> p (b t)").rearrange("p (n d) -> p n d", n=NT)
        sq = big[:, 3 * KB:4 * KB, :]

        def rows(ap, n):
            return ap.rearrange("(r p) -> r p", p=P) if len(ap.shape) == 1 else ap.rearrange("a (r p) -> (a r) p", p=P)

        V_N2, V_NF, V_MIX, V_FFN2, V_FIN = 0, 8, 16, 32, 48
        V_SC, V_GN, V_GG, V_GQ, V_GKV, V_BG, V_END = 56, 80, 81, 83, 86, 88, 92
        tables = [
            [(0, rows(a["b_ada_f"], 16)), (16, rows(a["ada_b_2"], 96))],
            [(V_N2, rows(a["norm2_w"], 8)), (V_NF, rows(a["normf_w"], 8)),
             (V_MIX, rows(a["norm_mix_2"], 16)), (V_FFN2, rows(a["norm_ffn_2"], 16)), (V_FIN, rows(a["final_norm_2"], 8)),
             (V_SC, a["sc_conv_w"][0].rearrange("k (r p) -> (k r) p", p=P)),
             (V_GN, a["gdn_norm_w"]), (V_GG, rows(a["gla_g_out_2"], 2)), (V_GQ, rows(a["mla_g_q_2"], 3)),
             (V_GKV, rows(a["mla_g_kv_2"], 2)), (V_BG, rows(a["gla_b_gate_2"], 4))],
            [(0, a["gdn_conv_w"][0].rearrange("k (r p) -> (k r) p", p=P))],
        ]
        table_rows = [112, V_END, TAPS1 * W_QKV // P]
        n_table_dmas = sum(len(t) for t in tables) + 4
        crows = sb("crows", [72, P])

        SCRATCH = 12034
        scratch = sb("scratch", [P, SCRATCH])
        taken = [0]

        def piece(shape):
            n = int(np.prod(shape))
            ap = scratch[:, taken[0]:taken[0] + n]
            taken[0] += n
            assert taken[0] <= SCRATCH, taken[0]
            if len(shape) == 2:
                ap = ap.rearrange("p (a b) -> p a b", a=shape[0])
            elif len(shape) == 3:
                ap = ap.rearrange("p (a b c) -> p a b c", a=shape[0], b=shape[1])
            elif len(shape) == 4:
                ap = ap.rearrange("p (a b c d) -> p a b c d", a=shape[0], b=shape[1], c=shape[2])
            return ap

        PAD = TAPS1 - 1
        NHV = 16
        qkv_pad = piece((3, T + PAD))
        conv = piece((3, T))
        act3 = piece((3, T))
        sq2 = piece((2, T))
        rn2 = conv[:, 0:2, :]
        kq = piece((2, T))
        gmat = piece((4, P))
        dec = piece((NT, P))
        egb = piece((NT * P,))
        bstrict = piece((NT, P))
        qkdec = piece((NT, P))
        ldec = piece((NT, P))
        LT = piece((NT, P))
        o_ln, o_rn = egb, ldec.rearrange("p t c -> p (t c)")
        QKT = piece((NT, P))
        LTm = piece((LEVELS, NT, P))
        kdec = piece((NT, P))
        kbeg = piece((NT, P))
        vb = piece((NT, P))
        inv = piece((2, NT, P))
        xs = piece((NT, P))
        wz = piece((NCH, P))
        vnew = piece((NT, P))
        state = piece((P,))
        qg = piece((NT * P,))
        onrm = piece((NT * P,))
        scb = piece((T,))
        scc = piece((T,))
        scx_pad = piece((T + TAPS2 - 1,))
        scv = piece((T,))
        hv = piece((H1, NHV))
        hcur = piece((NHV,))
        ab_in = piece((NT, 2, H1))
        ab_t = piece((5, NT, H1))

        taken[0] = 0
        DV2 = 2
        gb = piece((H2, T))
        expo = piece((8 * T,))
        gl_a, gl_m = (expo[:, n * H2 * T:(n + 1) * H2 * T].rearrange("p (h t) -> p h t", h=H2) for n in range(2))
        qkv2 = piece((4, T))
        kt = piece((LEVELS, T))
        qt = piece((LEVELS, NT, CHUNK))
        halves_c = piece((LEVELS, CHUNK))
        qe = piece((T,))
        kd = piece((T,))
        qk2 = piece((T,))
        kd_tok = piece((NT, P))
        v_tok = piece((NT, DV2 * P))
        qk_col = piece((NT,))
        segment = piece((H2 * T,))
        taken[0] -= H2 * T
        att_l = piece((NT, LEVELS, CHUNK))
        att = piece((NT, P))
        states = piece((NCH - 1, DV2 * P))
        sq_o = piece((DV2, T))
        on2 = piece((DV2, T))
        wglr = piece((KB, RANK))
        glr = piece((T,))
        wgate = piece((H2 * DK2,))

        taken[0] = 0
        lat = piece((NT, QR + KVR + ROPE))
        lat_sq = piece((QR,))
        lat_ss = piece((NT, 2))
        lat_ln = piece((NT, 2))
        lat_rn = piece((NT, 2))
        cqT = piece((QB, T))
        ckvT = piece((KVB, T))
        krT = piece((T,))
        k_rot = piece((NT, 2, ROPE))
        qkT = piece((2, 2, T))
        vr = piece((2, NT * (NOPE + ROPE)))
        q_rot = piece((NT, 2, ROPE))
        rot_u = piece((2, 4, NT, ROPE // 2))
        qrT = piece((T,))
        neg3 = piece((3, P))
        sc3 = piece((2, 3 * P))
        p3 = piece((2, 3 * P))
        mx3 = piece((2, NT))
        nm3 = piece((2, NT))
        sum3 = piece((2, NT))
        inv3 = piece((2, NT))
        pT3 = piece((2, 3 * P))

        pos_i = sb("pos_i", [NT, P], I32)
        pos_f = sb("pos_f", [NT, P])
        pos_c = sb("pos_c", [P, NT])
        inv_freq = sb("inv_freq", [P, ROPE // 2])
        angle = sb("angle", [P, NT, ROPE // 2])
        turns = sb("turns", [P, NT, ROPE // 2])
        sin_t = sb("sin_t", [P, NT, ROPE // 2])
        cos_t = sb("cos_t", [P, NT, ROPE // 2])

        oall, ybin = big[:, 0:KB, :], big[:, KB:2 * KB, :]
        gates = big[:, 2 * KB:4 * KB, :]

        Stream.slots_filled, Stream.slot_user, Stream.blocks = {}, {}, 0
        st_h1 = Stream(H1, 9, 0)
        st_pb = Stream(1, 8, HALF)
        st_pa = Stream(KB // 2, 2, 0)
        st_o1 = Stream(KB // 4, 4, 4)
        st_f1 = Stream(FB // 2, 4, HALF)
        st_d1 = Stream(KB // 2, 2, 0, wide=3)

        st_h2 = Stream(H2, 6, HALF)
        st_o2 = Stream(KB // 4, 4, 0)
        st_f2 = Stream(FB // 2, 4, HALF)
        st_d2 = Stream(KB // 2, 2, 0, wide=3)
        st_lat = Stream(1, 1, HALF, wide=6)
        st_h3 = Stream(H3 // 2, 4, 0)
        st_o3 = Stream(KB // 4, 4, HALF)
        st_f3 = Stream(FB // 2, 4, 0)
        st_d3 = Stream(KB // 2, 2, HALF, wide=3)

        def slot(s, kb=KB, n=P):
            return ring[:, s * SLOT:s * SLOT + kb * n].rearrange("p (k n) -> p k n", k=kb)

        SPREAD1 = [4, 8, 14, 0, 12] + [2, 2] * (LEVELS - 1) + [2] + [2] * 6 + [0]
        SPREAD1[-1] = 9 * KB - sum(SPREAD1)
        assert SPREAD1[-1] >= 0, SPREAD1
        run1 = np.cumsum(SPREAD1)
        ready_step = [int(np.argmax(run1 >= KB * (j + 1))) for j in range(9)]
        w_in = a["w_in"][0]
        head_cols = [Q_OFF, K_OFF, V_OFF, Z_OFF, SCB_OFF, SCC_OFF, SCX_OFF, GA_OFF, GB_OFF]

        G2 = 8
        STEPS2 = 6
        ready_step2 = [-(-KB * (j + 1) // G2) for j in range(6)]
        head_cols2 = [(R_OFF2, 2), (R_OFF2 + P, 2), (2 * H2 * DK2, 2), (2 * H2 * DK2 + P, 2), (0, 1), (H2 * DK2, 1)]
        NORMS = [(None, KB), (V_N2, 4 * KB), (V_NF, 7 * KB), (V_MIX, 9 * KB), (V_FFN2, 12 * KB), (V_MIX + KB, 15 * KB),
                 (V_FFN2 + KB, 18 * KB)]

        def kview(w):
            return w.rearrange("(k p) n -> p k n", p=P)

        PRE = 5
        early = [ada_w[:, :].rearrange("p a k n -> p (a k) n")] + \
                [ring[:, s * SLOT:(s + 4) * SLOT].rearrange("p (k n) -> p k n", k=KB) for s in (HALF, HALF + 4)] + \
                [big[:, KB:3 * KB, :].rearrange("p b t -> p (b t)").rearrange("p (k n) -> p k n", k=KB)]
        acc_early = [ada_acc[:, :], LTm.rearrange("p a b c -> p (a b c)")[:, 0:ADA]]
        M_HEAD, M_PROJ = PRE, PRE + H1 - 1
        M_WO = M_PROJ + st_pa.n
        M_FFN1 = M_WO + st_o1.n
        M_FFN2 = M_FFN1 + st_f1.n

        eps_col = sb("eps_col", [P, 1])
        causal_q = sb("causal_q", [P, P])
        block = ctx.enter_context(nc.Block())

        @block.sync
        def _(sp):
            def load_ada(m, w, col):
                u = m - len(early) + 1
                for h in range(2):
                    sp.wait_ge(S("ada_used"), 2 * u + h - 1)
                    rows = w[:, h * D // 2:(h + 1) * D // 2, bass.ds(col, ADA)].rearrange("l (k p) n -> p (l k) n", p=P)
                    sp.dma_start(ada_w[:, h], rows).then_inc(S(f"ada_landed{h}"), 16)

            def load_block(st, i, j, src):
                sp.dma_start(src[0], src[1]).then_inc(S(f"landed{st.slots[j]}"), 16)

            def stream(st, src, extra=None, used=lambda j: j):
                for j in range(st.per):
                    if st.free[j]:
                        sp.wait_ge(S("gemm_done"), st.free[j])
                    load_block(st, 0, j, src(0, j))
                if extra:
                    extra(0)
                with sp.Fori(1, st.n) as i:
                    for j in range(st.per):
                        sp.wait_ge(S("gemm_done"), st.done(i - 1, used(j)))
                        load_block(st, i, j, src(i, j))
                        if extra and j == (st.per - 1) // 2:
                            extra(i)

            sp.dma_start(crows[0:KB, :], rows(c1, KB)).then_inc(S("c_landed"), 16)
            sp.dma_start(crows[KB:2 * KB, :], rows(c2, KB)).then_inc(S("c_landed"), 16)
            sp.dma_start(crows[2 * KB:3 * KB, :], rows(a["norm1_w"], KB)).then_inc(S("c_landed"), 16)
            sp.dma_start(crows[3 * KB:9 * KB, :], rows(a["b_ada"], 6 * KB)).then_inc(S("c_landed"), 16)
            sp.dma_start(xtok, x[0].rearrange("(n p) d -> p n d", p=P)).then_inc(S("x_landed"), 16)
            for m, dst in enumerate(early):
                sp.dma_start(dst, kview(a["w_ada"][0])[:, :, m * ADA:(m + 1) * ADA]).then_inc(S(f"early{m}"), 16)
            for n, table in enumerate(tables):
                for r, src in table:
                    sp.dma_start(vrows[r:r + src.shape[0], n, :], src).then_inc(S("rows_landed"), 16)
            sp.dma_start(wab[:, :, :], kview(w_in)[:, :, AB_OFF:AB_OFF + 2 * H1]).then_inc(S("rows_landed"), 16)
            sp.dma_start(head_rows[:, 0, :], a["gdn_dt_bias"].broadcast_to([P, H1])).then_inc(S("rows_landed"), 16)
            sp.dma_start(head_rows[:, 1, :], a["gdn_a_log"].broadcast_to([P, H1])).then_inc(S("rows_landed"), 16)
            sp.dma_start(pos_i[:, :], pos.rearrange("a (n p) -> (a n) p", p=P)).then_inc(S("rows_landed"), 16)
            wv = kview(w_in)

            def ada1(i):
                load_ada(PRE - 1 + i, a["w_ada"], (PRE - 1) * ADA + i * ADA)

            stream(st_h1, lambda i, j: (slot(st_h1.slots[j]), wv[:, :, bass.ds(i * P + head_cols[j], P)]), extra=ada1)
            wa, wb = kview(a["w_gdn_proj"][0]), kview(a["w_sc_out"][0])
            for j in range(st_pb.per):
                load_block(st_pb, 0, j, (slot(st_pb.slots[j]), wb[:, :, j * P:(j + 1) * P]))

            def ada2(i):
                load_ada(M_PROJ + i, a["w_ada_f"].rearrange("(l k) n -> l k n", l=1), i * ADA)

            stream(st_pa, lambda i, j: (slot(st_pa.slots[j]), wa[:, :, bass.ds(i * 2 * P + j * P, P)]), extra=ada2)
            wo = kview(a["w_o"][0])

            def ada3(i):
                load_ada(M_WO + i, a["ada_w_2"][bass.ds(i, 1)], 11 * ADA)

            stream(st_o1, lambda i, j: (slot(st_o1.slots[j]), wo[:, :, bass.ds(i * 4 * P + j * P, P)]), extra=ada3)
            wf = kview(a["w_ffn_in"][0])

            def ada4(i):
                load_ada(M_FFN1 + i, a["ada_w_2"][0:1], i * ADA)

            stream(st_f1, lambda i, j: (slot(st_f1.slots[j]), wf[:, :, bass.ds(i * 2 * P + (j // 2) * P + (j % 2) * DFF, P)]), extra=ada4)
            wd = kview(a["w_ffn_out"][0])
            stream(st_d1, lambda i, j: (slot(st_d1.slots[j], FB), wd[:, :, bass.ds(i * 2 * P + j * P, P)]))

            wg = kview(a["gla_w_in_2"][0])
            sp.wait_ge(S("head_out"), H1)
            sp.dma_start(wglr, wg[:, :, R_OFF2 + D:R_OFF2 + D + RANK]).then_inc(S("glr_landed"), 16)
            sp.dma_start(wgate[0:RANK, :], a["gla_w_gate_2"][0]).then_inc(S("glr_landed"), 16)
            stream(st_h2, lambda i, j: (slot(st_h2.slots[j]), wg[:, :, bass.ds(i * (P * head_cols2[j][1]) + head_cols2[j][0], P)]))
            wo2 = kview(a["gla_w_out_2"][0])
            stream(st_o2, lambda i, j: (slot(st_o2.slots[j]), wo2[:, :, bass.ds(i * 4 * P + j * P, P)]))

            def ffn_stream(st_f, st_d, layer, extra=None):
                wf, wd = kview(a["ffn_w_in_2"][layer]), kview(a["ffn_w_out_2"][layer])
                stream(st_f, lambda i, j: (slot(st_f.slots[j]), wf[:, :, bass.ds(i * 2 * P + (j // 2) * P + (j % 2) * DFF, P)]), extra)
                stream(st_d, lambda i, j: (slot(st_d.slots[j], FB), wd[:, :, bass.ds(i * 2 * P + j * P, P)]))

            ffn_stream(st_f2, st_d2, 0, lambda i: load_ada(M_FFN2 + i, a["ada_w_2"][1:2], i * ADA))
            sp.wait_ge(S("gemm_done"), st_lat.free[0])
            sp.dma_start(slot(HALF, KB, MLA_COLS), kview(a["mla_w_in_2"][0])).then_inc(S(f"landed{HALF}"), 16)
            wq, wkv = kview(a["mla_w_q_up_2"][0]), kview(a["mla_w_kv_up_2"][0])

            def head3_src(i, j):
                if j % 2 == 0:
                    n = NOPE + ROPE
                    return slot(st_h3.slots[j], QB, n), wq[:, :, bass.ds(i * 2 * n + j // 2 * n, n)]
                n = 2 * NOPE
                return slot(st_h3.slots[j], KVB, n), wkv[:, :, bass.ds(i * 2 * n + j // 2 * n, n)]

            stream(st_h3, head3_src, used=lambda j: j | 1)
            wo3 = kview(a["mla_w_out_2"][0])
            stream(st_o3, lambda i, j: (slot(st_o3.slots[j]), wo3[:, :, bass.ds(i * 4 * P + j * P, P)]))
            ffn_stream(st_f3, st_d3, 1)
            for n in range(NT):
                sp.wait_ge(S("y_copied"), (n + 1) * KB // 4)
                sp.dma_start(out[0, n * P:(n + 1) * P, :], xtok[:, n, :]).then_inc(S("stored"), 16)
            sp.wait_ge(S("stored"), 16 * NT)

        @block.gpsimd
        def _(pool):
            pool.memset(ident[:, :], 1.0).then_inc(S("const"), 1)
            pool.memset(ones[:, :], 1.0).then_inc(S("ones"), 1)
            pool.memset(halves[:, :, :], 0.0).then_inc(S("const"), 1)
            pool.memset(causal_q[:, :], 1.0).then_inc(S("causal_q"), 1)
            pool.wait_ge(S("causal_q"), 1)
            pool.affine_select(out=causal_q[:, :], in_=causal_q[:, :], compare_op=ALU.is_ge, fill=0.0, base=0,
                               pattern=[[-1, P]], channel_multiplier=1).then_inc(S("masks"), 1)
            pool.memset(chunk_ones[:, :], 1.0).then_inc(S("const"), 1)
            pool.memset(chunk_rows[:, :, :], 1.0).then_inc(S("const"), 1)
            pool.memset(qkv_pad[:, :, 0:PAD], 0.0).then_inc(S("padded"), 1)
            pool.memset(scx_pad[:, 0:TAPS2 - 1], 0.0).then_inc(S("padded"), 1)
            pool.memset(wz, 0.0).then_inc(S("padded"), 1)
            for f in range(ROPE // 2):
                pool.memset(inv_freq[:, f:f + 1], float(np.float32(10000.0 ** (-2.0 * f / ROPE)))).then_inc(S("masks"), 1)
            pool.wait_ge(S("const"), 4)
            n = 4
            pool.affine_select(out=ident[:, :], in_=ident[:, :], compare_op=ALU.is_equal, fill=0.0, base=0,
                               pattern=[[-1, P]], channel_multiplier=1).then_inc(S("ident"), 1)
            for l in range(LEVELS):
                b = 1 << l
                v = halves[:, l, :].rearrange("p (n h b) -> p n h b", h=2, b=b)[:, :, 1, :]
                pool.memset(v, 1.0).then_inc(S("const"), 1)
                n += 1
                pool.wait_ge(S("const"), n)
                pool.affine_select(out=v, in_=v, compare_op=ALU.is_ge, fill=0.0, base=0,
                                   pattern=[[-2 * b, P // (2 * b)], [0, b]], channel_multiplier=1).then_inc(S("const"), 1)
                n += 1
                pool.wait_ge(S("const"), n)
                pool.affine_select(out=v, in_=v, compare_op=ALU.is_ge, fill=0.0, base=b - 1,
                                   pattern=[[2 * b, P // (2 * b)], [0, b]], channel_multiplier=-1).then_inc(S("const"), 1)
                n += 1
            v = chunk_ones[:, :].rearrange("p (n b) -> p n b", b=CHUNK)
            for v, pat in ((v, CHUNK), (chunk_rows[:, :, :], P)):
                pool.affine_select(out=v, in_=v, compare_op=ALU.is_ge, fill=0.0, base=0,
                                   pattern=[[-CHUNK, 2], [0, pat]], channel_multiplier=1).then_inc(S("const"), 1)
                n += 1
                pool.wait_ge(S("const"), n)
                pool.affine_select(out=v, in_=v, compare_op=ALU.is_ge, fill=0.0, base=CHUNK - 1,
                                   pattern=[[CHUNK, 2], [0, pat]], channel_multiplier=-1).then_inc(S("const"), 1)
                n += 1
            pool.wait_ge(S("const"), n)
            pool.wait_ge(S("ident"), 1)
            pool.tensor_tensor(strict[:, :], halves[:, 0, :], halves[:, 1, :], ALU.add).then_inc(S("const"), 1)
            for l in range(2, LEVELS):
                n += 1
                pool.wait_ge(S("const"), n)
                pool.tensor_tensor(strict[:, :], strict[:, :], halves[:, l, :], ALU.add).then_inc(S("const"), 1)
            n += 1
            pool.wait_ge(S("const"), n)
            pool.tensor_tensor(causal[:, :], strict[:, :], ident[:, :], ALU.add).then_inc(S("masks"), 1)

        @block.tensor
        def _(pe):
            def ada_sum(m):
                acc = acc_early[m % 2] if isinstance(m, int) and m < PRE else acc_early[0]
                pe.wait_ge(S("ada_mac"), KB * m + KB)
                pe.wait_ge(S("mod_ready"), m + 1)
                for b in range(ADA // P):
                    mm = pe.matmul(ADA_BANK[:, b:b + 1], acc[:, b * P:(b + 1) * P], ones[:, 0:1], start=True, stop=True)
                mm.then_inc(S("ada_sum"), 1)

            def norm_sum(n):
                pe.wait_ge(S("norm_free"), n + 1)
                for f in range(KB):
                    pe.wait_ge(S("norm_sq"), KB * n + f + 1)
                    mm = pe.matmul(bank[6][:, 0:T], ones[:, :], sq[:, f, :], start=f == 0, stop=f == KB - 1)
                mm.then_inc(S("norm_sum"), 1)

            def block_product(st, i, j, acc, rhs, nacc, kb=KB, part=None, ready=None):
                w = slot(st.slots[j], kb)
                for k in part if part is not None else range(kb):
                    if k == 0:
                        pe.wait_ge(S(f"landed{st.slots[j]}"), st.landed(i, j))
                        pe.wait_ge(S("evacuated"), st.done(i, j) + 3 - nacc)
                    if ready and j == 0:
                        pe.wait_ge(S(ready[0]), ready[1] + k + 1)
                    mm = pe.matmul(acc[:, 0:T], w[:, k, :], rhs[:, k, :], start=k == 0, stop=k == kb - 1)
                    if k == kb - 1:
                        mm.then_inc(S("gemm_done"), 1)

            def stream(st, rhs, kb=KB, ready=None, step=None):
                with pe.Fori(0, st.n) as i:
                    for j in range(st.per):
                        if step and j == st.per - 1 and st.per > 2:
                            ada_sum(step + i)
                        block_product(st, i, j, bank[j % 2], rhs(j), 2, kb, ready=ready)
                    if step and st.per == 2:
                        ada_sum(step + i)

            pe.wait_ge(S("ident"), 1)
            pe.wait_ge(S("c_landed"), 64)
            pe.matmul(bank[2][:, 0:9 * KB], crows[:, :], ident[0:9 * KB, 0:9 * KB], start=True, stop=True, is_transpose=True).then_inc(S("c_turned"), 1)
            pe.wait_ge(S("x_landed"), 16)
            for g in range(KB // 2):
                if g >= 2:
                    pe.wait_ge(S("x_copied"), g - 1)
                    pe.wait_ge(S("norm_sq"), 2 * (g - 1))
                for q in range(4):
                    f, n = 2 * g + q // 2, q % 2
                    mm = pe.matmul(bank[g % 2][:, q * P:(q + 1) * P], xtok[:, n, f * P:(f + 1) * P], ident[:, :],
                                   start=True, stop=True, is_transpose=True)
                mm.then_inc(S("turned"), 1)
            pe.wait_ge(S("ones"), 1)
            norm_sum(0)
            for m in range(len(early)):
                ada_sum(m)
            pe.wait_ge(S("rows_landed"), 16 * n_table_dmas)
            pe.wait_ge(S("c_ready"), 3)
            for n, r in enumerate(table_rows):
                mm = pe.matmul(bank[2 + n][:, 0:r], vrows[0:r, n, :], ident[0:r, 0:r], start=True, stop=True, is_transpose=True)
            mm.then_inc(S("cols_turned"), 1)

            def gates_low():
                pe.wait_ge(S("pos"), 1)
                pe.matmul(bank[5][:, 0:NT], pos_f[:, :], ident[0:NT, 0:NT], start=True, stop=True, is_transpose=True).then_inc(S("pos_turned"), 1)
                pe.wait_ge(S("h_ready"), KB)
                for n in range(NT):
                    for k in range(KB):
                        mm = pe.matmul(bank[3][:, n * 2 * H1:(n + 1) * 2 * H1], hT[:, k, n * P:(n + 1) * P], wab[:, k, :],
                                       start=k == 0, stop=k == KB - 1)
                mm.then_inc(S("gates_done"), 1)

            def head_sums():
                pe.wait_ge(S("g_ready"), 1)
                pe.wait_ge(S("masks"), ROPE // 2 + 2)
                g = ab_t[:, 4]
                for n in range(NT):
                    pe.matmul(bank[4][:, n * H1:(n + 1) * H1], causal[:, :], g[:, n, :], start=True, stop=True)
                    pe.matmul(bank[4][:, (NT + n) * H1:(NT + n + 1) * H1], chunk_ones[:, :], g[:, n, :], start=True, stop=True)
                    for c in range(2):
                        k = 2 * NT + 2 * n + c
                        mm = pe.matmul(bank[4][:, k * H1:(k + 1) * H1], chunk_rows[:, c, :], g[:, n, :], start=True, stop=True)
                mm.then_inc(S("gates_done"), 1)

            def head1(i, gemm, chain):
                at, step = [0], [0]

                def some(n):
                    for _ in range(n):
                        j, k = divmod(at[0], KB)
                        if gemm:
                            block_product(st_h1, i, j, bank[j % 3], hT, 3, part=[k], ready=None if chain else ("h_ready", 0))
                        elif j < st_pb.per:
                            pe.wait_ge(S("short"), 5 * H1)
                            block_product(st_pb, 0, j, bank[j % 3], ybin, 3, part=[k])
                        at[0] += 1

                def products():
                    some(SPREAD1[step[0]])
                    step[0] += 1

                if not chain:
                    some(3 * KB)
                    gates_low()
                    some(4 * KB)
                    head_sums()
                    some(2 * KB)
                    return
                n = i
                kT, qT = kq[:, 0, :], kq[:, 1, :]
                tok = [slice(t * P, (t + 1) * P) for t in range(NT)]

                products()
                pe.wait_ge(S("qk_sq"), n)
                pe.matmul(bank[3][:, :], ones[:, :], sq2.rearrange("p a b -> p (a b)"), start=True, stop=True).then_inc(S("qk_sum"), 1)
                products()
                pe.wait_ge(S("gmat"), 4 * n)
                pe.matmul(bank[4][:, :], ones[:, :], gmat.rearrange("p a b -> p (a b)"), start=True, stop=True).then_inc(S("gb_done"), 1)
                products()
                pe.wait_ge(S("kq_ready"), 2 * n)
                for t in range(NT):
                    mm = pe.matmul(bank[5][:, t * 2 * P:(t + 1) * 2 * P], kT[:, tok[t]], kq[:, :, tok[t]], start=True, stop=True)
                mm.then_inc(S("kk_done"), 1)
                products()
                for q in range(4):
                    src = (kT, act3[:, 2, :])[q // 2]
                    mm = pe.matmul(bank[6][:, q * P:(q + 1) * P], src[:, tok[q % 2]], ident[:, :], start=True, stop=True, is_transpose=True)
                mm.then_inc(S("kv_turned"), 1)
                products()
                pe.wait_ge(S("levels"), 2 * n)
                for t in range(NT):
                    mm = pe.matmul(bank[3][:, tok[t]], LTm[:, 0, t, :], ident[:, :], start=True, stop=True)
                mm.then_inc(S("x_done"), 1)
                for l in range(1, LEVELS):
                    products()
                    pe.wait_ge(S("inv"), 7 * (n - 1) + l + 1)
                    for t in range(NT):
                        mm = pe.matmul(bank[3][:, tok[t]], LTm[:, l, t, :], inv[:, 0, t, :], start=True, stop=True)
                    mm.then_inc(S("x_done"), 1)
                    products()
                    pe.wait_ge(S("xs"), 5 * (n - 1) + l)
                    for t in range(NT):
                        pe.matmul(bank[4][:, t * P:(t + 1) * P], inv[:, 1, t, :], xs[:, t, :], start=True, stop=True)
                        mm = pe.matmul(bank[4][:, (NT + t) * P:(NT + t + 1) * P], xs[:, t, :], inv[:, 1, t, :], start=True, stop=True)
                    mm.then_inc(S("y_done"), 1)
                products()
                pe.wait_ge(S("inv"), 7 * n)
                pe.wait_ge(S("tok_copied"), 6 * n)
                for t in range(NT):
                    mm = pe.matmul(bank[5][:, tok[t]], kbeg[:, t, :], inv[:, 1, t, :], start=True, stop=True)
                mm.then_inc(S("w_done"), 1)
                for t in range(NT):
                    mm = pe.matmul(bank[3][:, tok[t]], inv[:, 1, t, :], vb[:, t, :], start=t == 0, stop=True, skip_group_check=True)
                mm.then_inc(S("v_done"), 1)
                for c in range(NCH):
                    t, r = c // 2, slice(c % 2 * CHUNK, c % 2 * CHUNK + CHUNK)
                    cols = slice(c * CHUNK, (c + 1) * CHUNK)
                    if c:
                        products()
                        if c == 1:
                            pe.wait_ge(S("wz"), 2 * n)
                        pe.wait_ge(S("state"), 3 * (n - 1) + c)
                        pe.matmul(bank[3][:, tok[t]], wz[:, c, :], state, start=False, stop=True, skip_group_check=True).then_inc(S("v_done"), 1)
                        if c == 1:
                            pe.wait_ge(S("qg"), n)
                        pe.matmul(bank[6][:, cols], state, qg[:, cols], start=c == 1, stop=False, skip_group_check=True)
                    if c < NCH - 1:
                        products()
                        pe.wait_ge(S("vnew"), 4 * (n - 1) + c + 1)
                        pe.matmul(bank[4][:, 0:P], kdec[r, t, :], vnew[r, t, :], start=True, stop=True).then_inc(S("s_done"), 1)
                    if c % 2:
                        pe.wait_ge(S("vnew"), 4 * (n - 1) + c + 1)
                        mm = pe.matmul(bank[6][:, tok[t]], vnew[:, t, :], QKT[:, t, :], start=False, stop=c == NCH - 1, skip_group_check=True)
                mm.then_inc(S("o_done"), 1)
                if gemm:
                    ada_sum(M_HEAD - 1 + i)
                products()
                pe.wait_ge(S("o_sq"), n)
                pe.matmul(bank[5][:, 0:T], ones[:, :], onrm, start=True, stop=True).then_inc(S("o_sum"), 1)

            pe.wait_ge(S("evacuated"), 3)
            head1(0, True, False)
            ada_sum(PRE - 1)
            with pe.Fori(1, H1) as i:
                head1(i, True, True)
            head1(H1, False, True)
            pe.wait_ge(S("evacuated"), st_pa.block0 + 3)
            pe.wait_ge(S("head_out"), H1)
            stream(st_pa, lambda j: oall, step=M_PROJ)
            stream(st_o1, lambda j: hT, ready=("mix_ready", 0), step=M_WO)
            norm_sum(1)
            stream(st_f1, lambda j: hT, ready=("h_ready", KB), step=M_FFN1)
            stream(st_d1, lambda j: big, FB, ready=("ffn_act", 0))
            norm_sum(2)
            norm_sum(3)
            pe.wait_ge(S("h_ready"), 4 * KB)
            pe.wait_ge(S("glr_landed"), 32)
            for k in range(KB):
                mm = pe.matmul(bank[3][0:RANK, 0:T], wglr[:, k, :], hT[:, k, :], start=k == 0, stop=k == KB - 1)
            mm.then_inc(S("gates_done"), 1)
            pe.wait_ge(S("gate_act"), 1)
            for h in range(H2):
                mm = pe.matmul(bank[4 + h // 2][:, h % 2 * T:(h % 2 + 1) * T], wgate[0:RANK, h * DK2:(h + 1) * DK2], glr[0:RANK, :],
                               start=True, stop=True)
            mm.then_inc(S("gates_done"), 1)

            def head2(i, gemm, chain):
                at = [0]

                def products(n):
                    for _ in range(n if gemm else 0):
                        j, k = divmod(at[0], KB)
                        block_product(st_h2, i, j, bank[j % 3], hT, 3, part=[k])
                        at[0] += 1

                if not chain:
                    products(6 * KB)
                    return
                n = i
                tok = [slice(t * P, (t + 1) * P) for t in range(NT)]
                products(G2)
                pe.wait_ge(S("evacuated"), st_h2.done(i - 1, 3) + 3)
                for q in range(4):
                    mm = pe.matmul(bank[3][:, (q % 2 * 2 + q // 2) * P:(q % 2 * 2 + q // 2 + 1) * P], qkv2[:, 2 + q // 2, tok[q % 2]], ident[:, :],
                                   start=True, stop=True, is_transpose=True)
                mm.then_inc(S("v2_turned"), 1)
                products(G2)
                pe.wait_ge(S("scaled2"), 15 * (n - 1) + 2)
                for t in range(NT):
                    mm = pe.matmul(bank[4][:, tok[t]], kd[:, tok[t]], ident[:, :], start=True, stop=True, is_transpose=True)
                mm.then_inc(S("kd_turned"), 1)
                products(G2)
                pe.wait_ge(S("scaled2"), 15 * n)
                pe.wait_ge(S("tok2"), 2 * n)
                for t in range(NT):
                    for l in range(LEVELS):
                        pe.matmul(bank[3 + t][:, l * CHUNK:(l + 1) * CHUNK], kt[:, l, tok[t]], qt[:, l, t, :], start=True, stop=True)
                    mm = pe.matmul(bank[3 + t][:, 2 * T - 1:2 * T], qk2[:, tok[t]], ones[:, 0:1], start=True, stop=True)
                mm.then_inc(S("att_done"), 1)
                for c in range(2):
                    r = slice(c * CHUNK, (c + 1) * CHUNK)
                    if c == 1:
                        pe.wait_ge(S("kv_done"), 3 * (n - 1) + 1)
                    pe.matmul(bank[6][:, c * T:(c + 1) * T], kd_tok[r, 0, :], v_tok[r, 0, :], start=True, stop=True).then_inc(S("kv_done"), 1)
                products(G2)
                pe.wait_ge(S("state2"), 3 * (n - 1) + 2)
                mm = pe.matmul(bank[6][:, 0:T], kd_tok[0:CHUNK, 1, :], v_tok[0:CHUNK, 1, :], start=True, stop=True)
                mm.then_inc(S("kv_done"), 1)
                products(G2)
                pe.wait_ge(S("att"), 8 * n)
                pe.wait_ge(S("state2"), 3 * n)
                for d in range(DV2):
                    for t in range(NT):
                        pe.matmul(bank[5][:, d * T + t * P:d * T + (t + 1) * P], v_tok[:, t, d * P:(d + 1) * P], att[:, t, :],
                                  start=d == 0 and t == 0, stop=False, skip_group_check=True)
                    for c in range(1, NCH):
                        mm = pe.matmul(bank[5][:, d * T + c * CHUNK:d * T + (c + 1) * CHUNK], states[:, c - 1, d * P:(d + 1) * P],
                                       qe[:, c * CHUNK:(c + 1) * CHUNK], start=False, stop=True, skip_group_check=True)
                mm.then_inc(S("o2_done"), 1)
                products(6 * KB - at[0])
                pe.wait_ge(S("o2_sq"), n)
                for d in range(DV2):
                    mm = pe.matmul(bank[4][:, 0:T], ones[:, :], sq_o[:, d, :], start=d == 0, stop=d == DV2 - 1)
                mm.then_inc(S("o2_sum"), 1)

            pe.wait_ge(S("evacuated"), st_h2.block0 + 3)
            head2(0, True, False)
            with pe.Fori(1, H2) as i:
                head2(i, True, True)
            head2(H2, False, True)
            pe.wait_ge(S("head2_out"), H2)
            pe.wait_ge(S("evacuated"), st_o2.block0 + 3)
            stream(st_o2, lambda j: big)

            def ffn(n, st_f, st_d, step=None):
                norm_sum(n)
                stream(st_f, lambda j: hT, ready=("h_ready", n * KB), step=step)
                stream(st_d, lambda j: big, FB, ready=("ffn_act", (n // 2 - 1) * FB))

            ffn(4, st_f2, st_d2, M_FFN2)
            norm_sum(5)
            pe.wait_ge(S("h_ready"), 6 * KB)
            pe.wait_ge(S(f"landed{HALF}"), st_lat.landed(0, 0))
            pe.wait_ge(S("evacuated"), st_lat.block0 + 3)
            wl = slot(HALF, KB, MLA_COLS)
            for t in range(NT):
                for c0, c1_, b in ((0, QR, 2 * t), (QR, MLA_COLS, 2 * t + 1)):
                    for k in range(KB):
                        mm = pe.matmul(bank[b][:, 0:c1_ - c0], hT[:, k, t * P:(t + 1) * P], wl[:, k, c0:c1_], start=k == 0, stop=k == KB - 1)
            mm.then_inc(S("gemm_done"), 1)
            pe.wait_ge(S("lat_scaled"), 2 * NT)
            for t in range(NT):
                for k in range(QB):
                    pe.matmul(bank[4 + t][:, k * P:(k + 1) * P], lat[:, t, k * P:(k + 1) * P], ident[:, :], start=True, stop=True, is_transpose=True)
            for t in range(NT):
                for k in range(KVB):
                    mm = pe.matmul(bank[6][:, (2 * t + k) * P:(2 * t + k + 1) * P], lat[:, t, QR + k * P:QR + (k + 1) * P], ident[:, :],
                                   start=True, stop=True, is_transpose=True)
            mm.then_inc(S("lat_turned"), 1)
            pe.wait_ge(S("k_rot"), 4)
            for t in range(NT):
                mm = pe.matmul(ADA_BANK[:, t * P:(t + 1) * P], k_rot[:, t].rearrange("p e f -> p (e f)"), ident[:, :],
                               start=True, stop=True, is_transpose=True)
            mm.then_inc(S("lat_turned"), 1)
            pe.wait_ge(S("latT"), 2 * QB + 2 * KVB + 1)
            with pe.Fori(0, st_h3.n) as i:
                tok = [slice(t * P, (t + 1) * P) for t in range(NT)]
                wq = [slot(st_h3.slots[2 * e], QB, NOPE + ROPE) for e in range(2)]
                wkv = [slot(st_h3.slots[2 * e + 1], KVB, 2 * NOPE) for e in range(2)]
                for e in range(2):
                    pe.wait_ge(S(f"landed{st_h3.slots[2 * e]}"), st_h3.landed(i, 2 * e))
                    pe.wait_ge(S(f"landed{st_h3.slots[2 * e + 1]}"), st_h3.landed(i, 2 * e + 1))
                    if e == 0:
                        pe.wait_ge(S("free3"), i + 1)
                    for k in range(QB):
                        pe.matmul(bank[e][:, 0:T], wq[e][:, k, 0:NOPE], cqT[:, k, :], start=k == 0, stop=k == QB - 1)
                    for k in range(KVB):
                        mm = pe.matmul(bank[e][:, T:2 * T], wkv[e][:, k, 0:NOPE], ckvT[:, k, :], start=k == 0, stop=k == KVB - 1)
                    mm.then_inc(S("gemm_done"), 1)
                    for t in range(NT):
                        for k in range(KVB):
                            pe.matmul(bank[2 + e][:, tok[t]], ckvT[:, k, tok[t]], wkv[e][:, k, NOPE:2 * NOPE], start=k == 0, stop=k == KVB - 1)
                        for k in range(QB):
                            mm = pe.matmul(bank[2 + e][:, T + t * ROPE:T + (t + 1) * ROPE], cqT[:, k, tok[t]], wq[e][:, k, NOPE:NOPE + ROPE],
                                           start=k == 0, stop=k == QB - 1)
                    mm.then_inc(S("gemm_done"), 1)
                pe.wait_ge(S("q_rot"), 4 * i + 4)
                for t in range(NT):
                    mm = pe.matmul(bank[4][:, tok[t]], q_rot[:, t].rearrange("p e f -> p (e f)"), ident[:, :],
                                   start=True, stop=True, is_transpose=True)
                mm.then_inc(S("qr_turned"), 1)
                for e in range(2):
                    half = slice(e * ROPE, (e + 1) * ROPE)
                    if e == 0:
                        pe.wait_ge(S("qrT"), i + 1)
                    for t in range(NT):
                        cols = slice(t * P, 3 * P if t else P)
                        keys = slice(0, (t + 1) * P)
                        pe.matmul(bank[5 + e][:, cols], qkT[:, e, 0, tok[t]], qkT[:, e, 1, keys], start=True, stop=False)
                        mm = pe.matmul(bank[5 + e][:, cols], qrT[half, tok[t]], krT[half, keys], start=False, stop=True)
                    mm.then_inc(S("score3"), 1)
                for e in range(2):
                    pe.wait_ge(S("p3"), 4 * i + 2 * e + 2)
                    for q in range(3):
                        mm = pe.matmul(bank[e][:, q * P:(q + 1) * P], p3[:, e, q * P:(q + 1) * P], ident[:, :], start=True, stop=True, is_transpose=True)
                    mm.then_inc(S("p3_turned"), 1)
                for e in range(2):
                    pe.wait_ge(S("pT3"), 2 * i + e + 1)
                    pe.matmul(bank[2 + e][:, 0:T], vr[:, e, 0:P], pT3[:, e, 0:T], start=True, stop=False, skip_group_check=True)
                    pe.matmul(bank[2 + e][:, P:T], vr[:, e, P:2 * P], pT3[:, e, T:T + P], start=False, stop=True, skip_group_check=True)\
                      .then_inc(S("o3_done"), 1)
            pe.wait_ge(S("o3"), H3)
            pe.wait_ge(S("evacuated"), st_o3.block0 + 3)
            stream(st_o3, lambda j: big)
            ffn(6, st_f3, st_d3)
            norm_sum(7)
            pe.wait_ge(S("h_scaled"), 8 * KB + 1)
            for n in range(NT):
                for g in range(KB // 4):
                    m = n * (KB // 4) + g
                    if m >= 2:
                        pe.wait_ge(S("y_copied"), m - 1)
                    for q in range(4):
                        f = 4 * g + q
                        mm = pe.matmul(bank[m % 2][:, q * P:(q + 1) * P], hT[:, f, n * P:(n + 1) * P], ident[:, :], start=True, stop=True, is_transpose=True)
                    mm.then_inc(S("turned"), 1)

        @block.scalar
        def _(act):
            def norm(n):
                act.wait_ge(S("norm_sum"), n + 1)
                act.wait_ge(S("h_scaled"), KB * n + 1)
                if n == 0:
                    act.wait_ge(S("eps"), 1)
                act.activation(lnb[:, 0:T], bank[6][:, 0:T], ACT.Ln, bias=eps_col[:, 0:1], scale=1.0 / D).then_inc(S("norm_free"), 1)
                act.wait_ge(S("norm_free"), n + 2)
                act.activation(rstd[:, :], lnb[:, 0:T], ACT.Exp, scale=-0.5).then_inc(S("rstd"), 1)

            def shift(n, dst, col):
                for f in range(KB):
                    act.wait_ge(S("h_scaled"), KB * n + f + 2)
                    act.activation(dst[:, f, :], dst[:, f, :], ACT.Identity, bias=mod[:, col + f:col + f + 1])\
                       .then_inc(S("h_ready"), 1)

            def copy_out(st, i, j, dst, nacc, func=ACT.Copy, scale=1.0, bank_of=None):
                act.wait_ge(S("gemm_done"), st.done(i, j))
                return act.activation(dst, bank[(j % nacc)][:, 0:T], func, scale=scale).then_inc(S("evacuated"), 1)

            act.sem_inc(S("free3"), 1)
            act.sem_inc(S("o_rn"), 1)
            act.sem_inc(S("lat_sq"), 1)
            act.sem_inc(S("evacuated"), 3)
            act.sem_inc(S("norm_free"), 1)
            act.wait_ge(S("c_turned"), 1)
            act.activation(cact[:, :], bank[2][:, 0:2 * KB], ACT.Silu).then_inc(S("c_ready"), 1)
            act.activation(n1_cols[:, :], bank[2][:, 2 * KB:3 * KB], ACT.Copy).then_inc(S("c_ready"), 1)
            act.activation(bias_cols[:, 0:6 * KB], bank[2][:, 3 * KB:9 * KB], ACT.Copy).then_inc(S("c_ready"), 1)
            for g in range(KB // 2):
                act.wait_ge(S("turned"), g + 1)
                xf = xT[:, 2 * g:2 * g + 2, :]
                act.activation(xf.rearrange("p a b -> p (a b)"), bank[g % 2][:, :], ACT.Copy).then_inc(S("x_copied"), 1)
                for f in range(2):
                    act.activation(sq[:, 2 * g + f, :], bank[g % 2][:, f * T:(f + 1) * T], ACT.Square).then_inc(S("norm_sq"), 1)
            norm(0)
            act.wait_ge(S("cols_turned"), 1)
            for n, dst in enumerate((bias_cols[:, 6 * KB:], vec_cols[:, :], conv_cols[:, :])):
                act.activation(dst, bank[2 + n][:, 0:table_rows[n]], ACT.Copy).then_inc(S("cols_ready"), 1)
            act.wait_ge(S("mod_ready"), 3)
            shift(0, hT, 0)

            dests = ([qkv_pad[:, b, PAD:PAD + T] for b in range(3)] + [None, scb, scc, scx_pad[:, TAPS2 - 1:TAPS2 - 1 + T]])

            def part(tile, i):
                return tile[:, i, :] if isinstance(i, int) else tile[:, bass.ds(i, 1), :]

            def copy_out1(i, j):
                first = isinstance(i, int) and i == 0
                if j < 3:
                    if not first:
                        act.wait_ge(S("conv"), 12 * i)
                    dst = dests[j]
                elif j == 3:
                    dst = part(oall, i)
                elif j < 7:
                    if not first:
                        act.wait_ge(S("short"), 5 * i)
                    dst = dests[j]
                else:
                    dst = part(gates, i + (j - 7) * KB)
                copy_out(st_h1, i, j, dst, 3)

            def activate(i):
                if not (isinstance(i, int) and i == 0):
                    act.wait_ge(S("kv_turned"), i)
                    act.wait_ge(S("kq_ready"), 2 * i)
                act.wait_ge(S("evacuated"), st_h1.done(i, 3) + 3)
                act.wait_ge(S("conv"), 12 * i + 12)
                act.activation(act3, conv, ACT.Silu).then_inc(S("silu"), 1)
                act.activation(part(oall, i), part(oall, i), ACT.Silu).then_inc(S("silu"), 1)
                act.wait_ge(S("silu"), 2 * i + 1)
                act.activation(sq2, act3[:, 0:2, :], ACT.Square).then_inc(S("qk_sq"), 1)

            for j in range(3):
                copy_out1(0, j)
            act.activation(head_rows[:, 1, :], head_rows[:, 1, :], ACT.Exp).then_inc(S("ab_act"), 1)
            act.wait_ge(S("ab_copied"), 1)
            act.activation(ab_t[:, 0], ab_in[:, :, 0, :], ACT.Abs).then_inc(S("ab_act"), 1)
            act.wait_ge(S("ab_act"), 2)
            act.activation(ab_t[:, 1], ab_t[:, 0], ACT.Exp, scale=-1.0).then_inc(S("ab_act"), 1)
            act.wait_ge(S("ab_act"), 3)
            act.activation(ab_t[:, 2], ab_t[:, 1], ACT.Ln, bias=1.0).then_inc(S("ab_act"), 1)
            act.wait_ge(S("ab_copied"), 2)
            act.activation(ab_t[:, 3], ab_in[:, :, 1, :], ACT.Exp, scale=-1.0).then_inc(S("ab_act"), 1)
            for j in range(3, 7):
                copy_out1(0, j)
            act.wait_ge(S("hv"), 4)
            hvt = hv.rearrange("p h v -> p v h")
            act.activation(hvt[:, 6:6 + NT, :], hvt[:, 4:4 + NT, :], ACT.Exp).then_inc(S("hv_act"), 1)
            act.activation(hvt[:, 8:8 + NT, :], hvt[:, 8:8 + NT, :], ACT.Exp).then_inc(S("hv_act"), 1)
            act.activation(hvt[:, 10:10 + NCH, :], hvt[:, 10:10 + NCH, :], ACT.Exp).then_inc(S("hv_act"), 1)
            for j in range(7, 9):
                copy_out1(0, j)
            activate(0)
            act.wait_ge(S("angles"), 1)
            act.activation(sin_t[:, :, :], sin_t[:, :, :], ACT.Sin).then_inc(S("rotary"), 1)
            act.activation(cos_t[:, :, :], cos_t[:, :, :], ACT.Sin).then_inc(S("rotary"), 1)

            def head1(i, gemm, chain):
                at = [0]

                def copies(step):
                    while at[0] < 9 and ready_step[at[0]] <= step:
                        j = at[0]
                        if gemm:
                            copy_out1(i, j)
                        elif j < st_pb.per:
                            copy_out(st_pb, 0, j, hT[:, j, :], 3)
                        at[0] += 1

                n = i
                copies(0)
                act.wait_ge(S("qk_sum"), n)
                act.activation(lnb[:, :], bank[3][:, :], ACT.Ln, bias=eps_col[:, 0:1]).then_inc(S("qk_rn"), 1)
                act.wait_ge(S("qk_rn"), 2 * n - 1)
                act.activation(rn2.rearrange("p a b -> p (a b)"), lnb[:, :], ACT.Exp, scale=-0.5).then_inc(S("qk_rn"), 1)
                copies(1)
                act.wait_ge(S("dec_in"), 4 * n)
                act.activation(dec, dec, ACT.Exp).then_inc(S("dec"), 1)
                act.wait_ge(S("o_rn"), 2 * n - 1)
                act.activation(egb, bank[4][:, 0:NT * P], ACT.Exp).then_inc(S("dec"), 1)
                copies(3)
                act.wait_ge(S("kv_turned"), n)
                for dst, src, v in ((kdec, 0, 8), (kbeg, 0, 14), (vb, 2, 2)):
                    for t in range(NT):
                        act.activation(dst[:, t, :], bank[6][:, (src + t) * P:(src + t + 1) * P], ACT.Copy, scale=hcur[:, v + t:v + t + 1])\
                           .then_inc(S("tok_copied"), 1)
                for l in range(1, LEVELS):
                    copies(3 + 2 * l)
                    act.wait_ge(S("x_done"), 6 * (n - 1) + l + 1)
                    act.activation(xs.rearrange("p a b -> p (a b)"), bank[3][:, 0:NT * P], ACT.Copy).then_inc(S("xs"), 1)
                    copies(4 + 2 * l)
                copies(5 + 2 * (LEVELS - 1))
                act.wait_ge(S("w_done"), n)
                wzv = wz.rearrange("p (t c) k -> p t c k", t=NT)
                for c in range(2):
                    act.activation(wzv[:, :, c, c * CHUNK:(c + 1) * CHUNK],
                                   bank[5][:, 0:NT * P].rearrange("p (t c k) -> p t c k", t=NT, c=2)[:, :, c, :], ACT.Copy, scale=-1.0)\
                       .then_inc(S("wz"), 1)
                copies(len(SPREAD1) - 2)
                if gemm:
                    activate(i)
                else:
                    for b in range(2):
                        act.activation(gates[:, b * KB:(b + 1) * KB, :], gates[:, b * KB:(b + 1) * KB, :], ACT.Sigmoid).then_inc(S("gates"), 1)
                act.wait_ge(S("o_done"), n)
                act.activation(onrm, bank[6][:, 0:T], ACT.Square).then_inc(S("o_sq"), 1)
                copies(len(SPREAD1) - 1)
                act.wait_ge(S("o_sum"), n)
                act.activation(o_ln, bank[5][:, 0:T], ACT.Ln, bias=eps_col[:, 0:1], scale=1.0 / P).then_inc(S("o_rn"), 1)
                act.wait_ge(S("o_rn"), 2 * n)
                act.activation(o_rn, o_ln, ACT.Exp, scale=-0.5).then_inc(S("o_rn"), 1)

            act.wait_ge(S("padded"), 3)
            with act.Fori(1, H1) as i:
                head1(i, True, True)
            head1(H1, False, True)

            def out_blocks(st, sem, base, per, gate):
                with act.Fori(0, st.n) as i:
                    for j in range(per):
                        act.wait_ge(S(sem), base + per * i + j + 1)
                        copy_out(st, i, j, evac[:, j, :], 2, scale=mod[:, bass.ds(per * i + gate * KB + j, 1)])

            with act.Fori(0, st_pa.n) as i:
                for j in range(2):
                    act.wait_ge(S("mixed"), 2 * i + j + 1)
                    copy_out(st_pa, i, j, evac[:, j, :], 2)
            out_blocks(st_o1, "o_added", 0, 4, 2)
            norm(1)
            shift(1, hT, 3 * KB)
            with act.Fori(0, st_f1.n) as i:
                for j in range(4):
                    act.wait_ge(S("ffn_free"), 2 * i + j // 2 + 1)
                    copy_out(st_f1, i, j, evac[:, j, :], 2, func=ACT.Silu if j % 2 == 0 else ACT.Copy)
            out_blocks(st_d1, "d_added", 0, 2, 5)
            norm(2)
            shift(2, xT, 6 * KB)
            for f in range(KB):
                act.wait_ge(S("h_ready"), 2 * KB + f + 1)
                act.activation(sq[:, f, :], xT[:, f, :], ACT.Square).then_inc(S("norm_sq"), 1)
            norm(3)
            shift(3, hT, 8 * KB)
            act.wait_ge(S("gates_done"), 3)
            act.activation(glr[0:RANK, :], bank[3][0:RANK, 0:T], ACT.Copy).then_inc(S("gate_act"), 1)
            act.wait_ge(S("gates_done"), 4)
            for h in range(H2):
                act.activation(gb[:, h, :], bank[4 + h // 2][:, h % 2 * T:(h % 2 + 1) * T], ACT.Identity, bias=vec_cols[:, V_BG + h:V_BG + h + 1])\
                   .then_inc(S("gate_act"), 1)
            act.wait_ge(S("gate_act"), 1 + H2)
            act.activation(gl_a, gb, ACT.Abs).then_inc(S("gate_act"), 1)
            act.wait_ge(S("gate_act"), H2 + 2)
            act.activation(gl_a, gl_a, ACT.Exp, scale=-1.0).then_inc(S("gate_act"), 1)
            act.wait_ge(S("gate_act"), H2 + 3)
            act.activation(gl_a, gl_a, ACT.Ln, bias=1.0).then_inc(S("gate_act"), 1)

            def copy_out2(i, j):
                first = isinstance(i, int) and i == 0
                if j < 2:
                    dst = big[:, 2 * i + j, :] if isinstance(i, int) else big[:, bass.ds(2 * i + j, 1), :]
                else:
                    if not first:
                        if j < 4:
                            act.wait_ge(S("v2_turned"), i)
                        else:
                            act.wait_ge(S("scaled2"), 15 * i)
                    dst = qkv2[:, {2: 2, 3: 3, 4: 0, 5: 1}[j], :]
                copy_out(st_h2, i, j, dst, 3, scale=float(DK2) ** -0.5 if j == 4 else 1.0)

            def head2(i, gemm, chain):
                at = [0]

                def copies(step):
                    while gemm and at[0] < 6 and ready_step2[at[0]] <= step:
                        copy_out2(i, at[0])
                        at[0] += 1

                if not chain:
                    copies(99)
                    return
                n = i
                r = big[:, bass.ds(2 * i - 2, 2), :] if not isinstance(i, int) else big[:, 2 * i - 2:2 * i, :]
                act.wait_ge(S("evacuated"), st_h2.done(i - 1, 1) + 3)
                act.activation(r, r, ACT.Silu).then_inc(S("expo_done"), 1)
                act.wait_ge(S("expo"), 14 * n)
                act.activation(expo, expo, ACT.Exp, scale=1.0 / TAU).then_inc(S("expo_done"), 1)
                copies(1)
                act.wait_ge(S("v2_turned"), n)
                act.activation(v_tok.rearrange("p t d -> p (t d)"), bank[3][:, :], ACT.Copy).then_inc(S("tok2"), 1)
                act.wait_ge(S("kd_turned"), n)
                act.activation(kd_tok.rearrange("p t d -> p (t d)"), bank[4][:, 0:NT * P], ACT.Copy).then_inc(S("tok2"), 1)
                copies(5)
                act.wait_ge(S("o2_done"), n)
                act.activation(sq_o.rearrange("p d t -> p (d t)"), bank[5][:, :], ACT.Square).then_inc(S("o2_sq"), 1)
                copies(6)
                act.wait_ge(S("o2_sum"), n)
                act.activation(lnb[:, 0:T], bank[4][:, 0:T], ACT.Ln, bias=eps_col[:, 0:1], scale=1.0 / (DV2 * P)).then_inc(S("o2_rn"), 1)
                act.wait_ge(S("o2_rn"), 2 * n - 1)
                act.activation(lnb[:, T:2 * T], lnb[:, 0:T], ACT.Exp, scale=-0.5).then_inc(S("o2_rn"), 1)

            head2(0, True, False)
            with act.Fori(1, H2) as i:
                head2(i, True, True)
            head2(H2, False, True)

            def ffn(n, st_f, st_d, shift_sec):
                norm(n)
                shift(n, hT, shift_sec * KB)
                base = (n // 2 - 1) * FB
                with act.Fori(0, st_f.n) as i:
                    for j in range(4):
                        act.wait_ge(S("ffn_free"), base + 2 * i + j // 2 + 1)
                        copy_out(st_f, i, j, evac[:, j, :], 2, func=ACT.Silu if j % 2 == 0 else ACT.Copy)
                out_blocks(st_d, "d_added", (n // 2 - 1) * KB, 2, shift_sec + 2)

            out_blocks(st_o2, "o_added", KB, 4, 10)
            ffn(4, st_f2, st_d2, 11)
            norm(5)
            shift(5, hT, 14 * KB)
            act.wait_ge(S("gemm_done"), st_lat.end)
            for t in range(NT):
                for q, (b, n) in enumerate(((2 * t, QR), (2 * t + 1, KVR))):
                    act.wait_ge(S("lat_sq"), 2 * t + q + 1)
                    act.activation(lat_sq[:, 0:n], bank[b][:, 0:n], ACT.Square, accum_out=lat_ss[:, t, q:q + 1]).then_inc(S("lat_sq"), 1)
            act.wait_ge(S("lat_sq"), 2 * NT + 1)
            for q, n in enumerate((QR, KVR)):
                act.activation(lat_ln[:, :, q], lat_ss[:, :, q], ACT.Ln, bias=eps_col[:, 0:1], scale=1.0 / n).then_inc(S("lat_rn"), 1)
            act.wait_ge(S("lat_rn"), 2)
            act.activation(lat_rn, lat_ln, ACT.Exp, scale=-0.5).then_inc(S("lat_rn"), 1)
            act.wait_ge(S("lat_rn"), 3)
            for t in range(NT):
                act.activation(lat[:, t, 0:QR], bank[2 * t][:, 0:QR], ACT.Copy, scale=lat_rn[:, t, 0:1]).then_inc(S("lat_scaled"), 1)
                act.activation(lat[:, t, QR:QR + KVR], bank[2 * t + 1][:, 0:KVR], ACT.Copy, scale=lat_rn[:, t, 1:2]).then_inc(S("lat_scaled"), 1)
            for t in range(NT):
                act.activation(lat[:, t, QR + KVR:MLA_COLS], bank[2 * t + 1][:, KVR:KVR + ROPE], ACT.Copy).then_inc(S("k_raw"), 1)
            act.wait_ge(S("lat_turned"), 1)
            for t in range(NT):
                for k in range(QB):
                    act.activation(cqT[:, k, t * P:(t + 1) * P], bank[4 + t][:, k * P:(k + 1) * P], ACT.Copy, scale=vec_cols[:, V_GQ + k:V_GQ + k + 1])\
                       .then_inc(S("latT"), 1)
                for k in range(KVB):
                    act.activation(ckvT[:, k, t * P:(t + 1) * P], bank[6][:, (2 * t + k) * P:(2 * t + k + 1) * P], ACT.Copy,
                                   scale=vec_cols[:, V_GKV + k:V_GKV + k + 1]).then_inc(S("latT"), 1)
            act.wait_ge(S("lat_turned"), 2)
            act.activation(krT, ADA_BANK[:, 0:T], ACT.Copy).then_inc(S("latT"), 1)
            act.wait_ge(S("k_raw"), NT)
            act.wait_ge(S("lat_scaled"), 2 * NT)
            act.sem_inc(S("evacuated"), 1)
            SCALE3 = float(NOPE + ROPE) ** -0.5
            with act.Fori(0, st_h3.n) as i:
                for e in range(2):
                    act.wait_ge(S("gemm_done"), st_h3.done(i, 2 * e))
                    act.activation(qkT[:, e].rearrange("p a t -> p (a t)"), bank[e][:, :], ACT.Copy).then_inc(S("evacuated"), 1)
                    act.wait_ge(S("gemm_done"), st_h3.done(i, 2 * e + 1))
                    act.activation(vr[:, e, :], bank[2 + e][:, 0:NT * (NOPE + ROPE)], ACT.Copy).then_inc(S("evacuated"), 1)
                act.wait_ge(S("qr_turned"), i + 1)
                act.activation(qrT, bank[4][:, 0:T], ACT.Copy).then_inc(S("qrT"), 1)
                for e in range(2):
                    for t in range(NT):
                        act.wait_ge(S("nm3"), 2 * i + e + 1)
                        cols = slice(t * P, 3 * P if t else P)
                        act.activation(p3[:, e, cols], sc3[:, e, cols], ACT.Exp, bias=nm3[:, e, t:t + 1], scale=SCALE3,
                                       accum_out=sum3[:, e, t:t + 1]).then_inc(S("exp3"), 1)
                for e in range(2):
                    act.wait_ge(S("p3_turned"), 2 * i + e + 1)
                    act.activation(pT3[:, e, :], bank[e][:, 0:3 * P], ACT.Copy).then_inc(S("pT3"), 1)
                for e in range(2):
                    act.wait_ge(S("o3_done"), 2 * i + e + 1)
                    act.activation(big[:, bass.ds(2 * i + e, 1), :], bank[2 + e][:, 0:T], ACT.Copy).then_inc(S("o3"), 1)
                act.wait_ge(S("o3"), 2 * i + 2)
                act.sem_inc(S("free3"), 1)
            out_blocks(st_o3, "o_added", 2 * KB, 4, 16)
            ffn(6, st_f3, st_d3, 17)
            norm(7)
            for m in range(NT * KB // 4):
                act.wait_ge(S("turned"), KB // 2 + m + 1)
                n, g = divmod(m, KB // 4)
                act.activation(xtok[:, n, g * 512:(g + 1) * 512], bank[m % 2][:, :], ACT.Copy).then_inc(S("y_copied"), 1)

        @block.vector
        def _(dve):
            def ada_mac(m, c0, ks=range(KB)):
                pre = isinstance(m, int) and m < PRE
                acc = acc_early[m % 2] if pre else acc_early[0]
                u = m - len(early) + 1
                for k in ks:
                    if pre and m < len(early):
                        dve.wait_ge(S(f"early{m}"), 16)
                        w = early[m][:, k, :]
                    else:
                        if k % 4 == 0:
                            dve.wait_ge(S(f"ada_landed{k // 4}"), 16 * u)
                        w = ada_w[:, k // 4, k % 4, :]
                    if k == 0:
                        if not (pre and m < 2):
                            dve.wait_ge(S("ada_sum"), m - 1 if pre and m < len(early) else m)
                        dve.tensor_scalar(acc, w, cact[:, c0:c0 + 1], None, ALU.mult).then_inc(S("ada_mac"), 1)
                    else:
                        dve.wait_ge(S("ada_mac"), KB * m + k)
                        dve.scalar_tensor_tensor(acc, w, cact[:, c0 + k:c0 + k + 1], acc, ALU.mult, ALU.add).then_inc(S("ada_mac"), 1)
                    if k % 4 == 3 and not (pre and 0 < m < len(early)):
                        dve.wait_ge(S("ada_mac"), KB * m + k + 1)
                        dve.sem_inc(S("ada_used"), 1)

            def ada_bias(m, col):
                dve.wait_ge(S("ada_sum"), m + 1)
                dve.tensor_tensor(mod[:, bass.ds(col, 4)], ADA_BANK[:, 0:4], bias_cols[:, bass.ds(col, 4)], ALU.add).then_inc(S("mod_ready"), 1)

            def norm_scale(n, w_cols, sc_col):
                dve.wait_ge(S("nscale"), n + 1)
                dve.wait_ge(S("h_scaled"), KB * n + 1)
                dve.scalar_tensor_tensor(nscale[:, :], mod[:, sc_col:sc_col + KB], 1.0, w_cols, ALU.add, ALU.mult)\
                   .then_inc(S("nscale"), 1)
                dve.wait_ge(S("nscale"), n + 2)
                dve.wait_ge(S("rstd"), n + 1)

            def norm_apply(n, dst):
                for f in range(KB):
                    dve.scalar_tensor_tensor(dst[:, f, :], xT[:, f, :], nscale[:, f:f + 1], rstd[:, :], ALU.mult, ALU.mult)\
                       .then_inc(S("h_scaled"), 1)

            dve.memset(eps_col[:, :], EPS).then_inc(S("eps"), 1)
            dve.sem_inc(S("mod_ready"), 1)
            dve.sem_inc(S("h_scaled"), 1)
            dve.sem_inc(S("nscale"), 1)
            dve.sem_inc(S("mixed"), 2)
            dve.sem_inc(S("o_added"), 4)
            dve.sem_inc(S("d_added"), 2)
            dve.sem_inc(S("ffn_free"), 2)
            dve.wait_ge(S("c_ready"), 3)
            for m in range(len(early)):
                ada_mac(m, 0)
                if m:
                    ada_bias(m - 1, 4 * (m - 1))
            ada_bias(len(early) - 1, 4 * len(early) - 4)
            dve.wait_ge(S("mod_ready"), 1 + len(early))
            norm_scale(0, n1_cols[:, :], KB)
            norm_apply(0, hT)
            dve.wait_ge(S("rows_landed"), 16 * n_table_dmas)
            dve.tensor_copy(pos_f[:, :], pos_i[:, :]).then_inc(S("pos"), 1)

            def angles():
                dve.wait_ge(S("pos_turned"), 1)
                dve.tensor_copy(pos_c[:, :], bank[5][:, 0:NT]).then_inc(S("pos"), 1)
                dve.wait_ge(S("pos"), 2)
                dve.wait_ge(S("masks"), ROPE // 2 + 2)
                for t in range(NT):
                    dve.tensor_scalar(angle[:, t, :], inv_freq[:, :], pos_c[:, t:t + 1], None, ALU.mult).then_inc(S("angle"), 1)
                n = NT
                dve.wait_ge(S("angle"), n)
                TWO_PI, ROUND, PI = 2 * np.pi, 1.5 * 2.0 ** 23, float(np.float32(3.1415925))
                for dst, src, scalar, op0, in1, op1 in (
                        (turns, angle, 1 / TWO_PI, ALU.mult, ROUND, ALU.add), (turns, turns, ROUND, ALU.subtract, None, None),
                        (sin_t, turns, -6.25, ALU.mult, angle, ALU.add), (sin_t, turns, -17 / 512, ALU.mult, sin_t, ALU.add),
                        (sin_t, turns, -(TWO_PI - 6.25 - 17 / 512), ALU.mult, sin_t, ALU.add), (sin_t, sin_t, PI, ALU.min, -PI, ALU.max),
                        (cos_t, sin_t, TWO_PI / 4, ALU.add, None, None), (turns, cos_t, np.pi, ALU.is_gt, -TWO_PI, ALU.mult),
                        (cos_t, turns, 0.0, ALU.add, cos_t, ALU.add), (cos_t, cos_t, PI, ALU.min, -PI, ALU.max)):
                    if in1 is None:
                        ins = dve.tensor_scalar(dst[:, :, :], src[:, :, :], scalar, None, op0)
                    elif isinstance(in1, float):
                        ins = dve.tensor_scalar(dst[:, :, :], src[:, :, :], scalar, in1, op0, op1)
                    else:
                        ins = dve.scalar_tensor_tensor(dst[:, :, :], src[:, :, :], scalar, in1[:, :, :], op0, op1)
                    ins.then_inc(S("angle"), 1)
                    n += 1
                    dve.wait_ge(S("angle"), n)
                dve.sem_inc(S("angles"), 1)

            dve.wait_ge(S("gates_done"), 1)
            ps = bank[3][:, 0:NT * 2 * H1].rearrange("p (n k h) -> p n k h", n=NT, k=2)
            for n in range(NT):
                dve.tensor_tensor(ab_in[:, n, 0, :], ps[:, n, 0, :], head_rows[:, 0, :], ALU.add).then_inc(S("ab_part"), 1)
            dve.wait_ge(S("ab_part"), NT)
            dve.sem_inc(S("ab_copied"), 1)
            dve.tensor_copy(ab_in[:, :, 1, :], ps[:, :, 1, :]).then_inc(S("ab_copied"), 1)
            dve.wait_ge(S("ab_act"), 4)
            dve.scalar_tensor_tensor(ab_t[:, 0], ab_in[:, :, 0, :], 0.0, ab_t[:, 2], ALU.max, ALU.add).then_inc(S("ab_part"), 1)
            dve.wait_ge(S("ab_part"), NT + 1)
            for n in range(NT):
                dve.scalar_tensor_tensor(ab_t[:, 4, n], ab_t[:, 0, n], -1.0, head_rows[:, 1, :], ALU.mult, ALU.mult).then_inc(S("ab_part"), 1)
            dve.wait_ge(S("ab_part"), 2 * NT + 1)
            dve.sem_inc(S("g_ready"), 1)
            hvt = hv.rearrange("p h v -> p v h")
            dve.tensor_copy(hvt[:, 0:NT, :], ab_t[:, 4]).then_inc(S("hv"), 1)
            dve.wait_ge(S("ab_act"), 5)
            dve.tensor_scalar(ab_t[:, 1], ab_t[:, 3], 1.0, None, ALU.add).then_inc(S("ab_part"), 1)
            dve.wait_ge(S("ab_part"), 2 * NT + 2)
            dve.reciprocal(hvt[:, 2:2 + NT, :], ab_t[:, 1]).then_inc(S("hv"), 1)
            def col(tile, first, i):
                return tile[:, first + i:first + i + 1] if isinstance(i, int) else tile[:, bass.ds(i + first, 1)]

            def part(tile, i):
                return tile[:, i, :] if isinstance(i, int) else tile[:, bass.ds(i, 1), :]

            def short_conv(i):
                n = i
                dve.wait_ge(S("evacuated"), st_h1.done(i, 5) + 3)
                x_in = scx_pad[:, TAPS2 - 1:TAPS2 - 1 + T]
                dve.tensor_tensor(x_in, x_in, scc, ALU.mult).then_inc(S("short"), 1)
                for k in range(TAPS2):
                    dve.wait_ge(S("short"), 5 * n + k + 1)
                    w = col(vec_cols, V_SC + k * KB, i)
                    if k == 0:
                        dve.tensor_scalar(scv, scx_pad[:, 0:T], w, None, ALU.mult).then_inc(S("short"), 1)
                    else:
                        dve.scalar_tensor_tensor(scv, scx_pad[:, k:k + T], w, scv, ALU.mult, ALU.add).then_inc(S("short"), 1)
                dve.wait_ge(S("short"), 5 * n + TAPS2 + 1)
                dve.tensor_tensor(part(ybin, i), scv, scb, ALU.mult).then_inc(S("short"), 1)

            def convolve(i, k):
                if k == 0:
                    dve.wait_ge(S("evacuated"), st_h1.done(i, 2) + 3)
                    if not (isinstance(i, int) and i == 0):
                        dve.wait_ge(S("kq_ready"), 2 * i)
                for b in range(3):
                    w = col(conv_cols, k * 3 * KB + b * KB, i)
                    if k == 0:
                        dve.tensor_scalar(conv[:, b, :], qkv_pad[:, b, 0:T], w, None, ALU.mult).then_inc(S("conv"), 1)
                    else:
                        dve.wait_ge(S("conv"), 12 * i + 3 * k + b - 3 + 1)
                        dve.scalar_tensor_tensor(conv[:, b, :], qkv_pad[:, b, k:k + T], w, conv[:, b, :], ALU.mult, ALU.add)\
                           .then_inc(S("conv"), 1)

            dve.wait_ge(S("padded"), 3)
            for k in range(TAPS1):
                convolve(0, k)
            angles()
            dve.wait_ge(S("gates_done"), 2)
            sums = bank[4][:, 0:8 * H1].rearrange("p (k h) -> p k h", h=H1)
            dve.tensor_copy(hvt[:, 4:4 + NT, :], sums[:, 0:NT, :]).then_inc(S("hv"), 1)
            dve.wait_ge(S("hv"), 3)
            dve.tensor_copy(hvt[:, 10:10 + NCH, :], sums[:, 2 * NT:2 * NT + NCH, :]).then_inc(S("ab_part"), 1)
            dve.wait_ge(S("ab_part"), 2 * NT + 3)
            dve.tensor_tensor(hvt[:, 8:8 + NT, :], sums[:, NT:2 * NT, :], hvt[:, 4:4 + NT, :], ALU.subtract).then_inc(S("hv"), 1)
            dve.wait_ge(S("hv_act"), 3)
            dve.tensor_tensor(hvt[:, 14:14 + NT, :], hvt[:, 6:6 + NT, :], hvt[:, 2:2 + NT, :], ALU.mult).then_inc(S("hv"), 1)
            dve.wait_ge(S("hv"), 5)

            ada_mac(PRE - 1, 0)
            short_conv(0)
            ada_bias(PRE - 1, 4 * PRE - 4)

            def head1(i, gemm, chain):
                n = i
                c = i - 1
                m = M_HEAD - 1 + i
                dve.tensor_copy(hcur, part(hv, c)).then_inc(S("hcur"), 1)
                dve.wait_ge(S("hcur"), n)
                for t in range(NT):
                    dve.tensor_scalar(gmat[:, t, :], causal[:, :], hcur[:, t:t + 1], None, ALU.mult).then_inc(S("gmat"), 1)
                    dve.tensor_scalar(gmat[:, NT + t, :], ident[:, :], hcur[:, 2 + t:3 + t], None, ALU.mult).then_inc(S("gmat"), 1)
                dve.wait_ge(S("gb_done"), n)
                for t in range(NT):
                    dve.tensor_scalar(dec[:, t, :], bank[4][:, t * P:(t + 1) * P], hcur[:, 4 + t:5 + t], 0.0, ALU.subtract, ALU.min)\
                       .then_inc(S("dec_in"), 1)
                for t in range(NT):
                    dve.tensor_tensor(bstrict[:, t, :], bank[4][:, (NT + t) * P:(NT + t + 1) * P], strict[:, :], ALU.mult)\
                       .then_inc(S("dec_in"), 1)
                dve.wait_ge(S("qk_rn"), 2 * n)
                dve.scalar_tensor_tensor(kq[:, 1, :], act3[:, 0, :], float(P) ** -0.5, rn2[:, 0, :], ALU.mult, ALU.mult).then_inc(S("kq_ready"), 1)
                dve.tensor_tensor(kq[:, 0, :], act3[:, 1, :], rn2[:, 1, :], ALU.mult).then_inc(S("kq_ready"), 1)
                dve.wait_ge(S("dec"), 2 * n - 1)
                for t in range(NT):
                    dve.tensor_tensor(qkdec[:, t, :], dec[:, t, :], causal[:, :], ALU.mult).then_inc(S("masked"), 1)
                dve.wait_ge(S("dec_in"), 4 * n)
                dve.tensor_tensor(ldec, dec, bstrict, ALU.mult).then_inc(S("masked"), 1)
                dve.wait_ge(S("masked"), 3 * n)
                dve.wait_ge(S("kk_done"), n)
                kk = bank[5][:, :].rearrange("p (t w c) -> p t w c", t=NT, w=2)
                dve.tensor_tensor(LT, kk[:, :, 0, :], ldec, ALU.mult).then_inc(S("kk_used"), 1)
                dve.tensor_tensor(QKT, kk[:, :, 1, :], qkdec, ALU.mult).then_inc(S("kk_used"), 1)
                dve.wait_ge(S("kk_used"), 2 * n)
                for t in range(NT):
                    dve.tensor_tensor(LTm[:, :, t, :], LT[:, t:t + 1, :].broadcast_to([P, LEVELS, P]), halves[:, :, :], ALU.mult)\
                       .then_inc(S("levels"), 1)
                dve.wait_ge(S("levels"), 2 * n)
                idb = ident[:, :].rearrange("p (a b) -> p a b", a=1).broadcast_to([P, NT, P])
                dve.tensor_tensor(inv[:, 1], idb, LTm[:, 0], ALU.subtract).then_inc(S("inv"), 1)
                dve.wait_ge(S("x_done"), 6 * c + 1)
                dve.scalar_tensor_tensor(inv[:, 0], bank[3][:, 0:NT * P].rearrange("p (t c) -> p t c", t=NT), -1.0, idb, ALU.mult, ALU.add)\
                   .then_inc(S("inv"), 1)
                dve.wait_ge(S("dec"), 2 * n)
                dve.wait_ge(S("kq_ready"), 2 * n)
                dve.tensor_tensor(qg, kq[:, 1, :], egb, ALU.mult).then_inc(S("qg"), 1)
                for l in range(1, LEVELS):
                    dve.wait_ge(S("y_done"), 5 * c + l)
                    dve.wait_ge(S("inv"), 7 * c + l + 1)
                    flat = inv.rearrange("p a t c -> p (a t c)")
                    dve.tensor_tensor(flat, flat, bank[4][:, :], ALU.subtract).then_inc(S("inv"), 1)
                    if gemm and l <= TAPS1:
                        convolve(i, l - 1)
                if gemm:
                    ada_mac(m, 0, [0])
                for ch in range(NCH):
                    t, r = ch // 2, slice(ch % 2 * CHUNK, ch % 2 * CHUNK + CHUNK)
                    dve.wait_ge(S("v_done"), 4 * c + ch + 1)
                    dve.tensor_copy(vnew[r, t, :], bank[3][r, t * P:(t + 1) * P]).then_inc(S("vnew"), 1)
                    if gemm:
                        ada_mac(m, 0, [2 * ch + 1])
                    if ch < NCH - 1:
                        dve.wait_ge(S("s_done"), 3 * c + ch + 1)
                        if ch == 0:
                            dve.tensor_copy(state, bank[4][:, 0:P]).then_inc(S("state"), 1)
                        else:
                            dve.wait_ge(S("state"), 3 * c + ch)
                            dve.scalar_tensor_tensor(state, state, hcur[:, 10 + ch:11 + ch], bank[4][:, 0:P], ALU.mult, ALU.add).then_inc(S("state"), 1)
                        if gemm:
                            ada_mac(m, 0, [2 * ch + 2])
                if gemm:
                    short_conv(i)
                    ada_bias(m, 4 * PRE - 4 + 4 * i)
                dve.wait_ge(S("o_rn"), 2 * n + 1)
                dve.scalar_tensor_tensor(onrm, bank[6][:, 0:T], vec_cols[:, V_GN:V_GN + 1], o_rn, ALU.mult, ALU.mult).then_inc(S("o_norm"), 1)
                dve.wait_ge(S("o_norm"), n)
                dve.wait_ge(S("silu"), 2 * n)
                dve.tensor_tensor(part(oall, c), part(oall, c), onrm, ALU.mult).then_inc(S("head_out"), 1)

            with dve.Fori(1, H1) as i:
                head1(i, True, True)
            head1(H1, False, True)
            dve.wait_ge(S("gates"), 2)
            dve.wait_ge(S("evacuated"), st_pb.end + 3)
            dve.tensor_tensor(hT[:, :, :], hT[:, :, :], gates[:, KB:2 * KB, :], ALU.mult).then_inc(S("gated"), 1)
            dve.wait_ge(S("gated"), 1)
            with dve.Fori(0, st_pa.n) as i:
                ada_mac(M_PROJ + i, 0)
                for j in range(2):
                    dve.wait_ge(S("evacuated"), st_pa.done(i, j) + 3)
                    mix = hT[:, bass.ds(2 * i + j, 1), :]
                    dve.tensor_tensor(evac[:, j, :], evac[:, j, :], gates[:, bass.ds(2 * i + j, 1), :], ALU.mult).then_inc(S("gated"), 1)
                    dve.wait_ge(S("gated"), 2 * i + j + 2)
                    dve.tensor_tensor(mix, mix, evac[:, j, :], ALU.add).then_inc(S("mix_ready"), 1)
                    dve.wait_ge(S("mix_ready"), 2 * i + j + 1)
                    dve.sem_inc(S("mixed"), 1)
                ada_bias(M_PROJ + i, 4 * i + 6 * KB)

            def add_blocks(st, per, sem, first, step=None):
                with dve.Fori(0, st.n) as i:
                    if step:
                        ada_mac(step[0] + i, step[1] * KB)
                    for j in range(per):
                        dve.wait_ge(S("evacuated"), st.done(i, j) + 3)
                        xf = xT[:, bass.ds(per * i + j, 1), :]
                        dve.tensor_tensor(xf, xf, evac[:, j, :], ALU.add).then_inc(S(sem), 1)
                        dve.wait_ge(S(sem), first + per * i + j + 1)
                        dve.tensor_tensor(sq[:, bass.ds(per * i + j, 1), :], xf, xf, ALU.mult).then_inc(S("norm_sq"), 1)
                    if step:
                        ada_bias(step[0] + i, step[2] + i * step[3])

            def ffn_act(st, first, step=None):
                with dve.Fori(0, st.n) as i:
                    if step:
                        ada_mac(step[0] + i, step[1] * KB)
                    for q in range(2):
                        dve.wait_ge(S("evacuated"), st.done(i, 2 * q + 1) + 3)
                        dve.tensor_tensor(big[:, bass.ds(2 * i + q, 1), :], evac[:, 2 * q, :], evac[:, 2 * q + 1, :], ALU.mult).then_inc(S("ffn_act"), 1)
                        dve.wait_ge(S("ffn_act"), first + 2 * i + q + 1)
                        dve.sem_inc(S("ffn_free"), 1)
                    if step:
                        ada_bias(step[0] + i, step[2] + i * step[3])

            add_blocks(st_o1, 4, "o_added", 4, (M_WO, 1, 14 * KB - 4, 6 * KB))
            def norm_cols(n):
                w_col, sc_col = NORMS[n]
                return vec_cols[:, w_col:w_col + KB], sc_col

            norm_scale(1, *norm_cols(1))
            norm_apply(1, hT)
            ffn_act(st_f1, 0, (M_FFN1, 1, 8 * KB, 4))
            add_blocks(st_d1, 2, "d_added", 2)
            norm_scale(2, *norm_cols(2))
            norm_apply(2, xT)
            norm_scale(3, *norm_cols(3))
            norm_apply(3, hT)
            dve.memset(segment, 1.0).then_inc(S("segment"), 1)
            dve.wait_ge(S("segment"), 1)
            dve.memset(segment.rearrange("p (c k) -> p c k", k=CHUNK)[:, :, 0:1], 0.0).then_inc(S("segment"), 1)
            dve.memset(kt, 0.0).then_inc(S("segment"), 1)
            for l in range(LEVELS):
                b = 1 << l
                dve.tensor_copy(halves_c[:, l, :].rearrange("p (n b) -> p n b", b=b), halves[:, l, :].rearrange("p (n h b) -> p n h b", h=2, b=b)[:, :, 1, :])\
                   .then_inc(S("segment"), 1)
            dve.wait_ge(S("gate_act"), H2 + 4)
            dve.scalar_tensor_tensor(gl_m, gb, 0.0, gl_a, ALU.min, ALU.subtract).then_inc(S("gate_log"), 1)
            dve.wait_ge(S("gate_log"), 1)
            dve.wait_ge(S("segment"), 3 + LEVELS)
            dve.tensor_tensor_scan(gb.rearrange("p h t -> p (h t)"), segment, gl_m.rearrange("p h t -> p (h t)"), 0.0, ALU.mult, ALU.add)\
               .then_inc(S("gate_log"), 1)
            dve.wait_ge(S("gate_log"), 2)

            def head2(i):
                n, c = i, i - 1
                cum = expo[:, 7 * T:8 * T]
                dve.tensor_copy(cum, part(gb, c)).then_inc(S("expo"), 1)
                dve.wait_ge(S("expo"), 14 * c + 1)
                for l in range(LEVELS):
                    b = 1 << l
                    v = cum.rearrange("p (n h b) -> p n h b", h=2, b=b)
                    ref = v[:, :, 0, b - 1:b].broadcast_to([P, T // (2 * b), b])
                    e = expo[:, l * T:(l + 1) * T].rearrange("p (h n b) -> p h n b", h=2, b=b)
                    dve.tensor_tensor(e[:, 0], ref, v[:, :, 0, :], ALU.subtract).then_inc(S("expo"), 1)
                    dve.tensor_tensor(e[:, 1], v[:, :, 1, :], ref, ALU.subtract).then_inc(S("expo"), 1)
                v = cum.rearrange("p (n k) -> p n k", k=CHUNK)
                dve.tensor_tensor(expo[:, 6 * T:7 * T].rearrange("p (n k) -> p n k", k=CHUNK), v[:, :, CHUNK - 1:CHUNK].broadcast_to([P, NCH, CHUNK]), v,
                                  ALU.subtract).then_inc(S("expo"), 1)
                dve.wait_ge(S("evacuated"), st_h2.done(c, 5) + 3)
                q, k = qkv2[:, 0, :], qkv2[:, 1, :]
                dve.tensor_tensor(qk2, q, k, ALU.mult).then_inc(S("scaled2"), 1)
                dve.wait_ge(S("expo_done"), 2 * n)
                dve.tensor_tensor(kd, k, expo[:, 6 * T:7 * T], ALU.mult).then_inc(S("scaled2"), 1)
                for l in range(LEVELS):
                    b = 1 << l
                    e = expo[:, l * T:(l + 1) * T].rearrange("p (h n b) -> p h n b", h=2, b=b)
                    kv, qv = (w.rearrange("p (n h b) -> p n h b", h=2, b=b) for w in (k, q))
                    dve.tensor_tensor(kt[:, l, :].rearrange("p (n h b) -> p n h b", h=2, b=b)[:, :, 0, :], kv[:, :, 0, :], e[:, 0], ALU.mult)\
                       .then_inc(S("scaled2"), 1)
                    dve.tensor_tensor(qt[:, l].rearrange("p t k -> p (t k)").rearrange("p (n b) -> p n b", b=b), qv[:, :, 1, :], e[:, 1], ALU.mult)\
                       .then_inc(S("scaled2"), 1)
                dve.tensor_tensor(qe, q, cum, ALU.mult).then_inc(S("scaled2"), 1)
                dve.wait_ge(S("att_done"), n)
                for t in range(NT):
                    dve.tensor_copy(qk_col[:, t:t + 1], bank[3 + t][:, 2 * T - 1:2 * T]).then_inc(S("att_l"), 1)
                    dve.tensor_tensor(att_l[:, t], bank[3 + t][:, 0:LEVELS * CHUNK].rearrange("p (l k) -> p l k", l=LEVELS), halves_c, ALU.mult)\
                       .then_inc(S("att_l"), 1)
                dve.wait_ge(S("att_l"), 4 * n)
                for t in range(NT):
                    dve.tensor_scalar(att[:, t, :], ident[:, :], qk_col[:, t:t + 1], None, ALU.mult).then_inc(S("att"), 1)
                for l in range(LEVELS):
                    b = 1 << l
                    dve.wait_ge(S("att"), 8 * c + l + 2)
                    v = att.rearrange("p t (n h b) -> p t n h b", h=2, b=b)[:, :, :, 1, :]
                    dve.tensor_tensor(v, v, att_l[:, :, l, :].rearrange("p t (n b) -> p t n b", b=b), ALU.add).then_inc(S("att"), 1)
                dve.wait_ge(S("kv_done"), 3 * c + 2)
                dve.tensor_copy(states[:, 0, :], bank[6][:, 0:T]).then_inc(S("state2"), 1)
                for ch in range(1, NCH - 1):
                    dve.wait_ge(S("state2"), 3 * c + ch)
                    if ch == 2:
                        dve.wait_ge(S("kv_done"), 3 * c + 3)
                    last = cum[:, (ch + 1) * CHUNK - 1:(ch + 1) * CHUNK]
                    dve.scalar_tensor_tensor(states[:, ch, :], states[:, ch - 1, :], last, bank[6][:, (ch % 2) * T:(ch % 2 + 1) * T], ALU.mult, ALU.add)\
                       .then_inc(S("state2"), 1)
                dve.wait_ge(S("o2_rn"), 2 * n)
                for d in range(DV2):
                    dve.scalar_tensor_tensor(on2[:, d, :], bank[5][:, d * T:(d + 1) * T], vec_cols[:, V_GG + d:V_GG + d + 1], lnb[:, T:2 * T],
                                             ALU.mult, ALU.mult).then_inc(S("o2_norm"), 1)
                dve.wait_ge(S("o2_norm"), 2 * n)
                dve.wait_ge(S("expo_done"), 2 * n)
                r = big[:, bass.ds(2 * i - 2, 2), :] if not isinstance(i, int) else big[:, 2 * i - 2:2 * i, :]
                dve.tensor_tensor(r, r, on2, ALU.mult).then_inc(S("head2_out"), 1)

            with dve.Fori(1, H2) as i:
                head2(i)
            head2(H2)

            def ffn(n, st_f, st_d, step=None):
                norm_scale(n, *norm_cols(n))
                norm_apply(n, hT)
                ffn_act(st_f, (n // 2 - 1) * FB, step)
                add_blocks(st_d, 2, "d_added", 2 + (n // 2 - 1) * KB)

            add_blocks(st_o2, 4, "o_added", 4 + KB)
            ffn(4, st_f2, st_d2, (M_FFN2, 1, 14 * KB, 4))
            norm_scale(5, *norm_cols(5))
            norm_apply(5, hT)
            for q in (0, 2):
                dve.tensor_scalar(neg3[:, q, :], causal_q[:, :], 1.0, 1e30, ALU.subtract, ALU.mult).then_inc(S("neg3"), 1)
            dve.memset(neg3[:, 1, :], 0.0).then_inc(S("neg3"), 1)

            def rotate(dst, src, tmp, sem, base, name):
                v = src.rearrange("p t (f two) -> p t f two", two=2)
                for q, (part_, table) in enumerate(((0, cos_t), (1, sin_t), (0, sin_t), (1, cos_t))):
                    dve.tensor_tensor(tmp[:, q], v[:, :, :, part_], table[:, :, :], ALU.mult).then_inc(S(name), 1)
                dve.wait_ge(S(name), base + 4)
                dve.tensor_tensor(dst[:, :, 0:ROPE // 2], tmp[:, 0], tmp[:, 1], ALU.subtract).then_inc(S(sem), 1)
                dve.tensor_tensor(dst[:, :, ROPE // 2:ROPE], tmp[:, 2], tmp[:, 3], ALU.add).then_inc(S(sem), 1)

            dve.wait_ge(S("k_raw"), NT)
            dve.wait_ge(S("rotary"), 2)
            for e in range(2):
                rotate(k_rot[:, :, e], lat[:, :, QR + KVR:MLA_COLS], rot_u[:, e], "k_rot", 4 * e, "k_rot_t")
            dve.wait_ge(S("neg3"), 3)
            SCALE3 = float(NOPE + ROPE) ** -0.5
            with dve.Fori(0, st_h3.n) as i:
                for e in range(2):
                    dve.wait_ge(S("evacuated"), st_h3.done(i, 2 * e + 1) + 3)
                    rotate(q_rot[:, :, e], vr[:, e, NT * NOPE:].rearrange("p (t f) -> p t f", t=NT), rot_u[:, e], "q_rot", 8 * i + 4 * e, "q_rot_t")
                for e in range(2):
                    dve.wait_ge(S("score3"), 2 * i + e + 1)
                    dve.tensor_tensor(sc3[:, e, :], bank[5 + e][:, 0:3 * P], neg3.rearrange("p a b -> p (a b)"), ALU.add).then_inc(S("sc3"), 1)
                for e in range(2):
                    dve.wait_ge(S("sc3"), 2 * i + e + 1)
                    for t in range(NT):
                        dve.tensor_reduce(mx3[:, e, t:t + 1], sc3[:, e, (t * P):(3 * P if t else P)], AX_X, ALU.max).then_inc(S("mx3"), 1)
                    dve.wait_ge(S("mx3"), 4 * i + 2 * e + 2)
                    dve.tensor_scalar(nm3[:, e, :], mx3[:, e, :], -SCALE3, None, ALU.mult).then_inc(S("nm3"), 1)
                for e in range(2):
                    dve.wait_ge(S("exp3"), 4 * i + 2 * e + 2)
                    dve.reciprocal(inv3[:, e, :], sum3[:, e, :]).then_inc(S("inv3"), 1)
                    dve.wait_ge(S("inv3"), 2 * i + e + 1)
                    for t in range(NT):
                        cols = slice(t * P, 3 * P if t else P)
                        dve.tensor_scalar(p3[:, e, cols], p3[:, e, cols], inv3[:, e, t:t + 1], None, ALU.mult).then_inc(S("p3"), 1)
            add_blocks(st_o3, 4, "o_added", 4 + 2 * KB)
            ffn(6, st_f3, st_d3)
            dve.wait_ge(S("rstd"), 8)
            for f in range(KB):
                dve.scalar_tensor_tensor(hT[:, f, :], xT[:, f, :], vec_cols[:, V_FIN + f:V_FIN + f + 1], rstd[:, :], ALU.mult, ALU.mult)\
                   .then_inc(S("h_scaled"), 1)


def kernel(**inputs):
    from concourse import bacc
    from concourse.bass_utils import run_bass_kernel_spmd

    nc = bacc.Bacc("TRN2", target_bir_lowering=False, num_devices=1)
    arrays, views = {}, {}
    for name, value in inputs.items():
        value = np.ascontiguousarray(value)
        arrays[f"in_{name}"] = value
        views[name] = nc.dram_tensor(f"in_{name}", value.shape, mybir.dt.from_np(value.dtype), kind="ExternalInput").ap()
    shape = arrays["in_x"].shape
    out = nc.dram_tensor("out", shape, F32, kind="ExternalOutput").ap()
    program(nc, views, out)
    result = run_bass_kernel_spmd(nc, [arrays], core_ids=[0])
    return result.results[0]["out"]
```

```python
from contextlib import ExitStack

import numpy as np

import concourse.bass as bass
from concourse import mybir

F32 = mybir.dt.float32
F32R = mybir.dt.float32r
I32 = mybir.dt.int32
ALU = mybir.AluOpType
ACT = mybir.ActivationFunctionType
AX_X = mybir.AxisListType.X

P = 128
EPS = 1e-6
LOG_EXP = "natural_log_exp_and_others"
CHUNK = 64
LEVELS = 6


class Signals:

    def __init__(self, ctx, nc):
        self.ctx, self.nc, self.made = ctx, nc, {}

    def __call__(self, name):
        if name not in self.made:
            self.made[name] = self.ctx.enter_context(self.nc.semaphore(name))
        return self.made[name]


class Stream:

    slots_filled = {}
    slot_user = {}
    blocks = 0

    def __init__(self, n, per, first, wide=1):
        cls = Stream
        self.n, self.per, self.wide = n, per, wide
        self.slots = [first + j * wide for j in range(per)] if isinstance(first, int) else first
        self.block0 = cls.blocks
        self.fill0, self.free = [], []
        for j, s in enumerate(self.slots):
            spans = range(s, s + wide)
            self.free.append(max(cls.slot_user.get(x, 0) for x in spans))
            self.fill0.append(cls.slots_filled.get(s, 0))
            cls.slots_filled[s] = self.fill0[-1] + n
            for x in spans:
                cls.slot_user[x] = self.block0 + (n - 1) * per + j + 1
        cls.blocks += n * per
        self.end = cls.blocks

    def landed(self, i, j):
        return 16 * self.fill0[j] + 16 * i + 16

    def done(self, i, j):
        return self.block0 + i * self.per + j + 1


class SplitStream:

    SLOTS = 4
    RINGS = 3 * SLOTS
    pieces = 0

    def __init__(self, n, per, slots=SLOTS):
        self.n, self.per, self.slots = n, per, slots
        self.block0, self.piece0 = Stream.blocks, SplitStream.pieces
        Stream.blocks += n * per
        SplitStream.pieces += n * per
        self.end = Stream.blocks
        self.free = [Stream.slot_user.get(s, 0) for s in range(slots)]
        self.fill0 = [Stream.slots_filled.get(s, 0) for s in range(slots)]
        for s in range(slots):
            Stream.slots_filled[s] = self.fill0[s] + n * per // slots
        for s in range(self.RINGS):
            if s % self.SLOTS < slots:
                Stream.slot_user[s] = self.end

    def landed(self, i, j):
        return 16 * (i * (self.per // self.slots) + self.fill0[j % self.slots] + j // self.slots + 1)

    def done(self, i, j):
        return self.block0 + i * self.per + j + 1

    def piece(self, i, j):
        return self.piece0 + i * self.per + j + 1


def program(nc, a, out):
    x, c1, c2, pos = a["x"], a["c"], a["c_2"], a["positions_2"]
    SEQ, D = x.shape[1:]
    KB = D // P
    NT = SEQ // P
    NCH = SEQ // CHUNK
    H1 = a["gdn_a_log"].shape[1]
    W_QKV = a["gdn_conv_w"].shape[2]
    TAPS1, TAPS2 = a["gdn_conv_w"].shape[1], a["sc_conv_w"].shape[1]
    DFF = a["w_ffn_out"].shape[1]
    FB = DFF // P
    Q_OFF, K_OFF, V_OFF, Z_OFF = 0, D, 2 * D, 3 * D
    AB_OFF = 4 * D
    SCB_OFF = AB_OFF + 2 * H1
    SCC_OFF, SCX_OFF, GA_OFF, GB_OFF = (SCB_OFF + n * D for n in (1, 2, 3, 4))
    H2 = 4
    DK2 = a["gla_w_gate_2"].shape[2] // H2
    RANK = a["gla_w_gate_2"].shape[1]
    TAU = 16.0
    R_OFF2 = 2 * H2 * DK2 + D
    H3 = 8
    NOPE, ROPE = 128, 64
    QR, KVR = a["mla_w_q_up_2"].shape[1], a["mla_w_kv_up_2"].shape[1]
    QB, KVB = QR // P, KVR // P
    MLA_COLS = QR + KVR + ROPE
    ADA = 512
    T = SEQ

    ctx = ExitStack()
    with ctx:
        S = Signals(ctx, nc)

        def sb(name, shape, dt=F32):
            return ctx.enter_context(nc.sbuf_tensor(name, shape, dt))

        bank = [ctx.enter_context(nc.psum_tensor(f"bank{n}", [P, 512], F32)) for n in range(8)]
        ADA_BANK = bank[7]

        HALF = 9
        SLOT = KB * P
        with nc.sbuf_tensor("ring", [P, 2 * HALF * SLOT], F32) as ring:
            pass
        w_raw = sb("w_raw", [P, SplitStream.SLOTS, SLOT])
        w_high = sb("w_high", [P, SplitStream.SLOTS, SLOT], F32R)
        w_low = sb("w_low", [P, SplitStream.SLOTS, SLOT], F32R)
        h1_parts = sb("h1_parts", [P, KB, 2, T], F32R)
        H1_SLOTS = range(SplitStream.RINGS, SplitStream.RINGS + 2 * KB * T // SLOT)
        ring_rest = sb("ring_rest", [P, (2 * HALF - SplitStream.RINGS) * SLOT - 2 * KB * T])
        ada_w = sb("ada_w", [P, 2, KB // 2, ADA])
        ada_acc = sb("ada_acc", [P, ADA])
        xT = sb("xT", [P, KB, T])
        hT = sb("hT", [P, KB, T])
        with nc.sbuf_tensor("big", [P, 4 * KB, T], F32) as big:
            pass
        h_parts = sb("h_parts", [P, KB, 2, T], F32R)
        big_rest = sb("big_rest", [P, 2 * KB, T])
        rstd = sb("rstd", [P, T])
        lnb = sb("lnb", [P, 2 * T])
        ident = sb("ident", [P, P])
        ones = sb("ones", [P, P])
        halves = sb("halves", [P, LEVELS, P])
        causal = sb("causal", [P, P])
        strict = sb("strict", [P, P])
        chunk_ones = sb("chunk_ones", [P, P])
        chunk_rows = sb("chunk_rows", [P, 2, P])
        vrows = sb("vrows", [P, 3, P])
        bias_cols = sb("bias_cols", [P, 160])
        vec_cols = sb("vec_cols", [P, 92])
        n1_cols = sb("n1_cols", [P, KB])
        conv_cols = sb("conv_cols", [P, TAPS1 * W_QKV // P])
        mod = sb("mod", [P, 160])
        nscale = sb("nscale", [P, KB])
        cact = sb("cact", [P, 2 * KB])
        evac = sb("evac", [P, 4, T])
        wab = sb("wab", [P, KB, 2 * H1])
        head_rows = sb("head_rows", [P, 2, H1])

        xtok = big[:, 0:KB, :].rearrange("p b t -> p (b t)").rearrange("p (n d) -> p n d", n=NT)
        sq = big[:, 3 * KB:4 * KB, :]

        def rows(ap, n):
            return ap.rearrange("(r p) -> r p", p=P) if len(ap.shape) == 1 else ap.rearrange("a (r p) -> (a r) p", p=P)

        V_N2, V_NF, V_MIX, V_FFN2, V_FIN = 0, 8, 16, 32, 48
        V_SC, V_GN, V_GG, V_GQ, V_GKV, V_BG, V_END = 56, 80, 81, 83, 86, 88, 92
        tables = [
            [(0, rows(a["b_ada_f"], 16)), (16, rows(a["ada_b_2"], 96))],
            [(V_N2, rows(a["norm2_w"], 8)), (V_NF, rows(a["normf_w"], 8)),
             (V_MIX, rows(a["norm_mix_2"], 16)), (V_FFN2, rows(a["norm_ffn_2"], 16)), (V_FIN, rows(a["final_norm_2"], 8)),
             (V_SC, a["sc_conv_w"][0].rearrange("k (r p) -> (k r) p", p=P)),
             (V_GN, a["gdn_norm_w"]), (V_GG, rows(a["gla_g_out_2"], 2)), (V_GQ, rows(a["mla_g_q_2"], 3)),
             (V_GKV, rows(a["mla_g_kv_2"], 2)), (V_BG, rows(a["gla_b_gate_2"], 4))],
            [(0, a["gdn_conv_w"][0].rearrange("k (r p) -> (k r) p", p=P))],
        ]
        table_rows = [112, V_END, TAPS1 * W_QKV // P]
        n_table_dmas = sum(len(t) for t in tables) + 4
        crows = sb("crows", [72, P])

        SCRATCH = 12034
        with nc.sbuf_tensor("scratch", [P, SCRATCH], F32) as scratch:
            pass
        act_parts = sb("act_parts", [P, FB, 2, T], F32R)
        scratch_rest = sb("scratch_rest", [P, SCRATCH - 2 * FB * T])
        taken = [0]

        def piece(shape):
            n = int(np.prod(shape))
            ap = scratch[:, taken[0]:taken[0] + n]
            taken[0] += n
            assert taken[0] <= SCRATCH, taken[0]
            if len(shape) == 2:
                ap = ap.rearrange("p (a b) -> p a b", a=shape[0])
            elif len(shape) == 3:
                ap = ap.rearrange("p (a b c) -> p a b c", a=shape[0], b=shape[1])
            elif len(shape) == 4:
                ap = ap.rearrange("p (a b c d) -> p a b c d", a=shape[0], b=shape[1], c=shape[2])
            return ap

        PAD = TAPS1 - 1
        NHV = 16
        qkv_pad = piece((3, T + PAD))
        conv = piece((3, T))
        early_at = taken[0]
        act3 = piece((3, T))
        sq2 = piece((2, T))
        rn2 = conv[:, 0:2, :]
        kq = piece((2, T))
        gmat = piece((4, P))
        dec = piece((NT, P))
        egb = piece((NT * P,))
        bstrict = piece((NT, P))
        qkdec = piece((NT, P))
        ldec = piece((NT, P))
        LT = piece((NT, P))
        o_ln, o_rn = egb, ldec.rearrange("p t c -> p (t c)")
        QKT = piece((NT, P))
        assert taken[0] - early_at >= KB * ADA
        LTm = piece((LEVELS, NT, P))
        kdec = piece((NT, P))
        kbeg = piece((NT, P))
        vb = piece((NT, P))
        inv = piece((2, NT, P))
        xs = piece((NT, P))
        wz = piece((NCH, P))
        vnew = piece((NT, P))
        state = piece((P,))
        qg = piece((NT * P,))
        onrm = piece((NT * P,))
        scb = piece((T,))
        scc = piece((T,))
        scx_pad = piece((T + TAPS2 - 1,))
        scv = piece((T,))
        hv = piece((H1, NHV))
        hcur = piece((NHV,))
        ab_in = piece((NT, 2, H1))
        ab_t = piece((5, NT, H1))

        taken[0] = 0
        DV2 = 2
        gb = piece((H2, T))
        expo = piece((8 * T,))
        gl_a, gl_m = (expo[:, n * H2 * T:(n + 1) * H2 * T].rearrange("p (h t) -> p h t", h=H2) for n in range(2))
        qkv2 = piece((4, T))
        kt = piece((LEVELS, T))
        qt = piece((LEVELS, NT, CHUNK))
        halves_c = piece((LEVELS, CHUNK))
        qe = piece((T,))
        kd = piece((T,))
        qk2 = piece((T,))
        kd_tok = piece((NT, P))
        v_tok = piece((NT, DV2 * P))
        qk_col = piece((NT,))
        segment = piece((H2 * T,))
        taken[0] -= H2 * T
        att_l = piece((NT, LEVELS, CHUNK))
        att = piece((NT, P))
        states = piece((NCH - 1, DV2 * P))
        sq_o = piece((DV2, T))
        on2 = piece((DV2, T))
        glr = piece((T,))
        taken[0] = max(taken[0], 2 * FB * T)
        wglr = piece((KB, RANK))
        wgate = piece((H2 * DK2,))

        taken[0] = 0
        lat = piece((NT, QR + KVR + ROPE))
        lat_sq = piece((QR,))
        lat_ss = piece((NT, 2))
        lat_ln = piece((NT, 2))
        lat_rn = piece((NT, 2))
        cqT = piece((QB, T))
        ckvT = piece((KVB, T))
        krT = piece((T,))
        k_rot = piece((NT, 2, ROPE))
        qkT = piece((2, 2, T))
        vr = piece((2, T))
        q_raw = piece((2, NT, ROPE))
        q_rot = piece((NT, 2, ROPE))
        rot_u = piece((2, 4, NT, ROPE // 2))
        qrT = piece((T,))
        neg3 = piece((3, P))
        sc3 = piece((2, 3 * P))
        p3 = piece((2, 3 * P))
        mx3 = piece((2, NT))
        nm3 = piece((2, NT))
        sum3 = piece((2, NT))
        inv3 = piece((2, NT))
        pT3 = piece((2, 3 * P))

        pos_i = sb("pos_i", [NT, P], I32)
        pos_f = sb("pos_f", [NT, P])
        pos_c = sb("pos_c", [P, NT])
        inv_freq = sb("inv_freq", [P, ROPE // 2])
        angle = sb("angle", [P, NT, ROPE // 2])
        turns = sb("turns", [P, NT, ROPE // 2])
        sin_t = sb("sin_t", [P, NT, ROPE // 2])
        cos_t = sb("cos_t", [P, NT, ROPE // 2])

        oall, ybin = big[:, 0:KB, :], big[:, KB:2 * KB, :]
        gates = big[:, 2 * KB:4 * KB, :]

        Stream.slots_filled, Stream.slot_user, Stream.blocks, SplitStream.pieces = {}, {}, 0, 0
        st_h1 = SplitStream(H1, 9, slots=3)
        for at in H1_SLOTS:
            Stream.slot_user[at] = st_h1.end
        st_pb = Stream(1, KB, [3, 7, 11, 0, 1, 2, 4, 5])
        st_pa = Stream(KB // 2, 2, 8)
        st_o1 = Stream(KB // 4, 4, SplitStream.RINGS)
        st_f1, st_d1 = SplitStream(FB // 2, 4), SplitStream(KB // 2, 8)

        st_h2 = SplitStream(H2, 6, slots=3)
        for at in H1_SLOTS:
            Stream.slot_user[at] = st_h2.end
        st_o2 = Stream(1, KB, [3, 7, 11, 16, 17, 0, 1, 2])
        st_f2, st_d2 = SplitStream(FB // 2, 4), SplitStream(KB // 2, 8)
        LAT = SplitStream.RINGS
        st_lat = Stream(1, 1, LAT, wide=6)
        st_h3 = Stream(H3 // 2, 4, 0)
        for e in range(2):
            Stream.slot_user[2 * e] = Stream.slot_user[2 * e + 1]
        st_o3 = Stream(1, KB, SplitStream.SLOTS)
        st_f3, st_d3 = SplitStream(FB // 2, 4), SplitStream(KB // 2, 8)

        IN_PARTS = [range(KB)]
        OUT_PARTS = [range(0, 6), range(6, 12), range(12, 17), range(17, FB)]

        def slot(s, kb=KB, n=P):
            return ring[:, s * SLOT:s * SLOT + kb * n].rearrange("p (k n) -> p k n", k=kb)

        SPREAD1 = [2, 6, 10, 0, 10] + [4, 2] * (LEVELS - 1) + [2] + [2] * 6 + [0]
        SPREAD1[-1] = 9 * KB - sum(SPREAD1)
        assert SPREAD1[-1] >= 0, SPREAD1
        run1 = np.cumsum(SPREAD1)
        ready_step = [int(np.argmax(run1 >= KB * (j + 1))) for j in range(9)]
        w_in = a["w_in"][0]
        head_cols = [Q_OFF, K_OFF, V_OFF, Z_OFF, SCB_OFF, SCC_OFF, SCX_OFF, GA_OFF, GB_OFF]

        G2 = 8
        ready_step2 = [-(-KB * (j + 1) // G2) for j in range(6)]
        head_cols2 = [(R_OFF2, 2), (R_OFF2 + P, 2), (2 * H2 * DK2, 2), (2 * H2 * DK2 + P, 2), (0, 1), (H2 * DK2, 1)]
        NORMS = [(None, KB), (V_N2, 4 * KB), (V_NF, 7 * KB), (V_MIX, 9 * KB), (V_FFN2, 12 * KB), (V_MIX + KB, 15 * KB),
                 (V_FFN2 + KB, 18 * KB)]

        LOW_OF = {0: 0, 1: 1, 3: 2, 4: 3, 6: 4}
        FFN_OF = {1: 0, 4: 1, 6: 2}

        def kview(w):
            return w.rearrange("(k p) n -> p k n", p=P)

        PRE = 5
        def steps(ap):
            return ap.rearrange("p (k n) -> p k n", n=ADA)

        early = [ada_w[:, :].rearrange("p a k n -> p (a k) n")] + \
                [steps(ring[:, H1_SLOTS.start * SLOT:H1_SLOTS.start * SLOT + KB * ADA])] + \
                [steps(scratch[:, early_at:early_at + KB * ADA])] + \
                [steps(big[:, KB:3 * KB, :].rearrange("p b t -> p (b t)"))]
        spare_w = [steps(ring[:, H1_SLOTS.stop * SLOT:H1_SLOTS.stop * SLOT + KB // 2 * ADA]), steps(hT[:, :, :].rearrange("p b t -> p (b t)"))]
        acc_early = [ada_acc[:, :], LTm.rearrange("p a b c -> p (a b c)")[:, 0:ADA]]
        M_HEAD, M_PROJ = PRE, PRE + 2 * (H1 - 1)
        M_WO = M_PROJ + st_pa.n
        M_FFN1 = M_WO + st_o1.n
        M_D1 = M_FFN1 + st_f1.n
        M_END = M_D1 + st_d1.n
        SPARE = len(early) - 1 + H1 - 1

        OUT2 = bank[0:3] + [ADA_BANK]
        OUT3 = bank[0:4]
        eps_col = sb("eps_col", [P, 1])
        causal_q = sb("causal_q", [P, P])
        block = ctx.enter_context(nc.Block())

        @block.sync
        def _(sp):
            def load_ada(m, w, col, u=None, halves=(0, 1)):
                u = m - SPARE if u is None else u
                for h in halves:
                    sp.wait_ge(S("ada_used"), 2 * u + h - 1)
                    rows = w[:, h * D // 2:(h + 1) * D // 2, bass.ds(col, ADA)].rearrange("l (k p) n -> p (l k) n", p=P)
                    sp.dma_start(ada_w[:, h], rows).then_inc(S(f"ada_landed{h}"), 16)

            def load_block(st, i, j, src):
                sp.dma_start(src[0], src[1]).then_inc(S(f"landed{st.slots[j]}"), 16)

            def stream(st, src, extra=None, used=lambda j: j):
                for j in range(st.per):
                    if st.free[j]:
                        sp.wait_ge(S("gemm_done"), st.free[j])
                    load_block(st, 0, j, src(0, j))
                if extra:
                    extra(0)
                with sp.Fori(1, st.n) as i:
                    for j in range(st.per):
                        sp.wait_ge(S("gemm_done"), st.done(i - 1, used(j)))
                        load_block(st, i, j, src(i, j))
                        if extra and j == (st.per - 1) // 2:
                            extra(i)

            def split_stream(st, src, parts, extra=None, follows=False, at=None, between=None):
                def load(i, j):
                    ks, s = parts[j % len(parts)], j % st.slots
                    dst = w_raw[:, s, 0:len(ks) * P].rearrange("p (k n) -> p k n", n=P)
                    sp.dma_start(dst, src(i, j)).then_inc(S(f"landed{s}"), 16)

                at = (1, st.per - 1) if at is None else at
                for j in range(st.per):
                    if j >= st.slots or follows:
                        sp.wait_ge(S("split"), st.piece(0, j) - st.slots)
                    elif st.free[j]:
                        sp.wait_ge(S("gemm_done"), st.free[j])
                    load(0, j)
                    if between and j == st.slots - 1:
                        between()
                if extra:
                    extra(0, (0, 1))
                with sp.Fori(1, st.n) as i:
                    for j in range(st.per):
                        sp.wait_ge(S("split"), st.piece(i, j) - st.slots)
                        load(i, j)
                        if extra and j in at:
                            extra(i, (0, 1) if len(at) == 1 else [at.index(j)])

            def ffn_stream(st_f, st_d, w_in, w_out, extra=None, extra_out=None):
                wf, wd = kview(w_in), kview(w_out)
                split_stream(st_f, lambda i, j: wf[:, :, bass.ds(i * 2 * P + (j // 2) * P + (j % 2) * DFF, P)], IN_PARTS, extra)
                split_stream(st_d, lambda i, j: wd[:, OUT_PARTS[j % 4].start:OUT_PARTS[j % 4].stop, bass.ds(i * 2 * P + j // 4 * P, P)],
                             OUT_PARTS, extra_out, follows=True)

            def load_all(st, w):
                for j in range(st.per):
                    if st.free[j]:
                        sp.wait_ge(S("gemm_done"), st.free[j])
                    load_block(st, 0, j, (slot(st.slots[j]), w[:, :, j * P:(j + 1) * P]))

            sp.dma_start(crows[0:KB, :], rows(c1, KB)).then_inc(S("c_landed"), 16)
            sp.dma_start(crows[KB:2 * KB, :], rows(c2, KB)).then_inc(S("c_landed"), 16)
            sp.dma_start(crows[2 * KB:3 * KB, :], rows(a["norm1_w"], KB)).then_inc(S("c_landed"), 16)
            sp.dma_start(crows[3 * KB:9 * KB, :], rows(a["b_ada"], 6 * KB)).then_inc(S("c_landed"), 16)
            sp.dma_start(xtok, x[0].rearrange("(n p) d -> p n d", p=P)).then_inc(S("x_landed"), 16)
            for m, dst in enumerate(early):
                sp.dma_start(dst, kview(a["w_ada"][0])[:, :, m * ADA:(m + 1) * ADA]).then_inc(S(f"early{m}"), 16)
            def load_tables():
                for n, table in enumerate(tables):
                    for r, src in table:
                        sp.dma_start(vrows[r:r + src.shape[0], n, :], src).then_inc(S("rows_landed"), 16)
                sp.dma_start(wab[:, :, :], kview(w_in)[:, :, AB_OFF:AB_OFF + 2 * H1]).then_inc(S("rows_landed"), 16)
                sp.dma_start(head_rows[:, 0, :], a["gdn_dt_bias"].broadcast_to([P, H1])).then_inc(S("rows_landed"), 16)
                sp.dma_start(head_rows[:, 1, :], a["gdn_a_log"].broadcast_to([P, H1])).then_inc(S("rows_landed"), 16)
                sp.dma_start(pos_i[:, :], pos.rearrange("a (n p) -> (a n) p", p=P)).then_inc(S("rows_landed"), 16)

            wv = kview(w_in)

            def ada1(i, halves):
                if isinstance(i, int):
                    load_ada(PRE - 1, a["w_ada"], (PRE - 1) * ADA, u=1)
                    return
                sp.wait_ge(S("gates_done"), 1)
                sp.wait_ge(S("ada_mac"), KB * (M_HEAD + 2 * i - 4) + KB)
                for h in range(2):
                    w = kview(a["ada_w_2"][1])[:, h * KB // 2:(h + 1) * KB // 2, bass.ds(i * ADA - ADA, ADA)]
                    sp.dma_start(spare_w[h], w).then_inc(S("early1"), 16)
                load_ada(None, a["w_ada"], (PRE - 1) * ADA + i * ADA, u=i + 1)

            split_stream(st_h1, lambda i, j: wv[:, :, bass.ds(i * P + head_cols[j], P)], IN_PARTS, extra=ada1, at=(4,), between=load_tables)
            wa, wb = kview(a["w_gdn_proj"][0]), kview(a["w_sc_out"][0])
            load_all(st_pb, wb)

            def ada2(i):
                load_ada(M_PROJ + i, a["w_ada_f"].rearrange("(l k) n -> l k n", l=1), i * ADA)

            stream(st_pa, lambda i, j: (slot(st_pa.slots[j]), wa[:, :, bass.ds(i * 2 * P + j * P, P)]), extra=ada2)
            wo = kview(a["w_o"][0])

            def ada3(i):
                load_ada(M_WO + i, a["ada_w_2"][bass.ds(i, 1)], 11 * ADA)

            stream(st_o1, lambda i, j: (slot(st_o1.slots[j]), wo[:, :, bass.ds(i * 4 * P + j * P, P)]), extra=ada3)
            ffn_stream(st_f1, st_d1, a["w_ffn_in"][0], a["w_ffn_out"][0], lambda i, h: load_ada(M_FFN1 + i, a["ada_w_2"][0:1], i * ADA, halves=h),
                       lambda i, h: load_ada(M_D1 + i, a["ada_w_2"][1:2], i * ADA + (H1 - 1) * ADA, halves=h))

            wg = kview(a["gla_w_in_2"][0])
            sp.wait_ge(S("head_out"), H1)
            sp.dma_start(wglr, wg[:, :, R_OFF2 + D:R_OFF2 + D + RANK]).then_inc(S("glr_landed"), 16)
            sp.dma_start(wgate[0:RANK, :], a["gla_w_gate_2"][0]).then_inc(S("glr_landed"), 16)
            split_stream(st_h2, lambda i, j: wg[:, :, bass.ds(i * (P * head_cols2[j][1]) + head_cols2[j][0], P)], IN_PARTS, follows=True)
            wo2 = kview(a["gla_w_out_2"][0])
            load_all(st_o2, wo2)

            ffn_stream(st_f2, st_d2, a["ffn_w_in_2"][0], a["ffn_w_out_2"][0])
            sp.wait_ge(S("gemm_done"), st_lat.free[0])
            sp.dma_start(slot(LAT, KB, MLA_COLS), kview(a["mla_w_in_2"][0])).then_inc(S(f"landed{LAT}"), 16)
            wq, wkv = kview(a["mla_w_q_up_2"][0]), kview(a["mla_w_kv_up_2"][0])

            def head3_src(i, j):
                if j % 2 == 0:
                    n = NOPE + ROPE
                    return slot(st_h3.slots[j], QB, n), wq[:, :, bass.ds(i * 2 * n + j // 2 * n, n)]
                n = 2 * NOPE
                return slot(st_h3.slots[j], KVB, n), wkv[:, :, bass.ds(i * 2 * n + j // 2 * n, n)]

            stream(st_h3, head3_src, used=lambda j: j | 1)
            wo3 = kview(a["mla_w_out_2"][0])
            load_all(st_o3, wo3)
            ffn_stream(st_f3, st_d3, a["ffn_w_in_2"][1], a["ffn_w_out_2"][1])
            for n in range(NT):
                sp.wait_ge(S("y_copied"), (n + 1) * KB // 4)
                sp.dma_start(out[0, n * P:(n + 1) * P, :], xtok[:, n, :]).then_inc(S("stored"), 16)
            sp.wait_ge(S("stored"), 16 * NT)

        @block.gpsimd
        def _(pool):
            pool.memset(ident[:, :], 1.0).then_inc(S("const"), 1)
            pool.memset(ones[:, :], 1.0).then_inc(S("ones"), 1)
            pool.memset(halves[:, :, :], 0.0).then_inc(S("const"), 1)
            pool.memset(causal_q[:, :], 1.0).then_inc(S("masks"), 1)
            pool.wait_ge(S("masks"), 1)
            pool.affine_select(out=causal_q[:, :], in_=causal_q[:, :], compare_op=ALU.is_ge, fill=0.0, base=0,
                               pattern=[[-1, P]], channel_multiplier=1).then_inc(S("masks"), 1)
            pool.memset(chunk_ones[:, :], 1.0).then_inc(S("const"), 1)
            pool.memset(chunk_rows[:, :, :], 1.0).then_inc(S("const"), 1)
            pool.memset(qkv_pad[:, :, 0:PAD], 0.0).then_inc(S("padded"), 1)
            pool.memset(scx_pad[:, 0:TAPS2 - 1], 0.0).then_inc(S("padded"), 1)
            pool.memset(wz, 0.0).then_inc(S("padded"), 1)
            for f in range(ROPE // 2):
                pool.memset(inv_freq[:, f:f + 1], float(np.float32(10000.0 ** (-2.0 * f / ROPE)))).then_inc(S("masks"), 1)
            pool.wait_ge(S("const"), 4)
            n = 4
            pool.affine_select(out=ident[:, :], in_=ident[:, :], compare_op=ALU.is_equal, fill=0.0, base=0,
                               pattern=[[-1, P]], channel_multiplier=1).then_inc(S("ident"), 1)
            for l in range(LEVELS):
                b = 1 << l
                v = halves[:, l, :].rearrange("p (n h b) -> p n h b", h=2, b=b)[:, :, 1, :]
                pool.memset(v, 1.0).then_inc(S("const"), 1)
                n += 1
                pool.wait_ge(S("const"), n)
                pool.affine_select(out=v, in_=v, compare_op=ALU.is_ge, fill=0.0, base=0,
                                   pattern=[[-2 * b, P // (2 * b)], [0, b]], channel_multiplier=1).then_inc(S("const"), 1)
                n += 1
                pool.wait_ge(S("const"), n)
                pool.affine_select(out=v, in_=v, compare_op=ALU.is_ge, fill=0.0, base=b - 1,
                                   pattern=[[2 * b, P // (2 * b)], [0, b]], channel_multiplier=-1).then_inc(S("const"), 1)
                n += 1
            v = chunk_ones[:, :].rearrange("p (n b) -> p n b", b=CHUNK)
            for v, pat in ((v, CHUNK), (chunk_rows[:, :, :], P)):
                pool.affine_select(out=v, in_=v, compare_op=ALU.is_ge, fill=0.0, base=0,
                                   pattern=[[-CHUNK, 2], [0, pat]], channel_multiplier=1).then_inc(S("const"), 1)
                n += 1
                pool.wait_ge(S("const"), n)
                pool.affine_select(out=v, in_=v, compare_op=ALU.is_ge, fill=0.0, base=CHUNK - 1,
                                   pattern=[[CHUNK, 2], [0, pat]], channel_multiplier=-1).then_inc(S("const"), 1)
                n += 1
            pool.wait_ge(S("const"), n)
            pool.wait_ge(S("ident"), 1)
            pool.tensor_tensor(strict[:, :], halves[:, 0, :], halves[:, 1, :], ALU.add).then_inc(S("const"), 1)
            for l in range(2, LEVELS):
                n += 1
                pool.wait_ge(S("const"), n)
                pool.tensor_tensor(strict[:, :], strict[:, :], halves[:, l, :], ALU.add).then_inc(S("const"), 1)
            n += 1
            pool.wait_ge(S("const"), n)
            pool.tensor_tensor(causal[:, :], strict[:, :], ident[:, :], ALU.add).then_inc(S("masks"), 1)

            def low(st, i, j, parts):
                n, s = len(parts[j % len(parts)]) * P, j % st.slots
                pool.wait_ge(S("rounded"), st.piece(i, j))
                pool.tensor_tensor(w_low[:, s, 0:n], w_raw[:, s, 0:n], w_high[:, s, 0:n].bitcast(F32), ALU.subtract)\
                    .then_inc(S("split"), 1)

            for st, parts in ((st_h1, IN_PARTS), (st_f1, IN_PARTS), (st_d1, OUT_PARTS), (st_h2, IN_PARTS), (st_f2, IN_PARTS), (st_d2, OUT_PARTS),
                              (st_f3, IN_PARTS), (st_d3, OUT_PARTS)):
                with pool.Fori(0, st.n) as i:
                    for j in range(st.per):
                        low(st, i, j, parts)

        @block.tensor
        def _(pe):
            def ada_sum(m):
                acc = acc_early[m % 2] if isinstance(m, int) and m < PRE else acc_early[0]
                pe.wait_ge(S("ada_mac"), KB * m + KB)
                pe.wait_ge(S("mod_ready"), m + 1)
                for b in range(ADA // P):
                    mm = pe.matmul(ADA_BANK[:, b:b + 1], acc[:, b * P:(b + 1) * P], ones[:, 0:1], start=True, stop=True)
                mm.then_inc(S("ada_sum"), 1)

            def norm_sum(n, fs=range(KB)):
                for f in fs:
                    if f == 0:
                        pe.wait_ge(S("norm_free"), n + 1)
                    pe.wait_ge(S("norm_sq"), KB * n + f + 1)
                    mm = pe.matmul(bank[6][:, 0:T], ones[:, :], sq[:, f, :], start=f == 0, stop=f == KB - 1)
                    if f == KB - 1:
                        mm.then_inc(S("norm_sum"), 1)

            def block_product(st, i, j, acc, rhs, nacc, kb=KB, part=None, ready=None):
                w = slot(st.slots[j], kb)
                for k in part if part is not None else range(kb):
                    if k == 0:
                        pe.wait_ge(S(f"landed{st.slots[j]}"), st.landed(i, j))
                        pe.wait_ge(S("evacuated"), st.done(i, j) + 3 - nacc)
                    if ready and j == 0:
                        pe.wait_ge(S(ready[0]), ready[1] + k + 1)
                    mm = pe.matmul(acc[:, 0:T], w[:, k, :], rhs[:, k, :], start=k == 0, stop=k == kb - 1)
                    if k == kb - 1:
                        mm.then_inc(S("gemm_done"), 1)

            def stream(st, rhs, kb=KB, ready=None, step=None, norm=None):
                def body(i, last=False):
                    for j in range(st.per):
                        if step and j == st.per - 1 and st.per > 2:
                            ada_sum(step + i)
                        if last and j == st.per - 1:
                            norm_sum(norm, range(KB - 2))
                        block_product(st, i, j, bank[j % 2], rhs(j), 2, kb, ready=ready)
                    if step and st.per == 2:
                        ada_sum(step + i)

                with pe.Fori(0, st.n if norm is None else st.n - 1) as i:
                    body(i)
                if norm is not None:
                    body(st.n - 1, last=True)
                    norm_sum(norm, range(KB - 2, KB))

            def split_product(st, i, j, acc, x_parts, ks, kb, ready=None, part=None):
                hi, lo = (w[:, j % st.slots, :].rearrange("p (k n) -> p k n", n=P) for w in (w_high, w_low))
                for n, k in enumerate(ks):
                    if part is not None and k not in part:
                        continue
                    if n == 0:
                        pe.wait_ge(S("split"), st.piece(i, j))
                    if ready:
                        pe.wait_ge(S(ready[0]), ready[1] + k + 1)
                    pe.matmul(acc[:, 0:T], hi[:, n, :], x_parts[:, k, 0, :], start=k == 0, stop=False)
                    pe.matmul(acc[:, 0:T], hi[:, n, :], x_parts[:, k, 1, :], start=False, stop=False)
                    mm = pe.matmul(acc[:, 0:T], lo[:, n, :], x_parts[:, k, 0, :], start=False, stop=k == kb - 1)
                    if n == len(ks) - 1:
                        mm.then_inc(S("gemm_done"), 1)

            def ffn(n, st_f, st_d, step=None, step_out=None):
                m = FFN_OF[n]
                parts_made = LOW_OF[n] * KB
                with pe.Fori(0, st_f.n) as i:
                    for j in range(4):
                        pe.wait_ge(S("evacuated"), st_f.done(i, j) + 3 - 2)
                        split_product(st_f, i, j, bank[j % 2], h_parts, IN_PARTS[0], KB, ready=("h_low", parts_made) if j == 0 else None)
                    if step:
                        ada_sum(step + i)
                pe.wait_ge(S("evacuated"), st_d.block0 + 3 - 1)

                def output(i, last=False):
                    for j in range(8):
                        if j % 4 == 0:
                            if last and j:
                                norm_sum(n + 1, range(KB - 2))
                            pe.wait_ge(S("evacuated"), st_d.done(i, j) + 3 - 5)
                        split_product(st_d, i, j, bank[j // 4], act_parts, OUT_PARTS[j % 4], FB, ready=("act_low", m * FB) if j < 4 else None)
                    if step_out:
                        ada_sum(step_out + i)

                with pe.Fori(0, st_d.n - 1) as i:
                    output(i)
                output(st_d.n - 1, last=True)
                norm_sum(n + 1, range(KB - 2, KB))

            def out_part(st, accs, j, k, rhs):
                if k == 0:
                    pe.wait_ge(S(f"landed{st.slots[j]}"), st.landed(0, j))
                mm = pe.matmul(accs[j // 2][:, j % 2 * T:(j % 2 + 1) * T], slot(st.slots[j])[:, k, :], rhs[:, k, :],
                               start=k == 0 and j % 2 == 0, stop=k == KB - 1, skip_group_check=True)
                if k == KB - 1:
                    mm.then_inc(S("gemm_done"), 1)

            pe.wait_ge(S("ident"), 1)
            pe.wait_ge(S("c_landed"), 64)
            pe.matmul(bank[2][:, 0:9 * KB], crows[:, :], ident[0:9 * KB, 0:9 * KB], start=True, stop=True, is_transpose=True).then_inc(S("c_turned"), 1)
            pe.wait_ge(S("x_landed"), 16)
            for g in range(KB // 2):
                if g >= 2:
                    pe.wait_ge(S("x_copied"), g - 1)
                    pe.wait_ge(S("norm_sq"), 2 * (g - 1))
                for q in range(4):
                    f, n = 2 * g + q // 2, q % 2
                    mm = pe.matmul(bank[g % 2][:, q * P:(q + 1) * P], xtok[:, n, f * P:(f + 1) * P], ident[:, :],
                                   start=True, stop=True, is_transpose=True)
                mm.then_inc(S("turned"), 1)
            pe.wait_ge(S("ones"), 1)
            norm_sum(0)
            for m in range(len(early)):
                ada_sum(m)
            def gates_low():
                pe.wait_ge(S("rows_landed"), 16 * n_table_dmas)
                for n, r in enumerate(table_rows):
                    mm = pe.matmul(bank[4 + n][:, 0:r], vrows[0:r, n, :], ident[0:r, 0:r], start=True, stop=True, is_transpose=True)
                mm.then_inc(S("cols_turned"), 1)
                pe.wait_ge(S("pos"), 1)
                pe.matmul(bank[7][:, 0:NT], pos_f[:, :], ident[0:NT, 0:NT], start=True, stop=True, is_transpose=True).then_inc(S("pos_turned"), 1)
                pe.wait_ge(S("h_shifted"), KB)
                for n in range(NT):
                    for k in range(KB):
                        mm = pe.matmul(bank[3][:, n * 2 * H1:(n + 1) * 2 * H1], hT[:, k, n * P:(n + 1) * P], wab[:, k, :],
                                       start=k == 0, stop=k == KB - 1)
                mm.then_inc(S("gates_done"), 1)

            def head_sums():
                pe.wait_ge(S("ab_part"), 2 * NT + 1)
                pe.wait_ge(S("masks"), ROPE // 2 + 3)
                g = ab_t[:, 4]
                for n in range(NT):
                    pe.matmul(bank[4][:, n * H1:(n + 1) * H1], causal[:, :], g[:, n, :], start=True, stop=True)
                    pe.matmul(bank[4][:, (NT + n) * H1:(NT + n + 1) * H1], chunk_ones[:, :], g[:, n, :], start=True, stop=True)
                    for c in range(2):
                        k = 2 * NT + 2 * n + c
                        mm = pe.matmul(bank[4][:, k * H1:(k + 1) * H1], chunk_rows[:, c, :], g[:, n, :], start=True, stop=True)
                mm.then_inc(S("gates_done"), 1)

            def head1(i, gemm, chain):
                at, step = [0], [0]

                def some(n):
                    for _ in range(n):
                        j, k = divmod(at[0], KB)
                        if gemm:
                            if k == 0:
                                pe.wait_ge(S("evacuated"), st_h1.done(i, j) + 3 - 3)
                            split_product(st_h1, i, j, bank[j % 3], h1_parts, IN_PARTS[0], KB, part=[k],
                                          ready=None if chain or j else ("h_low", 0))
                        elif j < st_pb.per:
                            pe.wait_ge(S("short"), 5 * H1)
                            block_product(st_pb, 0, j, bank[j % 3], ybin, 3, part=[k])
                        at[0] += 1

                def products():
                    some(SPREAD1[step[0]])
                    step[0] += 1

                if not chain:
                    some(3 * KB)
                    gates_low()
                    some(4 * KB)
                    head_sums()
                    some(2 * KB)
                    return
                n = i
                kT, qT = kq[:, 0, :], kq[:, 1, :]
                tok = [slice(t * P, (t + 1) * P) for t in range(NT)]

                products()
                pe.wait_ge(S("qk_sq"), n)
                pe.matmul(bank[3][:, :], ones[:, :], sq2.rearrange("p a b -> p (a b)"), start=True, stop=True).then_inc(S("qk_sum"), 1)
                products()
                pe.wait_ge(S("gmat"), 4 * n)
                pe.matmul(bank[4][:, :], ones[:, :], gmat.rearrange("p a b -> p (a b)"), start=True, stop=True).then_inc(S("gb_done"), 1)
                products()
                pe.wait_ge(S("kq_ready"), 2 * n)
                for t in range(NT):
                    mm = pe.matmul(bank[5][:, t * 2 * P:(t + 1) * 2 * P], kT[:, tok[t]], kq[:, :, tok[t]], start=True, stop=True)
                mm.then_inc(S("kk_done"), 1)
                products()
                for q in range(4):
                    src = (kT, act3[:, 2, :])[q // 2]
                    mm = pe.matmul(bank[6][:, q * P:(q + 1) * P], src[:, tok[q % 2]], ident[:, :], start=True, stop=True, is_transpose=True)
                mm.then_inc(S("kv_turned"), 1)
                products()
                pe.wait_ge(S("levels"), 2 * n)
                for t in range(NT):
                    mm = pe.matmul(bank[3][:, tok[t]], LTm[:, 0, t, :], ident[:, :], start=True, stop=True)
                mm.then_inc(S("x_done"), 1)
                for l in range(1, LEVELS):
                    products()
                    pe.wait_ge(S("inv"), 7 * (n - 1) + l + 1)
                    for t in range(NT):
                        mm = pe.matmul(bank[3][:, tok[t]], LTm[:, l, t, :], inv[:, 0, t, :], start=True, stop=True)
                    mm.then_inc(S("x_done"), 1)
                    products()
                    pe.wait_ge(S("xs"), 5 * (n - 1) + l)
                    for t in range(NT):
                        pe.matmul(bank[4][:, t * P:(t + 1) * P], inv[:, 1, t, :], xs[:, t, :], start=True, stop=True)
                        mm = pe.matmul(bank[4][:, (NT + t) * P:(NT + t + 1) * P], xs[:, t, :], inv[:, 1, t, :], start=True, stop=True)
                    mm.then_inc(S("y_done"), 1)
                products()
                pe.wait_ge(S("inv"), 7 * n)
                pe.wait_ge(S("tok_copied"), 6 * n)
                for t in range(NT):
                    mm = pe.matmul(bank[5][:, tok[t]], kbeg[:, t, :], inv[:, 1, t, :], start=True, stop=True)
                mm.then_inc(S("w_done"), 1)
                for t in range(NT):
                    mm = pe.matmul(bank[3][:, tok[t]], inv[:, 1, t, :], vb[:, t, :], start=t == 0, stop=True, skip_group_check=True)
                mm.then_inc(S("v_done"), 1)
                if gemm:
                    ada_sum(M_HEAD - 2 + 2 * i)
                for c in range(NCH):
                    t, r = c // 2, slice(c % 2 * CHUNK, c % 2 * CHUNK + CHUNK)
                    cols = slice(c * CHUNK, (c + 1) * CHUNK)
                    if c:
                        products()
                        if c == 1:
                            pe.wait_ge(S("wz"), 2 * n)
                        pe.wait_ge(S("state"), 3 * (n - 1) + c)
                        pe.matmul(bank[3][:, tok[t]], wz[:, c, :], state, start=False, stop=True, skip_group_check=True).then_inc(S("v_done"), 1)
                        if c == 1:
                            pe.wait_ge(S("qg"), n)
                        pe.matmul(bank[6][:, cols], state, qg[:, cols], start=c == 1, stop=False, skip_group_check=True)
                    if c < NCH - 1:
                        products()
                        pe.wait_ge(S("vnew"), 4 * (n - 1) + c + 1)
                        pe.matmul(bank[4][:, 0:P], kdec[r, t, :], vnew[r, t, :], start=True, stop=True).then_inc(S("s_done"), 1)
                    if c % 2:
                        pe.wait_ge(S("vnew"), 4 * (n - 1) + c + 1)
                        mm = pe.matmul(bank[6][:, tok[t]], vnew[:, t, :], QKT[:, t, :], start=False, stop=c == NCH - 1, skip_group_check=True)
                mm.then_inc(S("o_done"), 1)
                if gemm:
                    ada_sum(M_HEAD - 1 + 2 * i)
                products()
                pe.wait_ge(S("o_sq"), n)
                pe.matmul(bank[5][:, 0:T], ones[:, :], onrm, start=True, stop=True).then_inc(S("o_sum"), 1)

            pe.wait_ge(S("evacuated"), 3)
            head1(0, True, False)
            ada_sum(PRE - 1)
            with pe.Fori(1, H1) as i:
                head1(i, True, True)
            head1(H1, False, True)
            pe.wait_ge(S("evacuated"), st_pa.block0 + 3)
            pe.wait_ge(S("head_out"), H1)
            stream(st_pa, lambda j: oall, step=M_PROJ)
            stream(st_o1, lambda j: hT, ready=("mix_ready", 0), step=M_WO, norm=1)
            ffn(1, st_f1, st_d1, M_FFN1, M_D1)
            norm_sum(3)

            def low_rank():
                pe.wait_ge(S("h_shifted"), 2 * KB)
                pe.wait_ge(S("glr_landed"), 32)
                for k in range(KB):
                    mm = pe.matmul(bank[3][0:RANK, 0:T], wglr[:, k, :], hT[:, k, :], start=k == 0, stop=k == KB - 1)
                mm.then_inc(S("gates_done"), 1)

            def gate_channels():
                pe.wait_ge(S("gate_act"), 1)
                for h in range(H2):
                    mm = pe.matmul(bank[4 + h // 2][:, h % 2 * T:(h % 2 + 1) * T], wgate[0:RANK, h * DK2:(h + 1) * DK2], glr[0:RANK, :],
                                   start=True, stop=True)
                mm.then_inc(S("gates_done"), 1)

            def head2(i, gemm, chain):
                at = [0]

                def products(n):
                    for _ in range(n):
                        if gemm:
                            j, k = divmod(at[0], KB)
                            if k == 0:
                                pe.wait_ge(S("evacuated"), st_h2.done(i, j) + 3 - 3)
                            split_product(st_h2, i, j, bank[j % 3], h1_parts, IN_PARTS[0], KB, part=[k],
                                          ready=None if chain or j else ("h_low", LOW_OF[3] * KB))
                        else:
                            j, k = divmod(at[0], KB - DV2)
                            if at[0] == 0:
                                pe.wait_ge(S("head2_out"), H2 - 1)
                                pe.wait_ge(S("evacuated"), st_h2.end + 3)
                                pe.wait_ge(S("mod_ready"), M_END + 1)
                            if j < KB:
                                out_part(st_o2, OUT2, j, k, big)
                        at[0] += 1

                if not chain:
                    products(KB)
                    low_rank()
                    products(KB)
                    gate_channels()
                    products(4 * KB)
                    return
                n = i
                tok = [slice(t * P, (t + 1) * P) for t in range(NT)]
                products(G2)
                pe.wait_ge(S("evacuated"), st_h2.done(i - 1, 3) + 3)
                for q in range(4):
                    mm = pe.matmul(bank[3][:, (q % 2 * 2 + q // 2) * P:(q % 2 * 2 + q // 2 + 1) * P], qkv2[:, 2 + q // 2, tok[q % 2]], ident[:, :],
                                   start=True, stop=True, is_transpose=True)
                mm.then_inc(S("v2_turned"), 1)
                products(G2)
                pe.wait_ge(S("scaled2"), 15 * (n - 1) + 2)
                for t in range(NT):
                    mm = pe.matmul(bank[4][:, tok[t]], kd[:, tok[t]], ident[:, :], start=True, stop=True, is_transpose=True)
                mm.then_inc(S("kd_turned"), 1)
                products(G2)
                pe.wait_ge(S("scaled2"), 15 * n)
                pe.wait_ge(S("tok2"), 2 * n)
                for t in range(NT):
                    for l in range(LEVELS):
                        pe.matmul(bank[3 + t][:, l * CHUNK:(l + 1) * CHUNK], kt[:, l, tok[t]], qt[:, l, t, :], start=True, stop=True)
                    mm = pe.matmul(bank[3 + t][:, 2 * T - 1:2 * T], qk2[:, tok[t]], ones[:, 0:1], start=True, stop=True)
                mm.then_inc(S("att_done"), 1)
                for c in range(2):
                    r = slice(c * CHUNK, (c + 1) * CHUNK)
                    if c == 1:
                        pe.wait_ge(S("kv_done"), 3 * (n - 1) + 1)
                    pe.matmul(bank[6][:, c * T:(c + 1) * T], kd_tok[r, 0, :], v_tok[r, 0, :], start=True, stop=True).then_inc(S("kv_done"), 1)
                products(G2)
                pe.wait_ge(S("state2"), 3 * (n - 1) + 2)
                mm = pe.matmul(bank[6][:, 0:T], kd_tok[0:CHUNK, 1, :], v_tok[0:CHUNK, 1, :], start=True, stop=True)
                mm.then_inc(S("kv_done"), 1)
                products(G2)
                pe.wait_ge(S("att"), 8 * n)
                pe.wait_ge(S("state2"), 3 * n)
                for d in range(DV2):
                    for t in range(NT):
                        pe.matmul(bank[5][:, d * T + t * P:d * T + (t + 1) * P], v_tok[:, t, d * P:(d + 1) * P], att[:, t, :],
                                  start=d == 0 and t == 0, stop=False, skip_group_check=True)
                    for c in range(1, NCH):
                        mm = pe.matmul(bank[5][:, d * T + c * CHUNK:d * T + (c + 1) * CHUNK], states[:, c - 1, d * P:(d + 1) * P],
                                       qe[:, c * CHUNK:(c + 1) * CHUNK], start=False, stop=True, skip_group_check=True)
                mm.then_inc(S("o2_done"), 1)
                products(6 * KB - at[0])
                pe.wait_ge(S("o2_sq"), n)
                for d in range(DV2):
                    mm = pe.matmul(bank[4][:, 0:T], ones[:, :], sq_o[:, d, :], start=d == 0, stop=d == DV2 - 1)
                mm.then_inc(S("o2_sum"), 1)

            pe.wait_ge(S("evacuated"), st_h2.block0 + 3)
            head2(0, True, False)
            with pe.Fori(1, H2) as i:
                head2(i, True, True)
            head2(H2, False, True)
            pe.wait_ge(S("head2_out"), H2)
            for j in range(KB):
                if j >= 6:
                    norm_sum(4, range(3 * (j - 6), 3 * (j - 5)))
                for k in range(KB - DV2, KB):
                    out_part(st_o2, OUT2, j, k, big)
            norm_sum(4, range(KB - 2, KB))

            ffn(4, st_f2, st_d2)
            pe.wait_ge(S("h_ready"), 6 * KB)
            pe.wait_ge(S(f"landed{LAT}"), st_lat.landed(0, 0))
            pe.wait_ge(S("evacuated"), st_lat.block0 + 3)
            wl = slot(LAT, KB, MLA_COLS)
            for q, (c0, c1_) in enumerate(((0, QR), (QR, MLA_COLS))):
                for t in range(NT):
                    for k in range(KB):
                        mm = pe.matmul(bank[2 * t + q][:, 0:c1_ - c0], hT[:, k, t * P:(t + 1) * P], wl[:, k, c0:c1_], start=k == 0, stop=k == KB - 1)
                    mm.then_inc(S("gemm_done") if q and t == NT - 1 else S("lat_done"), 1)
            pe.wait_ge(S("lat_scaled"), NT)
            for t in range(NT):
                for k in range(QB):
                    mm = pe.matmul(bank[4 + t][:, k * P:(k + 1) * P], lat[:, t, k * P:(k + 1) * P], ident[:, :], start=True, stop=True, is_transpose=True)
            mm.then_inc(S("lat_turned"), 1)
            pe.wait_ge(S("lat_scaled"), 2 * NT)
            for t in range(NT):
                for k in range(KVB):
                    mm = pe.matmul(bank[6][:, (2 * t + k) * P:(2 * t + k + 1) * P], lat[:, t, QR + k * P:QR + (k + 1) * P], ident[:, :],
                                   start=True, stop=True, is_transpose=True)
            mm.then_inc(S("lat_turned"), 1)
            pe.wait_ge(S("k_rot"), 4)
            for t in range(NT):
                mm = pe.matmul(ADA_BANK[:, t * P:(t + 1) * P], k_rot[:, t].rearrange("p e f -> p (e f)"), ident[:, :],
                               start=True, stop=True, is_transpose=True)
            mm.then_inc(S("lat_turned"), 1)
            pe.wait_ge(S("latT"), NT * (QB + KVB) + 1)
            tok = [slice(t * P, (t + 1) * P) for t in range(NT)]
            copied3 = st_h3.block0 + 3

            def project(i):
                wq = [slot(st_h3.slots[2 * e], QB, NOPE + ROPE) for e in range(2)]
                wkv = [slot(st_h3.slots[2 * e + 1], KVB, 2 * NOPE) for e in range(2)]
                for e in range(2):
                    pe.wait_ge(S(f"landed{st_h3.slots[2 * e]}"), st_h3.landed(i, 2 * e))
                    pe.wait_ge(S(f"landed{st_h3.slots[2 * e + 1]}"), st_h3.landed(i, 2 * e + 1))
                    if e == 0:
                        pe.wait_ge(S("evacuated"), copied3 + 4 * i)
                    for k in range(QB):
                        pe.matmul(bank[e][:, 0:T], wq[e][:, k, 0:NOPE], cqT[:, k, :], start=k == 0, stop=k == QB - 1)
                    for k in range(KVB):
                        mm = pe.matmul(bank[e][:, T:2 * T], wkv[e][:, k, 0:NOPE], ckvT[:, k, :], start=k == 0, stop=k == KVB - 1)
                    mm.then_inc(S("gemm_done"), 1)
                    for t in range(NT):
                        for k in range(KVB):
                            pe.matmul(bank[2 + e][:, tok[t]], ckvT[:, k, tok[t]], wkv[e][:, k, NOPE:2 * NOPE], start=k == 0, stop=k == KVB - 1)
                        for k in range(QB):
                            mm = pe.matmul(bank[2 + e][:, T + t * ROPE:T + (t + 1) * ROPE], cqT[:, k, tok[t]], wq[e][:, k, NOPE:NOPE + ROPE],
                                           start=k == 0, stop=k == QB - 1)
                    mm.then_inc(S("gemm_done"), 1)

            def turn_queries(i):
                pe.wait_ge(S("q_rot"), 4 * i + 4)
                for t in range(NT):
                    mm = pe.matmul(bank[4][:, tok[t]], q_rot[:, t].rearrange("p e f -> p (e f)"), ident[:, :],
                                   start=True, stop=True, is_transpose=True)
                mm.then_inc(S("qr_turned"), 1)

            def scores(i):
                pe.wait_ge(S("qrT"), i + 1)
                for e in range(2):
                    half = slice(e * ROPE, (e + 1) * ROPE)
                    for t in range(NT):
                        cols = slice(t * P, 3 * P if t else P)
                        keys = slice(0, (t + 1) * P)
                        pe.matmul(bank[5 + e][:, cols], qkT[:, e, 0, tok[t]], qkT[:, e, 1, keys], start=True, stop=False)
                        mm = pe.matmul(bank[5 + e][:, cols], qrT[half, tok[t]], krT[half, keys], start=False, stop=True)
                    mm.then_inc(S("score3"), 1)

            def values(i):
                for e in range(2):
                    pe.wait_ge(S("p3"), 4 * i + 2 * e + 2)
                    for q in range(3):
                        mm = pe.matmul(bank[5 + e][:, q * P:(q + 1) * P], p3[:, e, q * P:(q + 1) * P], ident[:, :], start=True, stop=True, is_transpose=True)
                    mm.then_inc(S("p3_turned"), 1)
                for e in range(2):
                    pe.wait_ge(S("pT3"), 2 * i + e + 1)
                    if e == 0:
                        pe.wait_ge(S("evacuated"), copied3 + 4 * i + 4)
                    pe.matmul(ADA_BANK[:, e * T:(e + 1) * T], vr[:, e, 0:P], pT3[:, e, 0:T], start=e == 0, stop=False, skip_group_check=True)
                    mm = pe.matmul(ADA_BANK[:, e * T + P:(e + 1) * T], vr[:, e, P:2 * P], pT3[:, e, T:T + P], start=False, stop=True, skip_group_check=True)
                mm.then_inc(S("o3_done"), 1)

            project(0)
            turn_queries(0)
            with pe.Fori(0, st_h3.n - 1) as i:
                scores(i)
                project(i + 1)
                values(i)
                turn_queries(i + 1)
            last = st_h3.n - 1
            scores(last)
            pe.wait_ge(S("o3"), H3 - 2)
            pe.wait_ge(S("evacuated"), st_o3.block0 + 3)
            for j in range(KB):
                for k in range(H3 - 2):
                    out_part(st_o3, OUT3, j, k, big)
            values(last)
            pe.wait_ge(S("o3"), H3)
            for j in range(KB):
                if j >= 6:
                    norm_sum(6, range(3 * (j - 6), 3 * (j - 5)))
                for k in range(H3 - 2, H3):
                    out_part(st_o3, OUT3, j, k, big)
            norm_sum(6, range(KB - 2, KB))
            ffn(6, st_f3, st_d3)
            pe.wait_ge(S("h_scaled"), 8 * KB + 1)
            for n in range(NT):
                for g in range(KB // 4):
                    m = n * (KB // 4) + g
                    if m >= 2:
                        pe.wait_ge(S("y_copied"), m - 1)
                    for q in range(4):
                        f = 4 * g + q
                        mm = pe.matmul(bank[m % 2][:, q * P:(q + 1) * P], hT[:, f, n * P:(n + 1) * P], ident[:, :], start=True, stop=True, is_transpose=True)
                    mm.then_inc(S("turned"), 1)

        @block.scalar
        def _(act):
            def norm(n):
                act.wait_ge(S("norm_sum"), n + 1)
                act.wait_ge(S("h_scaled"), KB * n + 1)
                if n == 0:
                    act.wait_ge(S("mod_ready"), 1)
                act.activation(lnb[:, 0:T], bank[6][:, 0:T], ACT.Ln, bias=eps_col[:, 0:1], scale=1.0 / D).then_inc(S("norm_free"), 1)
                act.wait_ge(S("norm_free"), n + 2)
                act.activation(rstd[:, :], lnb[:, 0:T], ACT.Exp, scale=-0.5).then_inc(S("rstd"), 1)

            def shift(n, dst, col):
                for f in range(KB):
                    act.wait_ge(S("h_scaled"), KB * n + f + 2)
                    act.activation(dst[:, f, :], dst[:, f, :], ACT.Identity, bias=mod[:, col + f:col + f + 1])\
                       .then_inc(S("h_ready"), 1)

            def copy_out(st, i, j, dst, nacc, func=ACT.Copy, scale=1.0, bank_of=None):
                act.wait_ge(S("gemm_done"), st.done(i, j))
                return act.activation(dst, bank[(j % nacc)][:, 0:T], func, scale=scale).then_inc(S("evacuated"), 1)

            def high(st, i, j, parts):
                m, s = len(parts[j % len(parts)]) * P, j % st.slots
                act.wait_ge(S(f"landed{s}"), st.landed(i, j))
                if st is not st_h1 or not (isinstance(i, int) and i == 0 and j < st.slots):
                    act.wait_ge(S("gemm_done"), st.done(i, j) - st.slots)
                act.activation(w_high[:, s, 0:m], w_raw[:, s, 0:m], ACT.Copy).then_inc(S("rounded"), 1)

            act.sem_inc(S("o_rn"), 1)
            act.sem_inc(S("lat_sq"), 1)
            act.sem_inc(S("evacuated"), 3)
            act.sem_inc(S("norm_free"), 1)
            act.wait_ge(S("c_turned"), 1)
            act.activation(cact[:, :], bank[2][:, 0:2 * KB], ACT.Silu).then_inc(S("c_ready"), 1)
            act.activation(n1_cols[:, :], bank[2][:, 2 * KB:3 * KB], ACT.Copy).then_inc(S("c_ready"), 1)
            act.activation(bias_cols[:, 0:6 * KB], bank[2][:, 3 * KB:9 * KB], ACT.Copy).then_inc(S("c_ready"), 1)
            for g in range(KB // 2):
                act.wait_ge(S("turned"), g + 1)
                xf = xT[:, 2 * g:2 * g + 2, :]
                act.activation(xf.rearrange("p a b -> p (a b)"), bank[g % 2][:, :], ACT.Copy).then_inc(S("x_copied"), 1)
                for f in range(2):
                    act.activation(sq[:, 2 * g + f, :], bank[g % 2][:, f * T:(f + 1) * T], ACT.Square).then_inc(S("norm_sq"), 1)
            act.preload_act_table_set(LOG_EXP)
            norm(0)
            for j in range(3):
                high(st_h1, 0, j, IN_PARTS)
            act.wait_ge(S("mod_ready"), 3)
            for f in range(KB):
                act.wait_ge(S("h_scaled"), f + 2)
                act.activation(h1_parts[:, f, 0, :], hT[:, f, :], ACT.Identity, bias=mod[:, f:f + 1]).then_inc(S("h_ready"), 1)
            for f in range(KB):
                act.wait_ge(S("h_low"), f + 1)
                act.activation(hT[:, f, :], hT[:, f, :], ACT.Identity, bias=mod[:, f:f + 1]).then_inc(S("h_shifted"), 1)

            dests = ([qkv_pad[:, b, PAD:PAD + T] for b in range(3)] + [None, scb, scc, scx_pad[:, TAPS2 - 1:TAPS2 - 1 + T]])

            def part(tile, i):
                return tile[:, i, :] if isinstance(i, int) else tile[:, bass.ds(i, 1), :]

            def copy_out1(i, j, last=False):
                first = isinstance(i, int) and i == 0
                if j < 3:
                    if not first:
                        act.wait_ge(S("conv"), 12 * i)
                    dst = dests[j]
                elif j == 3:
                    dst = part(oall, i)
                elif j < 7:
                    if not first:
                        act.wait_ge(S("short"), 5 * i)
                    dst = dests[j]
                else:
                    dst = part(gates, i + (j - 7) * KB)
                copy_out(st_h1, i, j, dst, 3)
                if j < 6:
                    high(st_h1, i, j + 3, IN_PARTS)
                elif not last:
                    high(st_h1, i + 1, j - 6, IN_PARTS)

            def activate(i):
                act.preload_act_table(ACT.Silu)
                if not (isinstance(i, int) and i == 0):
                    act.wait_ge(S("kv_turned"), i)
                    act.wait_ge(S("kq_ready"), 2 * i)
                act.wait_ge(S("evacuated"), st_h1.done(i, 3) + 3)
                act.wait_ge(S("conv"), 12 * i + 12)
                act.activation(act3, conv, ACT.Silu).then_inc(S("silu"), 1)
                act.activation(part(oall, i), part(oall, i), ACT.Silu).then_inc(S("silu"), 1)
                act.wait_ge(S("silu"), 2 * i + 1)
                act.activation(sq2, act3[:, 0:2, :], ACT.Square).then_inc(S("qk_sq"), 1)

            for j in range(3):
                copy_out1(0, j)
            act.wait_ge(S("cols_turned"), 1)
            for n, dst in enumerate((bias_cols[:, 6 * KB:], vec_cols[:, :], conv_cols[:, :])):
                act.activation(dst, bank[4 + n][:, 0:table_rows[n]], ACT.Copy).then_inc(S("c_ready"), 1)
            act.activation(head_rows[:, 1, :], head_rows[:, 1, :], ACT.Exp).then_inc(S("ab_act"), 1)
            act.wait_ge(S("ab_copied"), 1)
            act.activation(ab_t[:, 0], ab_in[:, :, 0, :], ACT.Abs).then_inc(S("ab_act"), 1)
            act.wait_ge(S("ab_act"), 2)
            act.activation(ab_t[:, 1], ab_t[:, 0], ACT.Exp, scale=-1.0).then_inc(S("ab_act"), 1)
            act.wait_ge(S("ab_act"), 3)
            act.activation(ab_t[:, 2], ab_t[:, 1], ACT.Ln, bias=1.0).then_inc(S("ab_act"), 1)
            act.wait_ge(S("ab_copied"), 2)
            act.activation(ab_t[:, 3], ab_in[:, :, 1, :], ACT.Exp, scale=-1.0).then_inc(S("ab_act"), 1)
            for j in range(3, 7):
                copy_out1(0, j)
            act.wait_ge(S("hv"), 4)
            hvt = hv.rearrange("p h v -> p v h")
            act.activation(hvt[:, 6:6 + NT, :], hvt[:, 4:4 + NT, :], ACT.Exp).then_inc(S("hv_act"), 1)
            act.activation(hvt[:, 8:8 + NT, :], hvt[:, 8:8 + NT, :], ACT.Exp).then_inc(S("hv_act"), 1)
            act.activation(hvt[:, 10:10 + NCH, :], hvt[:, 10:10 + NCH, :], ACT.Exp).then_inc(S("hv_act"), 1)
            for j in range(7, 9):
                copy_out1(0, j)
            activate(0)
            act.wait_ge(S("angle"), NT + 10)
            act.activation(sin_t[:, :, :], sin_t[:, :, :], ACT.Sin).then_inc(S("rotary"), 1)
            act.activation(cos_t[:, :, :], cos_t[:, :, :], ACT.Sin).then_inc(S("rotary"), 1)

            def head1(i, gemm, last=False):
                at = [0]

                def copies(step):
                    while at[0] < 9 and ready_step[at[0]] <= step:
                        j = at[0]
                        if gemm:
                            copy_out1(i, j, last)
                        elif j < st_pb.per:
                            copy_out(st_pb, 0, j, hT[:, j, :], 3)
                        at[0] += 1

                n = i
                copies(0)
                act.wait_ge(S("qk_sum"), n)
                act.activation(lnb[:, :], bank[3][:, :], ACT.Ln, bias=eps_col[:, 0:1]).then_inc(S("qk_rn"), 1)
                act.wait_ge(S("qk_rn"), 2 * n - 1)
                act.activation(rn2.rearrange("p a b -> p (a b)"), lnb[:, :], ACT.Exp, scale=-0.5).then_inc(S("qk_rn"), 1)
                copies(1)
                act.wait_ge(S("dec_in"), 4 * n)
                act.activation(dec, dec, ACT.Exp).then_inc(S("dec"), 1)
                act.wait_ge(S("o_rn"), 2 * n - 1)
                act.activation(egb, bank[4][:, 0:NT * P], ACT.Exp).then_inc(S("dec"), 1)
                copies(3)
                act.wait_ge(S("kv_turned"), n)
                for dst, src, v in ((kdec, 0, 8), (kbeg, 0, 14), (vb, 2, 2)):
                    for t in range(NT):
                        act.activation(dst[:, t, :], bank[6][:, (src + t) * P:(src + t + 1) * P], ACT.Copy, scale=hcur[:, v + t:v + t + 1])\
                           .then_inc(S("tok_copied"), 1)
                for l in range(1, LEVELS):
                    act.wait_ge(S("x_done"), 6 * (n - 1) + l + 1)
                    act.activation(xs.rearrange("p a b -> p (a b)"), bank[3][:, 0:NT * P], ACT.Copy).then_inc(S("xs"), 1)
                    copies(4 + 2 * l)
                copies(5 + 2 * (LEVELS - 1))
                act.wait_ge(S("w_done"), n)
                wzv = wz.rearrange("p (t c) k -> p t c k", t=NT)
                for c in range(2):
                    act.activation(wzv[:, :, c, c * CHUNK:(c + 1) * CHUNK],
                                   bank[5][:, 0:NT * P].rearrange("p (t c k) -> p t c k", t=NT, c=2)[:, :, c, :], ACT.Copy, scale=-1.0)\
                       .then_inc(S("wz"), 1)
                if gemm:
                    activate(i)
                else:
                    for b in range(2):
                        act.activation(gates[:, b * KB:(b + 1) * KB, :], gates[:, b * KB:(b + 1) * KB, :], ACT.Sigmoid).then_inc(S("gates"), 1)
                copies(len(SPREAD1) - 2)
                act.wait_ge(S("o_done"), n)
                act.activation(onrm, bank[6][:, 0:T], ACT.Square).then_inc(S("o_sq"), 1)
                act.preload_act_table_set(LOG_EXP)
                copies(len(SPREAD1) - 1)
                act.wait_ge(S("o_sum"), n)
                act.activation(o_ln, bank[5][:, 0:T], ACT.Ln, bias=eps_col[:, 0:1], scale=1.0 / P).then_inc(S("o_rn"), 1)
                act.wait_ge(S("o_rn"), 2 * n)
                act.activation(o_rn, o_ln, ACT.Exp, scale=-0.5).then_inc(S("o_rn"), 1)

            act.wait_ge(S("padded"), 3)
            act.preload_act_table_set(LOG_EXP)
            with act.Fori(1, H1 - 1) as i:
                head1(i, True)
            head1(H1 - 1, True, last=True)
            head1(H1, False)

            def out_blocks(st, sem, base, per, gate):
                with act.Fori(0, st.n) as i:
                    for j in range(per):
                        act.wait_ge(S(sem), base + per * i + j + 1)
                        copy_out(st, i, j, evac[:, j, :], 2, scale=mod[:, bass.ds(per * i + gate * KB + j, 1)])

            def out_pairs(st, accs, base, gate):
                for j in range(KB):
                    act.wait_ge(S("o_added"), base + j + 1)
                    act.wait_ge(S("gemm_done"), st.done(0, j | 1))
                    act.activation(evac[:, j % 4, :], accs[j // 2][:, j % 2 * T:(j % 2 + 1) * T], ACT.Copy,
                                   scale=mod[:, gate * KB + j:gate * KB + j + 1]).then_inc(S("evacuated"), 1)

            with act.Fori(0, st_pa.n) as i:
                for j in range(2):
                    act.wait_ge(S("mixed"), 2 * i + j + 1)
                    copy_out(st_pa, i, j, evac[:, j, :], 2)
            out_blocks(st_o1, "o_added", 0, 4, 2)
            def ffn(n, st_f, st_d, shift_sec):
                act.wait_ge(S("gemm_done"), st_f.block0)
                high(st_f, 0, 0, IN_PARTS)
                norm(n)
                for f in range(KB):
                    act.wait_ge(S("h_scaled"), KB * n + f + 2)
                    col = shift_sec * KB + f
                    act.activation(h_parts[:, f, 0, :], hT[:, f, :], ACT.Identity, bias=mod[:, col:col + 1]).then_inc(S("h_ready"), 1)
                    if f % 4 == 3:
                        high(st_f, 0, f // 4 + 1, IN_PARTS)
                act.preload_act_table(ACT.Silu)
                first = FFN_OF[n] * FB

                def hidden(i, last=False):
                    for j in range(4):
                        act.wait_ge(S("ffn_free"), first + 2 * i + j // 2 + 1)
                        copy_out(st_f, i, j, evac[:, j, :], 2, func=ACT.Silu if j % 2 == 0 else ACT.Copy)
                        if j < 1:
                            high(st_f, i, j + 3, IN_PARTS)
                        elif not last:
                            high(st_f, i + 1, j - 1, IN_PARTS)
                        else:
                            high(st_d, 0, j - 1, OUT_PARTS)
                        if j % 2:
                            dst = act_parts[:, 2 * i + j // 2, 0, :] if last else act_parts[:, bass.ds(2 * i + j // 2, 1), 0, :]
                            act.wait_ge(S("ffn_act"), first + 2 * i + j // 2 + 1)
                            act.activation(dst, evac[:, j - 1, :], ACT.Copy).then_inc(S("act_high"), 1)

                with act.Fori(0, st_f.n - 1) as i:
                    hidden(i)
                hidden(st_f.n - 1, last=True)

                def output(i, last=False):
                    for j in range(8):
                        if j % 4 == 3:
                            b = j // 4
                            act.wait_ge(S("d_added"), FFN_OF[n] * KB + 2 * i + b + 1)
                            act.wait_ge(S("gemm_done"), st_d.done(i, j))
                            col = (shift_sec + 2) * KB + 2 * i + b
                            scale = mod[:, col:col + 1] if last else mod[:, bass.ds(2 * i + ((shift_sec + 2) * KB + b), 1)]
                            act.activation(evac[:, b, :], bank[b][:, 0:T], ACT.Copy, scale=scale).then_inc(S("evacuated"), 4)
                        if j < 5:
                            high(st_d, i, j + 3, OUT_PARTS)
                        elif not last:
                            high(st_d, i + 1, j - 5, OUT_PARTS)

                act.preload_act_table_set(LOG_EXP)
                with act.Fori(0, st_d.n - 1) as i:
                    output(i)
                output(st_d.n - 1, last=True)

            ffn(1, st_f1, st_d1, 3)
            high(st_h2, 0, 0, IN_PARTS)
            norm(2)
            shift(2, xT, 6 * KB)
            for f in range(KB):
                act.wait_ge(S("h_ready"), 2 * KB + f + 1)
                act.activation(sq[:, f, :], xT[:, f, :], ACT.Square).then_inc(S("norm_sq"), 1)
            for j in (1, 2):
                high(st_h2, 0, j, IN_PARTS)
            norm(3)
            for f in range(KB):
                act.wait_ge(S("h_scaled"), 3 * KB + f + 2)
                act.activation(h1_parts[:, f, 0, :], hT[:, f, :], ACT.Identity, bias=mod[:, 8 * KB + f:8 * KB + f + 1]).then_inc(S("h_ready"), 1)
            for f in range(KB):
                act.wait_ge(S("h_low"), LOW_OF[3] * KB + f + 1)
                act.activation(hT[:, f, :], hT[:, f, :], ACT.Identity, bias=mod[:, 8 * KB + f:8 * KB + f + 1]).then_inc(S("h_shifted"), 1)

            def copy_out2(i, j, last=False):
                first = isinstance(i, int) and i == 0
                if j < 2:
                    dst = big[:, 2 * i + j, :] if isinstance(i, int) else big[:, bass.ds(2 * i + j, 1), :]
                else:
                    if not first:
                        if j < 4:
                            act.wait_ge(S("v2_turned"), i)
                        else:
                            act.wait_ge(S("scaled2"), 15 * i)
                    dst = qkv2[:, {2: 2, 3: 3, 4: 0, 5: 1}[j], :]
                copy_out(st_h2, i, j, dst, 3, scale=float(DK2) ** -0.5 if j == 4 else 1.0)
                if j < 3:
                    high(st_h2, i, j + 3, IN_PARTS)
                elif not last:
                    high(st_h2, i + 1, j - 3, IN_PARTS)

            copy_out2(0, 0)
            act.wait_ge(S("gates_done"), 3)
            act.activation(glr[0:RANK, :], bank[3][0:RANK, 0:T], ACT.Copy).then_inc(S("gate_act"), 1)
            copy_out2(0, 1)
            act.wait_ge(S("gates_done"), 4)
            for h in range(H2):
                act.activation(gb[:, h, :], bank[4 + h // 2][:, h % 2 * T:(h % 2 + 1) * T], ACT.Identity, bias=vec_cols[:, V_BG + h:V_BG + h + 1])\
                   .then_inc(S("gate_act"), 1)
            act.wait_ge(S("gate_act"), 1 + H2)
            act.activation(gl_a, gb, ACT.Abs).then_inc(S("gate_act"), 1)
            act.wait_ge(S("gate_act"), H2 + 2)
            act.activation(gl_a, gl_a, ACT.Exp, scale=-1.0).then_inc(S("gate_act"), 1)
            act.wait_ge(S("gate_act"), H2 + 3)
            act.activation(gl_a, gl_a, ACT.Ln, bias=1.0).then_inc(S("gate_act"), 1)

            def head2(i, gemm, chain, last=False):
                at = [0]

                def copies(step):
                    while gemm and at[0] < 6 and ready_step2[at[0]] <= step:
                        copy_out2(i, at[0], last)
                        at[0] += 1

                if not chain:
                    at[0] = 2
                    copies(len(ready_step2))
                    return
                n = i
                r = big[:, bass.ds(2 * i - 2, 2), :] if not isinstance(i, int) else big[:, 2 * i - 2:2 * i, :]
                act.wait_ge(S("evacuated"), st_h2.done(i - 1, 1) + 3)
                act.activation(r, r, ACT.Silu).then_inc(S("expo_done"), 1)
                act.preload_act_table_set(LOG_EXP)
                act.wait_ge(S("expo"), 14 * n)
                act.activation(expo, expo, ACT.Exp, scale=1.0 / TAU).then_inc(S("expo_done"), 1)
                copies(1)
                act.wait_ge(S("v2_turned"), n)
                act.activation(v_tok.rearrange("p t d -> p (t d)"), bank[3][:, :], ACT.Copy).then_inc(S("tok2"), 1)
                copies(2)
                act.wait_ge(S("kd_turned"), n)
                act.activation(kd_tok.rearrange("p t d -> p (t d)"), bank[4][:, 0:NT * P], ACT.Copy).then_inc(S("tok2"), 1)
                copies(5)
                act.wait_ge(S("o2_done"), n)
                act.activation(sq_o.rearrange("p d t -> p (d t)"), bank[5][:, :], ACT.Square).then_inc(S("o2_sq"), 1)
                copies(6)
                act.wait_ge(S("o2_sum"), n)
                act.activation(lnb[:, 0:T], bank[4][:, 0:T], ACT.Ln, bias=eps_col[:, 0:1], scale=1.0 / (DV2 * P)).then_inc(S("o2_rn"), 1)
                act.wait_ge(S("o2_rn"), 2 * n - 1)
                act.activation(lnb[:, T:2 * T], lnb[:, 0:T], ACT.Exp, scale=-0.5).then_inc(S("o2_rn"), 1)

            head2(0, True, False)
            with act.Fori(1, H2 - 1) as i:
                head2(i, True, True)
            head2(H2 - 1, True, True, last=True)
            head2(H2, False, True)

            out_pairs(st_o2, OUT2, KB, 10)
            ffn(4, st_f2, st_d2, 11)
            norm(5)
            shift(5, hT, 14 * KB)
            for q, (c0, n) in enumerate(((0, QR), (QR, KVR))):
                for t in range(NT):
                    if q and t == NT - 1:
                        act.wait_ge(S("gemm_done"), st_lat.end)
                    else:
                        act.wait_ge(S("lat_done"), 2 * q + t + 1)
                    if q:
                        act.activation(lat[:, t, QR + KVR:MLA_COLS], bank[2 * t + 1][:, KVR:KVR + ROPE], ACT.Copy).then_inc(S("k_raw"), 1)
                    act.wait_ge(S("lat_sq"), 2 * q + t + 1)
                    act.activation(lat_sq[:, 0:n], bank[2 * t + q][:, 0:n], ACT.Square, accum_out=lat_ss[:, t, q:q + 1]).then_inc(S("lat_sq"), 1)
                act.wait_ge(S("lat_sq"), 2 * q + NT + 1)
                act.activation(lat_ln[:, :, q], lat_ss[:, :, q], ACT.Ln, bias=eps_col[:, 0:1], scale=1.0 / n).then_inc(S("lat_rn"), 1)
                act.wait_ge(S("lat_rn"), 2 * q + 1)
                act.activation(lat_rn[:, :, q], lat_ln[:, :, q], ACT.Exp, scale=-0.5).then_inc(S("lat_rn"), 1)
                act.wait_ge(S("lat_rn"), 2 * q + 2)
                for t in range(NT):
                    act.activation(lat[:, t, c0:c0 + n], bank[2 * t + q][:, 0:n], ACT.Copy, scale=lat_rn[:, t, q:q + 1]).then_inc(S("lat_scaled"), 1)
            act.wait_ge(S("lat_scaled"), 2 * NT)
            act.wait_ge(S("k_raw"), NT)
            act.sem_inc(S("evacuated"), 1)
            act.wait_ge(S("lat_turned"), 1)
            for t in range(NT):
                for k in range(QB):
                    act.activation(cqT[:, k, t * P:(t + 1) * P], bank[4 + t][:, k * P:(k + 1) * P], ACT.Copy, scale=vec_cols[:, V_GQ + k:V_GQ + k + 1])\
                       .then_inc(S("latT"), 1)
            act.wait_ge(S("lat_turned"), 2)
            for t in range(NT):
                for k in range(KVB):
                    act.activation(ckvT[:, k, t * P:(t + 1) * P], bank[6][:, (2 * t + k) * P:(2 * t + k + 1) * P], ACT.Copy,
                                   scale=vec_cols[:, V_GKV + k:V_GKV + k + 1]).then_inc(S("latT"), 1)
            act.wait_ge(S("lat_turned"), 3)
            act.activation(krT, ADA_BANK[:, 0:T], ACT.Copy).then_inc(S("latT"), 1)
            SCALE3 = float(NOPE + ROPE) ** -0.5

            def copy_queries(i):
                for e in range(2):
                    act.wait_ge(S("gemm_done"), st_h3.done(i, 2 * e))
                    act.activation(qkT[:, e].rearrange("p a t -> p (a t)"), bank[e][:, :], ACT.Copy).then_inc(S("evacuated"), 1)
                    act.wait_ge(S("gemm_done"), st_h3.done(i, 2 * e + 1))
                    act.activation(q_raw[:, e].rearrange("p t f -> p (t f)"), bank[2 + e][:, T:T + NT * ROPE], ACT.Copy).then_inc(S("q_raw"), 1)

            def copy_values(i):
                for e in range(2):
                    act.activation(vr[:, e, :], bank[2 + e][:, 0:T], ACT.Copy).then_inc(S("evacuated"), 1)
                act.wait_ge(S("qr_turned"), i + 1)
                act.activation(qrT, bank[4][:, 0:T], ACT.Copy).then_inc(S("qrT"), 1)

            def softmax(i):
                for e in range(2):
                    for t in range(NT):
                        act.wait_ge(S("nm3"), 2 * i + e + 1)
                        cols = slice(t * P, 3 * P if t else P)
                        act.activation(p3[:, e, cols], sc3[:, e, cols], ACT.Exp, bias=nm3[:, e, t:t + 1], scale=SCALE3,
                                       accum_out=sum3[:, e, t:t + 1]).then_inc(S("exp3"), 1)

            def attended(i):
                for e in range(2):
                    act.wait_ge(S("p3_turned"), 2 * i + e + 1)
                    act.activation(pT3[:, e, :], bank[5 + e][:, 0:3 * P], ACT.Copy).then_inc(S("pT3"), 1)
                act.wait_ge(S("o3_done"), i + 1)
                for e in range(2):
                    dst = big[:, 2 * i + e, :] if isinstance(i, int) else big[:, bass.ds(2 * i + e, 1), :]
                    act.activation(dst, ADA_BANK[:, e * T:(e + 1) * T], ACT.Copy).then_inc(S("o3"), 1)

            copy_queries(0)
            copy_values(0)
            with act.Fori(0, st_h3.n - 1) as i:
                softmax(i)
                copy_queries(i + 1)
                attended(i)
                copy_values(i + 1)
            softmax(st_h3.n - 1)
            attended(st_h3.n - 1)
            out_pairs(st_o3, OUT3, 2 * KB, 16)
            ffn(6, st_f3, st_d3, 17)
            norm(7)
            for m in range(NT * KB // 4):
                act.wait_ge(S("turned"), KB // 2 + m + 1)
                n, g = divmod(m, KB // 4)
                act.activation(xtok[:, n, g * 512:(g + 1) * 512], bank[m % 2][:, :], ACT.Copy).then_inc(S("y_copied"), 1)

        @block.vector
        def _(dve):
            def ada_mac(m, c0, ks=range(KB), u=None, spare=None):
                pre = isinstance(m, int) and m < len(early)
                acc = acc_early[m % 2] if pre else acc_early[0]
                u = m - SPARE if u is None else u
                for k in ks:
                    if pre:
                        dve.wait_ge(S(f"early{m}"), 16)
                        w = early[m][:, k, :]
                    elif spare is not None:
                        dve.wait_ge(S("early1"), spare)
                        w = spare_w[k // 4][:, k % 4, :]
                    else:
                        if k % 4 == 0:
                            dve.wait_ge(S(f"ada_landed{k // 4}"), 16 * u)
                        w = ada_w[:, k // 4, k % 4, :]
                    if k == 0:
                        if not (pre and m < 2):
                            dve.wait_ge(S("ada_sum"), m - 1 if pre else m)
                        dve.tensor_scalar(acc, w, cact[:, c0:c0 + 1], None, ALU.mult).then_inc(S("ada_mac"), 1)
                    else:
                        dve.wait_ge(S("ada_mac"), KB * m + k)
                        dve.scalar_tensor_tensor(acc, w, cact[:, c0 + k:c0 + k + 1], acc, ALU.mult, ALU.add).then_inc(S("ada_mac"), 1)
                    if k % 4 == 3 and not (pre and m) and spare is None:
                        dve.wait_ge(S("ada_mac"), KB * m + k + 1)
                        dve.sem_inc(S("ada_used"), 1)

            def ada_bias(m, col):
                dve.wait_ge(S("ada_sum"), m + 1)
                dve.tensor_tensor(mod[:, bass.ds(col, 4)], ADA_BANK[:, 0:4], bias_cols[:, bass.ds(col, 4)], ALU.add).then_inc(S("mod_ready"), 1)

            def norm_scale(n, w_cols, sc_col):
                dve.wait_ge(S("nscale"), n + 1)
                dve.wait_ge(S("h_scaled"), KB * n + 1)
                dve.scalar_tensor_tensor(nscale[:, :], mod[:, sc_col:sc_col + KB], 1.0, w_cols, ALU.add, ALU.mult)\
                   .then_inc(S("nscale"), 1)
                dve.wait_ge(S("nscale"), n + 2)
                dve.wait_ge(S("rstd"), n + 1)

            def h_low(n, f, parts):
                col = NORMS[n][1] - KB + f
                dve.wait_ge(S("h_ready"), KB * n + f + 1)
                dve.scalar_tensor_tensor(parts[:, f, 1, :], hT[:, f, :], mod[:, col:col + 1], parts[:, f, 0, :].bitcast(F32), ALU.add, ALU.subtract)\
                   .then_inc(S("h_low"), 1)

            def norm_apply(n, dst):
                for f in range(KB):
                    dve.scalar_tensor_tensor(dst[:, f, :], xT[:, f, :], nscale[:, f:f + 1], rstd[:, :], ALU.mult, ALU.mult)\
                       .then_inc(S("h_scaled"), 1)

            dve.memset(eps_col[:, :], EPS).then_inc(S("mod_ready"), 1)
            dve.sem_inc(S("h_scaled"), 1)
            dve.sem_inc(S("nscale"), 1)
            dve.sem_inc(S("mixed"), 2)
            dve.sem_inc(S("o_added"), 4)
            dve.sem_inc(S("d_added"), 2)
            dve.sem_inc(S("ffn_free"), 2)
            dve.wait_ge(S("c_ready"), 3)
            for m in range(len(early)):
                ada_mac(m, 0)
                if m:
                    ada_bias(m - 1, 4 * (m - 1))
            ada_bias(len(early) - 1, 4 * len(early) - 4)
            dve.wait_ge(S("mod_ready"), 1 + len(early))
            norm_scale(0, n1_cols[:, :], KB)
            for f in range(KB):
                dve.scalar_tensor_tensor(hT[:, f, :], xT[:, f, :], nscale[:, f:f + 1], rstd[:, :], ALU.mult, ALU.mult).then_inc(S("h_scaled"), 1)
                if f:
                    h_low(0, f - 1, h1_parts)
            h_low(0, KB - 1, h1_parts)
            dve.wait_ge(S("rows_landed"), 16 * n_table_dmas)
            dve.tensor_copy(pos_f[:, :], pos_i[:, :]).then_inc(S("pos"), 1)

            def angles():
                dve.wait_ge(S("pos_turned"), 1)
                dve.tensor_copy(pos_c[:, :], ADA_BANK[:, 0:NT]).then_inc(S("pos"), 1)
                dve.wait_ge(S("pos"), 2)
                dve.wait_ge(S("masks"), ROPE // 2 + 3)
                for t in range(NT):
                    dve.tensor_scalar(angle[:, t, :], inv_freq[:, :], pos_c[:, t:t + 1], None, ALU.mult).then_inc(S("angle"), 1)
                n = NT
                dve.wait_ge(S("angle"), n)
                TWO_PI, ROUND, PI = 2 * np.pi, 1.5 * 2.0 ** 23, float(np.float32(3.1415925))
                for dst, src, scalar, op0, in1, op1 in (
                        (turns, angle, 1 / TWO_PI, ALU.mult, ROUND, ALU.add), (turns, turns, ROUND, ALU.subtract, None, None),
                        (sin_t, turns, -6.25, ALU.mult, angle, ALU.add), (sin_t, turns, -17 / 512, ALU.mult, sin_t, ALU.add),
                        (sin_t, turns, -(TWO_PI - 6.25 - 17 / 512), ALU.mult, sin_t, ALU.add), (sin_t, sin_t, PI, ALU.min, -PI, ALU.max),
                        (cos_t, sin_t, TWO_PI / 4, ALU.add, None, None), (turns, cos_t, np.pi, ALU.is_gt, -TWO_PI, ALU.mult),
                        (cos_t, turns, 0.0, ALU.add, cos_t, ALU.add), (cos_t, cos_t, PI, ALU.min, -PI, ALU.max)):
                    if in1 is None:
                        ins = dve.tensor_scalar(dst[:, :, :], src[:, :, :], scalar, None, op0)
                    elif isinstance(in1, float):
                        ins = dve.tensor_scalar(dst[:, :, :], src[:, :, :], scalar, in1, op0, op1)
                    else:
                        ins = dve.scalar_tensor_tensor(dst[:, :, :], src[:, :, :], scalar, in1[:, :, :], op0, op1)
                    ins.then_inc(S("angle"), 1)
                    n += 1
                    dve.wait_ge(S("angle"), n)

            dve.wait_ge(S("gates_done"), 1)
            ps = bank[3][:, 0:NT * 2 * H1].rearrange("p (n k h) -> p n k h", n=NT, k=2)
            for n in range(NT):
                dve.tensor_tensor(ab_in[:, n, 0, :], ps[:, n, 0, :], head_rows[:, 0, :], ALU.add).then_inc(S("ab_part"), 1)
            dve.wait_ge(S("ab_part"), NT)
            dve.sem_inc(S("ab_copied"), 1)
            dve.tensor_copy(ab_in[:, :, 1, :], ps[:, :, 1, :]).then_inc(S("ab_copied"), 1)
            dve.wait_ge(S("ab_act"), 4)
            dve.scalar_tensor_tensor(ab_t[:, 0], ab_in[:, :, 0, :], 0.0, ab_t[:, 2], ALU.max, ALU.add).then_inc(S("ab_part"), 1)
            dve.wait_ge(S("ab_part"), NT + 1)
            for n in range(NT):
                dve.scalar_tensor_tensor(ab_t[:, 4, n], ab_t[:, 0, n], -1.0, head_rows[:, 1, :], ALU.mult, ALU.mult).then_inc(S("ab_part"), 1)
            dve.wait_ge(S("ab_part"), 2 * NT + 1)
            hvt = hv.rearrange("p h v -> p v h")
            dve.tensor_copy(hvt[:, 0:NT, :], ab_t[:, 4]).then_inc(S("hv"), 1)
            dve.wait_ge(S("ab_act"), 5)
            dve.tensor_scalar(ab_t[:, 1], ab_t[:, 3], 1.0, None, ALU.add).then_inc(S("ab_part"), 1)
            dve.wait_ge(S("ab_part"), 2 * NT + 2)
            dve.reciprocal(hvt[:, 2:2 + NT, :], ab_t[:, 1]).then_inc(S("hv"), 1)
            def col(tile, first, i):
                return tile[:, first + i:first + i + 1] if isinstance(i, int) else tile[:, bass.ds(i + first, 1)]

            def part(tile, i):
                return tile[:, i, :] if isinstance(i, int) else tile[:, bass.ds(i, 1), :]

            def short_conv(i):
                n = i
                dve.wait_ge(S("evacuated"), st_h1.done(i, 5) + 3)
                x_in = scx_pad[:, TAPS2 - 1:TAPS2 - 1 + T]
                dve.tensor_tensor(x_in, x_in, scc, ALU.mult).then_inc(S("short"), 1)
                for k in range(TAPS2):
                    dve.wait_ge(S("short"), 5 * n + k + 1)
                    w = col(vec_cols, V_SC + k * KB, i)
                    if k == 0:
                        dve.tensor_scalar(scv, scx_pad[:, 0:T], w, None, ALU.mult).then_inc(S("short"), 1)
                    else:
                        dve.scalar_tensor_tensor(scv, scx_pad[:, k:k + T], w, scv, ALU.mult, ALU.add).then_inc(S("short"), 1)
                dve.wait_ge(S("short"), 5 * n + TAPS2 + 1)
                dve.tensor_tensor(part(ybin, i), scv, scb, ALU.mult).then_inc(S("short"), 1)

            def convolve(i, k):
                if k == 0:
                    dve.wait_ge(S("evacuated"), st_h1.done(i, 2) + 3)
                    if not (isinstance(i, int) and i == 0):
                        dve.wait_ge(S("kq_ready"), 2 * i)
                for b in range(3):
                    w = col(conv_cols, k * 3 * KB + b * KB, i)
                    if k == 0:
                        dve.tensor_scalar(conv[:, b, :], qkv_pad[:, b, 0:T], w, None, ALU.mult).then_inc(S("conv"), 1)
                    else:
                        dve.wait_ge(S("conv"), 12 * i + 3 * k + b - 3 + 1)
                        dve.scalar_tensor_tensor(conv[:, b, :], qkv_pad[:, b, k:k + T], w, conv[:, b, :], ALU.mult, ALU.add)\
                           .then_inc(S("conv"), 1)

            dve.wait_ge(S("padded"), 3)
            dve.wait_ge(S("c_ready"), 6)
            for k in range(TAPS1):
                convolve(0, k)
            angles()
            dve.wait_ge(S("gates_done"), 2)
            sums = bank[4][:, 0:8 * H1].rearrange("p (k h) -> p k h", h=H1)
            dve.tensor_copy(hvt[:, 4:4 + NT, :], sums[:, 0:NT, :]).then_inc(S("hv"), 1)
            dve.wait_ge(S("hv"), 3)
            dve.tensor_copy(hvt[:, 10:10 + NCH, :], sums[:, 2 * NT:2 * NT + NCH, :]).then_inc(S("ab_part"), 1)
            dve.wait_ge(S("ab_part"), 2 * NT + 3)
            dve.tensor_tensor(hvt[:, 8:8 + NT, :], sums[:, NT:2 * NT, :], hvt[:, 4:4 + NT, :], ALU.subtract).then_inc(S("hv"), 1)
            dve.wait_ge(S("hv_act"), 3)
            dve.tensor_tensor(hvt[:, 14:14 + NT, :], hvt[:, 6:6 + NT, :], hvt[:, 2:2 + NT, :], ALU.mult).then_inc(S("hv"), 1)
            dve.wait_ge(S("hv"), 5)

            ada_mac(PRE - 1, 0, u=1)
            short_conv(0)
            ada_bias(PRE - 1, 4 * PRE - 4)

            def head1(i, gemm, chain):
                n = i
                c = i - 1
                m = M_HEAD - 1 + 2 * i
                dve.tensor_copy(hcur, part(hv, c)).then_inc(S("hcur"), 1)
                dve.wait_ge(S("hcur"), n)
                for t in range(NT):
                    dve.tensor_scalar(gmat[:, t, :], causal[:, :], hcur[:, t:t + 1], None, ALU.mult).then_inc(S("gmat"), 1)
                    dve.tensor_scalar(gmat[:, NT + t, :], ident[:, :], hcur[:, 2 + t:3 + t], None, ALU.mult).then_inc(S("gmat"), 1)
                dve.wait_ge(S("gb_done"), n)
                for t in range(NT):
                    dve.tensor_scalar(dec[:, t, :], bank[4][:, t * P:(t + 1) * P], hcur[:, 4 + t:5 + t], 0.0, ALU.subtract, ALU.min)\
                       .then_inc(S("dec_in"), 1)
                for t in range(NT):
                    dve.tensor_tensor(bstrict[:, t, :], bank[4][:, (NT + t) * P:(NT + t + 1) * P], strict[:, :], ALU.mult)\
                       .then_inc(S("dec_in"), 1)
                if gemm:
                    ada_mac(m - 1, KB, range(3), spare=32 * i + 16)
                dve.wait_ge(S("qk_rn"), 2 * n)
                dve.scalar_tensor_tensor(kq[:, 1, :], act3[:, 0, :], float(P) ** -0.5, rn2[:, 0, :], ALU.mult, ALU.mult).then_inc(S("kq_ready"), 1)
                dve.tensor_tensor(kq[:, 0, :], act3[:, 1, :], rn2[:, 1, :], ALU.mult).then_inc(S("kq_ready"), 1)
                dve.wait_ge(S("dec"), 2 * n - 1)
                for t in range(NT):
                    dve.tensor_tensor(qkdec[:, t, :], dec[:, t, :], causal[:, :], ALU.mult).then_inc(S("masked"), 1)
                dve.wait_ge(S("dec_in"), 4 * n)
                dve.tensor_tensor(ldec, dec, bstrict, ALU.mult).then_inc(S("masked"), 1)
                dve.wait_ge(S("masked"), 3 * n)
                dve.wait_ge(S("kk_done"), n)
                kk = bank[5][:, :].rearrange("p (t w c) -> p t w c", t=NT, w=2)
                dve.tensor_tensor(LT, kk[:, :, 0, :], ldec, ALU.mult).then_inc(S("kk_used"), 1)
                dve.tensor_tensor(QKT, kk[:, :, 1, :], qkdec, ALU.mult).then_inc(S("kk_used"), 1)
                dve.wait_ge(S("kk_used"), 2 * n)
                for t in range(NT):
                    dve.tensor_tensor(LTm[:, :, t, :], LT[:, t:t + 1, :].broadcast_to([P, LEVELS, P]), halves[:, :, :], ALU.mult)\
                       .then_inc(S("levels"), 1)
                dve.wait_ge(S("levels"), 2 * n)
                idb = ident[:, :].rearrange("p (a b) -> p a b", a=1).broadcast_to([P, NT, P])
                dve.tensor_tensor(inv[:, 1], idb, LTm[:, 0], ALU.subtract).then_inc(S("inv"), 1)
                dve.wait_ge(S("x_done"), 6 * c + 1)
                dve.scalar_tensor_tensor(inv[:, 0], bank[3][:, 0:NT * P].rearrange("p (t c) -> p t c", t=NT), -1.0, idb, ALU.mult, ALU.add)\
                   .then_inc(S("inv"), 1)
                dve.wait_ge(S("dec"), 2 * n)
                dve.wait_ge(S("kq_ready"), 2 * n)
                dve.tensor_tensor(qg, kq[:, 1, :], egb, ALU.mult).then_inc(S("qg"), 1)
                for l in range(1, LEVELS):
                    dve.wait_ge(S("y_done"), 5 * c + l)
                    dve.wait_ge(S("inv"), 7 * c + l + 1)
                    flat = inv.rearrange("p a t c -> p (a t c)")
                    dve.tensor_tensor(flat, flat, bank[4][:, :], ALU.subtract).then_inc(S("inv"), 1)
                    if gemm and l <= TAPS1:
                        convolve(i, l - 1)
                    if gemm:
                        ada_mac(m - 1, KB, [l + 2], spare=32 * i + 16)
                for ch in range(NCH):
                    t, r = ch // 2, slice(ch % 2 * CHUNK, ch % 2 * CHUNK + CHUNK)
                    dve.wait_ge(S("v_done"), 4 * c + ch + 1)
                    dve.tensor_copy(vnew[r, t, :], bank[3][r, t * P:(t + 1) * P]).then_inc(S("vnew"), 1)
                    if gemm and ch == 0:
                        ada_bias(m - 1, 14 * KB - 4 + 4 * i)
                    if gemm:
                        ada_mac(m, 0, [2 * ch, 2 * ch + 1] if ch == NCH - 1 else [2 * ch], u=i + 1)
                    if ch < NCH - 1:
                        dve.wait_ge(S("s_done"), 3 * c + ch + 1)
                        if ch == 0:
                            dve.tensor_copy(state, bank[4][:, 0:P]).then_inc(S("state"), 1)
                        else:
                            dve.wait_ge(S("state"), 3 * c + ch)
                            dve.scalar_tensor_tensor(state, state, hcur[:, 10 + ch:11 + ch], bank[4][:, 0:P], ALU.mult, ALU.add).then_inc(S("state"), 1)
                        if gemm:
                            ada_mac(m, 0, [2 * ch + 1], u=i + 1)
                if gemm:
                    short_conv(i)
                    ada_bias(m, 4 * PRE - 4 + 4 * i)
                dve.wait_ge(S("o_rn"), 2 * n + 1)
                dve.scalar_tensor_tensor(onrm, bank[6][:, 0:T], vec_cols[:, V_GN:V_GN + 1], o_rn, ALU.mult, ALU.mult).then_inc(S("o_norm"), 1)
                dve.wait_ge(S("o_norm"), n)
                dve.wait_ge(S("silu"), 2 * n)
                dve.tensor_tensor(part(oall, c), part(oall, c), onrm, ALU.mult).then_inc(S("head_out"), 1)

            with dve.Fori(1, H1) as i:
                head1(i, True, True)
            head1(H1, False, True)
            dve.wait_ge(S("gates"), 2)
            dve.wait_ge(S("evacuated"), st_pb.end + 3)
            dve.tensor_tensor(hT[:, :, :], hT[:, :, :], gates[:, KB:2 * KB, :], ALU.mult).then_inc(S("gated"), 1)
            dve.wait_ge(S("gated"), 1)
            with dve.Fori(0, st_pa.n) as i:
                ada_mac(M_PROJ + i, 0)
                for j in range(2):
                    dve.wait_ge(S("evacuated"), st_pa.done(i, j) + 3)
                    mix = hT[:, bass.ds(2 * i + j, 1), :]
                    dve.tensor_tensor(evac[:, j, :], evac[:, j, :], gates[:, bass.ds(2 * i + j, 1), :], ALU.mult).then_inc(S("gated"), 1)
                    dve.wait_ge(S("gated"), 2 * i + j + 2)
                    dve.tensor_tensor(mix, mix, evac[:, j, :], ALU.add).then_inc(S("mix_ready"), 1)
                    dve.wait_ge(S("mix_ready"), 2 * i + j + 1)
                    dve.sem_inc(S("mixed"), 1)
                ada_bias(M_PROJ + i, 4 * i + 6 * KB)

            def norm_cols(n):
                w_col, sc_col = NORMS[n]
                return vec_cols[:, w_col:w_col + KB], sc_col

            def add_blocks(st, per, sem, first, step=None, pieces=1):
                with dve.Fori(0, st.n) as i:
                    if step:
                        ada_mac(step[0] + i, step[1] * KB)
                    for j in range(per):
                        dve.wait_ge(S("evacuated"), st.done(i, j * pieces + pieces - 1) + 3)
                        xf = xT[:, bass.ds(per * i + j, 1), :]
                        dve.tensor_tensor(xf, xf, evac[:, j, :], ALU.add).then_inc(S(sem), 1)
                        dve.wait_ge(S(sem), first + per * i + j + 1)
                        dve.tensor_tensor(sq[:, bass.ds(per * i + j, 1), :], xf, xf, ALU.mult).then_inc(S("norm_sq"), 1)
                    if step:
                        ada_bias(step[0] + i, step[2] + i * step[3])

            def add_pairs(st, first):
                for j in range(KB):
                    dve.wait_ge(S("evacuated"), st.done(0, j) + 3)
                    dve.tensor_tensor(xT[:, j, :], xT[:, j, :], evac[:, j % 4, :], ALU.add).then_inc(S("o_added"), 1)
                    dve.wait_ge(S("o_added"), first + j + 1)
                    dve.tensor_tensor(sq[:, j, :], xT[:, j, :], xT[:, j, :], ALU.mult).then_inc(S("norm_sq"), 1)

            def ffn(n, st_f, st_d, step=None, step_out=None):
                norm_scale(n, *norm_cols(n))
                for f in range(KB):
                    dve.scalar_tensor_tensor(hT[:, f, :], xT[:, f, :], nscale[:, f:f + 1], rstd[:, :], ALU.mult, ALU.mult)\
                       .then_inc(S("h_scaled"), 1)
                    if f:
                        h_low(n, f - 1, h_parts)
                h_low(n, KB - 1, h_parts)
                first = FFN_OF[n] * FB
                with dve.Fori(0, st_f.n) as i:
                    for q in range(2):
                        if step:
                            ada_mac(step[0] + i, step[1] * KB, range(4 * q, 4 * q + 4))
                        prod = evac[:, 2 * q, :]
                        dve.wait_ge(S("evacuated"), st_f.done(i, 2 * q + 1) + 3)
                        dve.tensor_tensor(prod, prod, evac[:, 2 * q + 1, :], ALU.mult).then_inc(S("ffn_act"), 1)
                        dve.wait_ge(S("act_high"), first + 2 * i + q + 1)
                        f = bass.ds(2 * i + q, 1)
                        dve.tensor_tensor(act_parts[:, f, 1, :], prod, act_parts[:, f, 0, :].bitcast(F32), ALU.subtract).then_inc(S("act_low"), 1)
                        dve.wait_ge(S("act_low"), first + 2 * i + q + 1)
                        dve.sem_inc(S("ffn_free"), 1)
                    if step:
                        ada_bias(step[0] + i, step[2] + i * step[3])
                add_blocks(st_d, 2, "d_added", 2 + FFN_OF[n] * KB, step_out, pieces=4)

            add_blocks(st_o1, 4, "o_added", 4, (M_WO, 1, 14 * KB - 4, 6 * KB))
            ffn(1, st_f1, st_d1, (M_FFN1, 1, 8 * KB, 4), (M_D1, 1, 14 * KB + 4 * (H1 - 1), 4))
            norm_scale(2, *norm_cols(2))
            norm_apply(2, xT)
            norm_scale(3, *norm_cols(3))
            for f in range(KB):
                dve.scalar_tensor_tensor(hT[:, f, :], xT[:, f, :], nscale[:, f:f + 1], rstd[:, :], ALU.mult, ALU.mult).then_inc(S("h_scaled"), 1)
                if f:
                    h_low(3, f - 1, h1_parts)
            h_low(3, KB - 1, h1_parts)
            dve.memset(segment, 1.0).then_inc(S("segment"), 1)
            dve.wait_ge(S("segment"), 1)
            dve.memset(segment.rearrange("p (c k) -> p c k", k=CHUNK)[:, :, 0:1], 0.0).then_inc(S("segment"), 1)
            dve.memset(kt, 0.0).then_inc(S("segment"), 1)
            for l in range(LEVELS):
                b = 1 << l
                dve.tensor_copy(halves_c[:, l, :].rearrange("p (n b) -> p n b", b=b), halves[:, l, :].rearrange("p (n h b) -> p n h b", h=2, b=b)[:, :, 1, :])\
                   .then_inc(S("segment"), 1)
            dve.wait_ge(S("gate_act"), H2 + 4)
            dve.scalar_tensor_tensor(gl_m, gb, 0.0, gl_a, ALU.min, ALU.subtract).then_inc(S("gate_log"), 1)
            dve.wait_ge(S("gate_log"), 1)
            dve.wait_ge(S("segment"), 3 + LEVELS)
            dve.tensor_tensor_scan(gb.rearrange("p h t -> p (h t)"), segment, gl_m.rearrange("p h t -> p (h t)"), 0.0, ALU.mult, ALU.add)\
               .then_inc(S("gate_log"), 1)
            dve.wait_ge(S("gate_log"), 2)

            def head2(i):
                n, c = i, i - 1
                cum = expo[:, 7 * T:8 * T]
                dve.tensor_copy(cum, part(gb, c)).then_inc(S("expo"), 1)
                dve.wait_ge(S("expo"), 14 * c + 1)
                for l in range(LEVELS):
                    b = 1 << l
                    v = cum.rearrange("p (n h b) -> p n h b", h=2, b=b)
                    ref = v[:, :, 0, b - 1:b].broadcast_to([P, T // (2 * b), b])
                    e = expo[:, l * T:(l + 1) * T].rearrange("p (h n b) -> p h n b", h=2, b=b)
                    dve.tensor_tensor(e[:, 0], ref, v[:, :, 0, :], ALU.subtract).then_inc(S("expo"), 1)
                    dve.tensor_tensor(e[:, 1], v[:, :, 1, :], ref, ALU.subtract).then_inc(S("expo"), 1)
                v = cum.rearrange("p (n k) -> p n k", k=CHUNK)
                dve.tensor_tensor(expo[:, 6 * T:7 * T].rearrange("p (n k) -> p n k", k=CHUNK), v[:, :, CHUNK - 1:CHUNK].broadcast_to([P, NCH, CHUNK]), v,
                                  ALU.subtract).then_inc(S("expo"), 1)
                dve.wait_ge(S("evacuated"), st_h2.done(c, 5) + 3)
                q, k = qkv2[:, 0, :], qkv2[:, 1, :]
                dve.tensor_tensor(qk2, q, k, ALU.mult).then_inc(S("scaled2"), 1)
                dve.wait_ge(S("expo_done"), 2 * n)
                dve.tensor_tensor(kd, k, expo[:, 6 * T:7 * T], ALU.mult).then_inc(S("scaled2"), 1)
                for l in range(LEVELS):
                    b = 1 << l
                    e = expo[:, l * T:(l + 1) * T].rearrange("p (h n b) -> p h n b", h=2, b=b)
                    kv, qv = (w.rearrange("p (n h b) -> p n h b", h=2, b=b) for w in (k, q))
                    dve.tensor_tensor(kt[:, l, :].rearrange("p (n h b) -> p n h b", h=2, b=b)[:, :, 0, :], kv[:, :, 0, :], e[:, 0], ALU.mult)\
                       .then_inc(S("scaled2"), 1)
                    dve.tensor_tensor(qt[:, l].rearrange("p t k -> p (t k)").rearrange("p (n b) -> p n b", b=b), qv[:, :, 1, :], e[:, 1], ALU.mult)\
                       .then_inc(S("scaled2"), 1)
                dve.tensor_tensor(qe, q, cum, ALU.mult).then_inc(S("scaled2"), 1)
                dve.wait_ge(S("att_done"), n)
                for t in range(NT):
                    dve.tensor_copy(qk_col[:, t:t + 1], bank[3 + t][:, 2 * T - 1:2 * T]).then_inc(S("att_l"), 1)
                    dve.tensor_tensor(att_l[:, t], bank[3 + t][:, 0:LEVELS * CHUNK].rearrange("p (l k) -> p l k", l=LEVELS), halves_c, ALU.mult)\
                       .then_inc(S("att_l"), 1)
                dve.wait_ge(S("att_l"), 4 * n)
                for t in range(NT):
                    dve.tensor_scalar(att[:, t, :], ident[:, :], qk_col[:, t:t + 1], None, ALU.mult).then_inc(S("att"), 1)
                for l in range(LEVELS):
                    b = 1 << l
                    dve.wait_ge(S("att"), 8 * c + l + 2)
                    v = att.rearrange("p t (n h b) -> p t n h b", h=2, b=b)[:, :, :, 1, :]
                    dve.tensor_tensor(v, v, att_l[:, :, l, :].rearrange("p t (n b) -> p t n b", b=b), ALU.add).then_inc(S("att"), 1)
                dve.wait_ge(S("kv_done"), 3 * c + 2)
                dve.tensor_copy(states[:, 0, :], bank[6][:, 0:T]).then_inc(S("state2"), 1)
                for ch in range(1, NCH - 1):
                    dve.wait_ge(S("state2"), 3 * c + ch)
                    if ch == 2:
                        dve.wait_ge(S("kv_done"), 3 * c + 3)
                    last = cum[:, (ch + 1) * CHUNK - 1:(ch + 1) * CHUNK]
                    dve.scalar_tensor_tensor(states[:, ch, :], states[:, ch - 1, :], last, bank[6][:, (ch % 2) * T:(ch % 2 + 1) * T], ALU.mult, ALU.add)\
                       .then_inc(S("state2"), 1)
                dve.wait_ge(S("o2_rn"), 2 * n)
                for d in range(DV2):
                    dve.scalar_tensor_tensor(on2[:, d, :], bank[5][:, d * T:(d + 1) * T], vec_cols[:, V_GG + d:V_GG + d + 1], lnb[:, T:2 * T],
                                             ALU.mult, ALU.mult).then_inc(S("o2_norm"), 1)
                dve.wait_ge(S("o2_norm"), 2 * n)
                dve.wait_ge(S("expo_done"), 2 * n)
                r = big[:, bass.ds(2 * i - 2, 2), :] if not isinstance(i, int) else big[:, 2 * i - 2:2 * i, :]
                dve.tensor_tensor(r, r, on2, ALU.mult).then_inc(S("head2_out"), 1)

            with dve.Fori(1, H2) as i:
                head2(i)
            head2(H2)

            add_pairs(st_o2, 4 + KB)
            ffn(4, st_f2, st_d2)
            norm_scale(5, *norm_cols(5))
            norm_apply(5, hT)
            for q in (0, 2):
                dve.tensor_scalar(neg3[:, q, :], causal_q[:, :], 1.0, 1e30, ALU.subtract, ALU.mult).then_inc(S("neg3"), 1)
            dve.memset(neg3[:, 1, :], 0.0).then_inc(S("neg3"), 1)

            def rotate(dst, src, tmp, sem, base):
                v = src.rearrange("p t (f two) -> p t f two", two=2)
                for q, (part_, table) in enumerate(((0, cos_t), (1, sin_t), (0, sin_t), (1, cos_t))):
                    dve.tensor_tensor(tmp[:, q], v[:, :, :, part_], table[:, :, :], ALU.mult).then_inc(S("rotated"), 1)
                dve.wait_ge(S("rotated"), base + 4)
                dve.tensor_tensor(dst[:, :, 0:ROPE // 2], tmp[:, 0], tmp[:, 1], ALU.subtract).then_inc(S(sem), 1)
                dve.tensor_tensor(dst[:, :, ROPE // 2:ROPE], tmp[:, 2], tmp[:, 3], ALU.add).then_inc(S(sem), 1)

            dve.wait_ge(S("k_raw"), NT)
            dve.wait_ge(S("rotary"), 2)
            for e in range(2):
                rotate(k_rot[:, :, e], lat[:, :, QR + KVR:MLA_COLS], rot_u[:, e], "k_rot", 4 * e)
            dve.wait_ge(S("neg3"), 3)
            SCALE3 = float(NOPE + ROPE) ** -0.5

            def rotate_queries(i):
                for e in range(2):
                    dve.wait_ge(S("q_raw"), 2 * i + e + 1)
                    rotate(q_rot[:, :, e], q_raw[:, e], rot_u[:, e], "q_rot", 8 * i + 4 * e + 8)

            def softmax(i):
                for e in range(2):
                    dve.wait_ge(S("score3"), 2 * i + e + 1)
                    dve.tensor_tensor(sc3[:, e, :], bank[5 + e][:, 0:3 * P], neg3.rearrange("p a b -> p (a b)"), ALU.add).then_inc(S("sc3"), 1)
                    dve.wait_ge(S("sc3"), 2 * i + e + 1)
                    for t in range(NT):
                        dve.tensor_reduce(mx3[:, e, t:t + 1], sc3[:, e, (t * P):(3 * P if t else P)], AX_X, ALU.max).then_inc(S("mx3"), 1)
                    dve.wait_ge(S("mx3"), 4 * i + 2 * e + 2)
                    dve.tensor_scalar(nm3[:, e, :], mx3[:, e, :], -SCALE3, None, ALU.mult).then_inc(S("nm3"), 1)
                for e in range(2):
                    dve.wait_ge(S("exp3"), 4 * i + 2 * e + 2)
                    dve.reciprocal(inv3[:, e, :], sum3[:, e, :]).then_inc(S("inv3"), 1)
                    dve.wait_ge(S("inv3"), 2 * i + e + 1)
                    for t in range(NT):
                        cols = slice(t * P, 3 * P if t else P)
                        dve.tensor_scalar(p3[:, e, cols], p3[:, e, cols], inv3[:, e, t:t + 1], None, ALU.mult).then_inc(S("p3"), 1)

            rotate_queries(0)
            with dve.Fori(0, st_h3.n - 1) as i:
                softmax(i)
                rotate_queries(i + 1)
            softmax(st_h3.n - 1)
            add_pairs(st_o3, 4 + 2 * KB)
            ffn(6, st_f3, st_d3)
            dve.wait_ge(S("rstd"), 8)
            for f in range(KB):
                dve.scalar_tensor_tensor(hT[:, f, :], xT[:, f, :], vec_cols[:, V_FIN + f:V_FIN + f + 1], rstd[:, :], ALU.mult, ALU.mult)\
                   .then_inc(S("h_scaled"), 1)


def kernel(**inputs):
    from concourse import bacc
    from concourse.bass_utils import run_bass_kernel_spmd

    nc = bacc.Bacc("TRN2", target_bir_lowering=False, num_devices=1)
    arrays, views = {}, {}
    for name, value in inputs.items():
        value = np.ascontiguousarray(value)
        arrays[f"in_{name}"] = value
        views[name] = nc.dram_tensor(f"in_{name}", value.shape, mybir.dt.from_np(value.dtype), kind="ExternalInput").ap()
    shape = arrays["in_x"].shape
    out = nc.dram_tensor("out", shape, F32, kind="ExternalOutput").ap()
    program(nc, views, out)
    result = run_bass_kernel_spmd(nc, [arrays], core_ids=[0])
    return result.results[0]["out"]
```
